# Optimizing a Trainium2 kernel written in Bass

```python
import math
import jax, jax.numpy as jnp
from jax import lax
import numpy as np

D_MODEL = 1024
BATCH = 1
SEQ = 256
DEPTH = 2

RET_WIDTH = D_MODEL // 2
RET_HEAD_DIM = 64
RET_HEADS = RET_WIDTH // RET_HEAD_DIM
DIFF_WIDTH = D_MODEL - RET_WIDTH
DIFF_HEAD_DIM = 64
DIFF_V_DIM = 2 * DIFF_HEAD_DIM
DIFF_HEADS = DIFF_WIDTH // DIFF_V_DIM
MIX_WIDTH = RET_WIDTH + DIFF_WIDTH
D_IN_PROJ = 4 * RET_WIDTH + 3 * DIFF_WIDTH
D_FF = -(-8 * D_MODEL // (3 * 256)) * 256
CHUNK = 128
Q_BLOCK = 128
EPS = 1e-6


def rms_norm(x, g):
    xf = x.astype(jnp.float32)
    y = xf * lax.rsqrt(jnp.mean(xf * xf, axis=-1, keepdims=True) + EPS)
    return (y * g.astype(jnp.float32)).astype(x.dtype)

def alibi_slopes(n):
    return 2.0 ** (-8.0 * jnp.arange(1, n + 1, dtype=jnp.float32) / n)

def retention_bidir(q, k, v, lg_f, lg_b):
    B, S, H, D = q.shape
    N = S // CHUNK
    qc = q.astype(jnp.float32).reshape(B, N, CHUNK, H, D)
    kc = k.astype(jnp.float32).reshape(B, N, CHUNK, H, D)
    vc = v.astype(jnp.float32).reshape(B, N, CHUNK, H, D)
    pos = jnp.arange(CHUNK, dtype=jnp.float32)
    dist = pos[:, None] - pos[None, :]
    mask_f = jnp.where(dist >= 0, jnp.exp(lg_f[:, None, None] * jnp.maximum(dist, 0.0)), 0.0)
    mask_b = jnp.where(dist < 0, jnp.exp(lg_b[:, None, None] * jnp.maximum(-dist, 0.0)), 0.0)
    dmask = mask_f + mask_b
    scores = jnp.einsum('bnthd,bnshd->bnhts', qc, kc) * dmask[None, None]
    intra = jnp.einsum('bnhts,bnshd->bnthd', scores, vc)

    wk_f = jnp.exp(lg_f[None, :] * (CHUNK - 1 - pos)[:, None])
    wq_f = jnp.exp(lg_f[None, :] * (pos + 1)[:, None])
    kv_f = jnp.einsum('bnshd,bnshe->nbhde', kc * wk_f[None, None, :, :, None], vc)
    dc_f = jnp.exp(lg_f * CHUNK)[None, :, None, None]
    wk_b = jnp.exp(lg_b[None, :] * pos[:, None])
    wq_b = jnp.exp(lg_b[None, :] * (CHUNK - pos)[:, None])
    kv_b = jnp.einsum('bnshd,bnshe->nbhde', kc * wk_b[None, None, :, :, None], vc)
    dc_b = jnp.exp(lg_b * CHUNK)[None, :, None, None]

    zeros = jnp.zeros((B, H, D, D), jnp.float32)

    def fwd_step(R, kv):
        return dc_f * R + kv, R

    def bwd_step(R, kv):
        return dc_b * R + kv, R

    _, R_f = lax.scan(fwd_step, zeros, kv_f)
    _, R_b = lax.scan(bwd_step, zeros, kv_b, reverse=True)
    cross_f = jnp.einsum('bnthd,nbhde->bnthe', qc * wq_f[None, None, :, :, None], R_f)
    cross_b = jnp.einsum('bnthd,nbhde->bnthe', qc * wq_b[None, None, :, :, None], R_b)
    out = (intra + cross_f + cross_b).reshape(B, S, H, D)
    return out.astype(q.dtype)

def diff_attention(q, k, v, lam, slopes):
    B, S, H, _, Dh = q.shape
    NB = S // Q_BLOCK
    q_blocks = q.reshape(B, NB, Q_BLOCK, H, 2, Dh).transpose(1, 0, 2, 3, 4, 5)
    starts = jnp.arange(NB, dtype=jnp.int32) * Q_BLOCK
    kpos = jnp.arange(S, dtype=jnp.int32)
    vf = v.astype(jnp.float32)

    def block(args):
        qb, start = args
        s = jnp.einsum('bqhmd,bkhmd->bhmqk', qb, k).astype(jnp.float32)
        qpos = start + jnp.arange(Q_BLOCK, dtype=jnp.int32)
        dist = jnp.abs(qpos[:, None] - kpos[None, :]).astype(jnp.float32)
        s = s - slopes[None, :, None, None, None] * dist[None, None, None]
        p = jax.nn.softmax(s, axis=-1)
        a = p[:, :, 0] - lam * p[:, :, 1]
        return jnp.einsum('bhqk,bkhe->bqhe', a, vf)

    o = lax.map(block, (q_blocks, starts))
    return o.transpose(1, 0, 2, 3, 4).reshape(B, S, H, DIFF_V_DIM).astype(q.dtype)

def first_inputs(seed: int = 0) -> dict:
    key = jax.random.key(seed)
    ks = jax.random.split(key, 20)
    f32 = jnp.float32
    nrm = lambda k, shape, scale: jax.random.normal(k, shape, f32) * scale
    heads = jnp.arange(RET_HEADS, dtype=f32)
    base = jnp.log(-jnp.log1p(-(2.0 ** (-5.0 - heads))))
    return {
        "x": jax.random.normal(ks[0], (BATCH, SEQ, D_MODEL), f32),
        "attn_norm_g": 1.0 + nrm(ks[1], (DEPTH, D_MODEL), 0.02),
        "w_in": nrm(ks[2], (DEPTH, D_MODEL, D_IN_PROJ), D_MODEL ** -0.5),
        "ret_decay_fwd": base[None, :] + nrm(ks[3], (DEPTH, RET_HEADS), 0.1),
        "ret_decay_bwd": base[None, :] + nrm(ks[4], (DEPTH, RET_HEADS), 0.1),
        "ret_norm_g": 1.0 + nrm(ks[5], (DEPTH, RET_HEAD_DIM), 0.02),
        "dq_norm_g": 1.0 + nrm(ks[6], (DEPTH, DIFF_HEAD_DIM), 0.02),
        "dk_norm_g": 1.0 + nrm(ks[7], (DEPTH, DIFF_HEAD_DIM), 0.02),
        "lambda_q1": nrm(ks[8], (DEPTH, DIFF_HEAD_DIM), 0.1),
        "lambda_k1": nrm(ks[9], (DEPTH, DIFF_HEAD_DIM), 0.1),
        "lambda_q2": nrm(ks[10], (DEPTH, DIFF_HEAD_DIM), 0.1),
        "lambda_k2": nrm(ks[11], (DEPTH, DIFF_HEAD_DIM), 0.1),
        "diff_norm_g": 1.0 + nrm(ks[12], (DEPTH, DIFF_V_DIM), 0.02),
        "w_out": nrm(ks[13], (DEPTH, MIX_WIDTH, D_MODEL), MIX_WIDTH ** -0.5),
        "ffn_norm_g": 1.0 + nrm(ks[14], (DEPTH, D_MODEL), 0.02),
        "w_gate": nrm(ks[15], (DEPTH, D_MODEL, D_FF), D_MODEL ** -0.5),
        "w_up": nrm(ks[16], (DEPTH, D_MODEL, D_FF), D_MODEL ** -0.5),
        "w_down": nrm(ks[17], (DEPTH, D_FF, D_MODEL), D_FF ** -0.5),
    }

def first_block(x, attn_norm_g, w_in, ret_decay_fwd, ret_decay_bwd, ret_norm_g,
              dq_norm_g, dk_norm_g, lambda_q1, lambda_k1, lambda_q2, lambda_k2,
              diff_norm_g, w_out, ffn_norm_g, w_gate, w_up, w_down):
    B, S, _ = x.shape
    slopes = alibi_slopes(DIFF_HEADS)
    split_at = [RET_WIDTH, 2 * RET_WIDTH, 3 * RET_WIDTH, 4 * RET_WIDTH,
                4 * RET_WIDTH + DIFF_WIDTH, 4 * RET_WIDTH + 2 * DIFF_WIDTH]
    for l in range(DEPTH):
        lam_init = 0.8 - 0.6 * math.exp(-0.3 * l)
        h = rms_norm(x, attn_norm_g[l])
        proj = h @ w_in[l]
        rq, rk, rv, rg, dq, dk, dv = jnp.split(proj, split_at, axis=-1)

        shp = (B, S, RET_HEADS, RET_HEAD_DIM)
        lg_f = -jnp.exp(ret_decay_fwd[l].astype(jnp.float32))
        lg_b = -jnp.exp(ret_decay_bwd[l].astype(jnp.float32))
        ret = retention_bidir(rq.reshape(shp), rk.reshape(shp) * RET_HEAD_DIM ** -0.5,
                              rv.reshape(shp), lg_f, lg_b)
        ret = rms_norm(ret, ret_norm_g[l]) * jax.nn.silu(rg.reshape(shp))
        ret = ret.reshape(B, S, RET_WIDTH)

        qk_shp = (B, S, DIFF_HEADS, 2, DIFF_HEAD_DIM)
        dqn = rms_norm(dq.reshape(qk_shp), dq_norm_g[l]) * DIFF_HEAD_DIM ** -0.5
        dkn = rms_norm(dk.reshape(qk_shp), dk_norm_g[l])
        lam = (jnp.exp(jnp.sum(lambda_q1[l].astype(jnp.float32) * lambda_k1[l].astype(jnp.float32)))
               - jnp.exp(jnp.sum(lambda_q2[l].astype(jnp.float32) * lambda_k2[l].astype(jnp.float32)))
               + lam_init)
        da = diff_attention(dqn, dkn, dv.reshape(B, S, DIFF_HEADS, DIFF_V_DIM), lam, slopes)
        da = (rms_norm(da, diff_norm_g[l]) * (1.0 - lam_init)).reshape(B, S, DIFF_WIDTH)

        x = x + jnp.concatenate([ret, da], axis=-1) @ w_out[l]

        h = rms_norm(x, ffn_norm_g[l])
        x = x + (jax.nn.silu(h @ w_gate[l]) * (h @ w_up[l])) @ w_down[l]
    return x


MIX_WIDTH_2 = D_MODEL
GROUP_WIDTH = MIX_WIDTH_2 // 4
MIX_HEAD_DIM = 64
MIX_HEADS = MIX_WIDTH_2 // MIX_HEAD_DIM

SC_WIDTH = GROUP_WIDTH
SC_KERNEL = 3

MLA_HEADS = 4
MLA_NOPE = 64
MLA_ROPE = 32
MLA_V = GROUP_WIDTH // MLA_HEADS
MLA_Q_RANK = 256
MLA_KV_RANK = 128
ROPE_THETA = 10000.0

CF_WIDTH = GROUP_WIDTH
CF_KERNEL = 31

SWA_Q_HEADS = 4
SWA_KV_HEADS = 2
SWA_HEAD_DIM = GROUP_WIDTH // SWA_Q_HEADS
WINDOW = 128

PEER_HEADS = 8
PEER_NKEYS = 128
PEER_EXPERTS = PEER_NKEYS * PEER_NKEYS
PEER_QDIM = 256
PEER_HALF = PEER_QDIM // 2
PEER_TOPK = 16
PEER_CHUNK = 128

ALPHA = (2 * DEPTH) ** 0.25
BETA = (8 * DEPTH) ** -0.25
NORM_EPS = 1e-5

SC_COLS = 3 * SC_WIDTH
MLA_COLS = MLA_Q_RANK + MLA_KV_RANK + MLA_ROPE
CF_COLS = 2 * CF_WIDTH
SWA_COLS = (SWA_Q_HEADS + 2 * SWA_KV_HEADS) * SWA_HEAD_DIM
IN_COLS = SC_COLS + MLA_COLS + CF_COLS + SWA_COLS


def _split_points(sizes):
    pts, acc = [], 0
    for s in sizes[:-1]:
        acc += s
        pts.append(acc)
    return pts

def layer_norm(x, g, b):
    xf = x.astype(jnp.float32)
    mu = jnp.mean(xf, axis=-1, keepdims=True)
    var = jnp.mean(jnp.square(xf - mu), axis=-1, keepdims=True)
    y = (xf - mu) * lax.rsqrt(var + NORM_EPS)
    return (y * g.astype(jnp.float32) + b.astype(jnp.float32)).astype(x.dtype)

def rms_norm_2(x, g):
    xf = x.astype(jnp.float32)
    y = xf * lax.rsqrt(jnp.mean(xf * xf, axis=-1, keepdims=True) + NORM_EPS)
    return (y * g.astype(jnp.float32)).astype(x.dtype)

def causal_depthwise_conv(x, w):
    k = w.shape[0]
    xp = jnp.pad(x, ((0, 0), (k - 1, 0), (0, 0)))
    return lax.conv_general_dilated(
        xp, w[:, None, :], window_strides=(1,), padding='VALID',
        dimension_numbers=('NWC', 'WIO', 'NWC'), feature_group_count=x.shape[-1])

def rope(x, positions):
    d = x.shape[-1]
    half = d // 2
    inv = ROPE_THETA ** (-jnp.arange(half, dtype=jnp.float32) / half)
    ang = positions.astype(jnp.float32)[..., None] * inv
    ang = ang.reshape(ang.shape[:2] + (1,) * (x.ndim - 3) + (half,))
    cos, sin = jnp.cos(ang), jnp.sin(ang)
    xf = x.astype(jnp.float32)
    x1, x2 = xf[..., :half], xf[..., half:]
    return jnp.concatenate([x1 * cos - x2 * sin, x2 * cos + x1 * sin], axis=-1).astype(x.dtype)

def alibi_slopes_2(n):
    return 2.0 ** (-8.0 * jnp.arange(1, n + 1, dtype=jnp.float32) / n)

def short_conv_mixer(gb, gc, h, conv_w):
    return gb * causal_depthwise_conv(gc * h, conv_w)

def mla_attention(c_q, c_kv, k_rope_in, positions, q_norm_g, kv_norm_g, w_uq, w_uk, w_uv):
    b, s, _ = c_q.shape
    q = (rms_norm_2(c_q, q_norm_g) @ w_uq).reshape(b, s, MLA_HEADS, MLA_NOPE + MLA_ROPE)
    q_nope = q[..., :MLA_NOPE]
    q_pe = rope(q[..., MLA_NOPE:], positions)
    ckv = rms_norm_2(c_kv, kv_norm_g)
    k_nope = (ckv @ w_uk).reshape(b, s, MLA_HEADS, MLA_NOPE)
    v = (ckv @ w_uv).reshape(b, s, MLA_HEADS, MLA_V)
    k_pe = rope(k_rope_in, positions)
    nq = s // Q_BLOCK
    qn = q_nope.reshape(b, nq, Q_BLOCK, MLA_HEADS, MLA_NOPE).swapaxes(0, 1)
    qp = q_pe.reshape(b, nq, Q_BLOCK, MLA_HEADS, MLA_ROPE).swapaxes(0, 1)
    key_idx = jnp.arange(s)
    scale = (MLA_NOPE + MLA_ROPE) ** -0.5

    def one_block(args):
        blk, qn_b, qp_b = args
        sc = (jnp.einsum('bqhd,bkhd->bhqk', qn_b, k_nope)
              + jnp.einsum('bqhd,bkd->bhqk', qp_b, k_pe)).astype(jnp.float32) * scale
        q_idx = blk * Q_BLOCK + jnp.arange(Q_BLOCK)
        causal = key_idx[None, :] <= q_idx[:, None]
        sc = jnp.where(causal, sc, -jnp.inf)
        p = jax.nn.softmax(sc, axis=-1).astype(v.dtype)
        return jnp.einsum('bhqk,bkhd->bqhd', p, v)

    out = lax.map(one_block, (jnp.arange(nq), qn, qp))
    return out.swapaxes(0, 1).reshape(b, s, MLA_HEADS * MLA_V)

def conformer_conv(a, gate, dw_w, dw_b, ln_g, ln_b):
    u = a * jax.nn.sigmoid(gate)
    u = causal_depthwise_conv(u, dw_w) + dw_b
    u = layer_norm(u, ln_g, ln_b)
    return jax.nn.silu(u)

def swa_sink_attention(q, k, v, sinks, slopes):
    b, s, _ = q.shape
    g = SWA_Q_HEADS // SWA_KV_HEADS
    nb = s // WINDOW
    qb = q.reshape(b, nb, WINDOW, SWA_KV_HEADS, g, SWA_HEAD_DIM)
    kb = k.reshape(b, nb, WINDOW, SWA_KV_HEADS, SWA_HEAD_DIM)
    vb = v.reshape(b, nb, WINDOW, SWA_KV_HEADS, SWA_HEAD_DIM)

    def with_prev(t):
        prev = jnp.pad(t, ((0, 0), (1, 0), (0, 0), (0, 0), (0, 0)))[:, :-1]
        return jnp.concatenate([prev, t], axis=2)

    kk, vv = with_prev(kb), with_prev(vb)
    sc = jnp.einsum('bnqkgd,bnskd->bnkgqs', qb, kk).astype(jnp.float32) * (SWA_HEAD_DIM ** -0.5)
    qi = jnp.arange(WINDOW)[:, None]
    kj = jnp.arange(2 * WINDOW)[None, :]
    dist = qi + WINDOW - kj
    blk = jnp.arange(nb)[:, None, None]
    valid = ((dist >= 0) & (dist < WINDOW))[None] & ((blk > 0) | (kj[None] >= WINDOW))
    sc = sc - slopes.reshape(SWA_KV_HEADS, g, 1, 1) * dist.astype(jnp.float32)
    sc = jnp.where(valid[None, :, None, None], sc, -jnp.inf)
    sink = jnp.broadcast_to(sinks.astype(jnp.float32).reshape(SWA_KV_HEADS, g, 1, 1), sc.shape[:-1] + (1,))
    p = jax.nn.softmax(jnp.concatenate([sc, sink], axis=-1), axis=-1)[..., :-1].astype(v.dtype)
    o = jnp.einsum('bnkgqs,bnskd->bnqkgd', p, vv)
    return o.reshape(b, s, SWA_Q_HEADS * SWA_HEAD_DIM)

def peer_ffn(x, w_q, sub_keys, u_tab, v_tab):
    b, s, d = x.shape
    xt = x.reshape((b * s) // PEER_CHUNK, PEER_CHUNK, d)

    def chunk(xc):
        c = xc.shape[0]
        q = (xc @ w_q).reshape(c, PEER_HEADS, 2, PEER_HALF)
        sc = jnp.einsum('chpd,hpnd->chpn', q, sub_keys).astype(jnp.float32)
        top_s, top_i = lax.top_k(sc, PEER_TOPK)
        cand_s = top_s[:, :, 0, :, None] + top_s[:, :, 1, None, :]
        cand_i = top_i[:, :, 0, :, None] * PEER_NKEYS + top_i[:, :, 1, None, :]
        best_s, best_j = lax.top_k(cand_s.reshape(c, PEER_HEADS, PEER_TOPK * PEER_TOPK), PEER_TOPK)
        idx = jnp.take_along_axis(cand_i.reshape(c, PEER_HEADS, PEER_TOPK * PEER_TOPK), best_j, axis=-1)
        gate = jax.nn.softmax(best_s, axis=-1).astype(xc.dtype)
        u = u_tab[idx]
        act = jax.nn.gelu(jnp.einsum('chkd,cd->chk', u, xc), approximate=False)
        vsel = v_tab[idx]
        return jnp.einsum('chk,chkd->cd', gate * act, vsel)

    return lax.map(chunk, xt).reshape(b, s, d)

def second_inputs(seed: int = 0) -> dict:
    key = jax.random.key(seed)
    ks = jax.random.split(key, 32)
    L = DEPTH

    def nrm(k, shape, scale):
        return jax.random.normal(k, shape, jnp.float32) * scale

    x = nrm(ks[0], (BATCH, SEQ, D_MODEL), 1.0)
    offs = jax.random.randint(ks[1], (BATCH, 1), 0, 4096, dtype=jnp.int32)
    positions = (offs + jnp.arange(SEQ, dtype=jnp.int32)[None, :]).astype(jnp.int32)
    return {
        "x": x,
        "positions": positions,
        "w_in": nrm(ks[2], (L, D_MODEL, IN_COLS), D_MODEL ** -0.5),
        "sc_conv_w": nrm(ks[3], (L, SC_KERNEL, SC_WIDTH), SC_KERNEL ** -0.5),
        "mla_q_norm": 1.0 + nrm(ks[4], (L, MLA_Q_RANK), 0.02),
        "mla_kv_norm": 1.0 + nrm(ks[5], (L, MLA_KV_RANK), 0.02),
        "mla_w_uq": nrm(ks[6], (L, MLA_Q_RANK, MLA_HEADS * (MLA_NOPE + MLA_ROPE)), MLA_Q_RANK ** -0.5),
        "mla_w_uk": nrm(ks[7], (L, MLA_KV_RANK, MLA_HEADS * MLA_NOPE), MLA_KV_RANK ** -0.5),
        "mla_w_uv": nrm(ks[8], (L, MLA_KV_RANK, MLA_HEADS * MLA_V), MLA_KV_RANK ** -0.5),
        "cf_dw_w": nrm(ks[9], (L, CF_KERNEL, CF_WIDTH), CF_KERNEL ** -0.5),
        "cf_dw_b": nrm(ks[10], (L, CF_WIDTH), 0.02),
        "cf_ln_g": 1.0 + nrm(ks[11], (L, CF_WIDTH), 0.02),
        "cf_ln_b": nrm(ks[12], (L, CF_WIDTH), 0.02),
        "swa_sinks": nrm(ks[13], (L, SWA_Q_HEADS), 0.5),
        "mix_norm_g": 1.0 + nrm(ks[14], (L, MIX_WIDTH_2), 0.02),
        "w_out": nrm(ks[15], (L, MIX_WIDTH_2, D_MODEL), BETA * MIX_WIDTH_2 ** -0.5),
        "ln1_g": 1.0 + nrm(ks[16], (L, D_MODEL), 0.02),
        "ln1_b": nrm(ks[17], (L, D_MODEL), 0.02),
        "peer_w_q": nrm(ks[18], (L, D_MODEL, PEER_HEADS * PEER_QDIM), D_MODEL ** -0.5),
        "peer_sub_keys": nrm(ks[19], (L, PEER_HEADS, 2, PEER_NKEYS, PEER_HALF), PEER_HALF ** -0.5),
        "peer_u": nrm(ks[20], (L, PEER_EXPERTS, D_MODEL), D_MODEL ** -0.5),
        "peer_v": nrm(ks[21], (L, PEER_EXPERTS, D_MODEL), BETA * PEER_HEADS ** -0.5),
        "ln2_g": 1.0 + nrm(ks[22], (L, D_MODEL), 0.02),
        "ln2_b": nrm(ks[23], (L, D_MODEL), 0.02),
    }

def second_block(x, positions, w_in, sc_conv_w, mla_q_norm, mla_kv_norm, mla_w_uq, mla_w_uk, mla_w_uv,
              cf_dw_w, cf_dw_b, cf_ln_g, cf_ln_b, swa_sinks, mix_norm_g, w_out, ln1_g, ln1_b,
              peer_w_q, peer_sub_keys, peer_u, peer_v, ln2_g, ln2_b):
    b, s, _ = x.shape
    slopes = alibi_slopes_2(SWA_Q_HEADS)
    split_sizes = [SC_WIDTH, SC_WIDTH, SC_WIDTH,
                   MLA_Q_RANK, MLA_KV_RANK, MLA_ROPE,
                   CF_WIDTH, CF_WIDTH,
                   SWA_Q_HEADS * SWA_HEAD_DIM, SWA_KV_HEADS * SWA_HEAD_DIM, SWA_KV_HEADS * SWA_HEAD_DIM]
    pts = _split_points(split_sizes)
    for l in range(DEPTH):
        proj = x @ w_in[l]
        (sc_b, sc_c, sc_h, m_cq, m_ckv, m_kr, cf_a, cf_g, sw_q, sw_k, sw_v) = jnp.split(proj, pts, axis=-1)
        y_sc = short_conv_mixer(sc_b, sc_c, sc_h, sc_conv_w[l])
        y_mla = mla_attention(m_cq, m_ckv, m_kr, positions, mla_q_norm[l], mla_kv_norm[l],
                              mla_w_uq[l], mla_w_uk[l], mla_w_uv[l])
        y_cf = conformer_conv(cf_a, cf_g, cf_dw_w[l], cf_dw_b[l], cf_ln_g[l], cf_ln_b[l])
        y_sw = swa_sink_attention(sw_q, sw_k, sw_v, swa_sinks[l], slopes)
        mix = jnp.concatenate([y_sc, y_mla, y_cf, y_sw], axis=-1)
        mix = rms_norm_2(mix.reshape(b, s, MIX_HEADS, MIX_HEAD_DIM),
                       mix_norm_g[l].reshape(MIX_HEADS, MIX_HEAD_DIM)).reshape(b, s, MIX_WIDTH_2)
        h = layer_norm(ALPHA * x + mix @ w_out[l], ln1_g[l], ln1_b[l])
        x = layer_norm(ALPHA * h + peer_ffn(h, peer_w_q[l], peer_sub_keys[l], peer_u[l], peer_v[l]),
                       ln2_g[l], ln2_b[l])
    return x


def setup_inputs(seed=0):
    out = dict(first_inputs(seed))
    for name, value in second_inputs(seed + 1).items():
        if name != "x":
            out[name + "_2"] = value
    return out


def reference(
    x, attn_norm_g, w_in, ret_decay_fwd, ret_decay_bwd, ret_norm_g, dq_norm_g, dk_norm_g,
    lambda_q1, lambda_k1, lambda_q2, lambda_k2, diff_norm_g, w_out, ffn_norm_g, w_gate, w_up,
    w_down, positions_2, w_in_2, sc_conv_w_2, mla_q_norm_2, mla_kv_norm_2, mla_w_uq_2,
    mla_w_uk_2, mla_w_uv_2, cf_dw_w_2, cf_dw_b_2, cf_ln_g_2, cf_ln_b_2, swa_sinks_2,
    mix_norm_g_2, w_out_2, ln1_g_2, ln1_b_2, peer_w_q_2, peer_sub_keys_2, peer_u_2, peer_v_2,
    ln2_g_2, ln2_b_2,
):
    x = first_block(
        x, attn_norm_g, w_in, ret_decay_fwd, ret_decay_bwd, ret_norm_g, dq_norm_g, dk_norm_g,
        lambda_q1, lambda_k1, lambda_q2, lambda_k2, diff_norm_g, w_out, ffn_norm_g, w_gate,
        w_up, w_down,
    )
    return second_block(
        x, positions_2, w_in_2, sc_conv_w_2, mla_q_norm_2, mla_kv_norm_2, mla_w_uq_2,
        mla_w_uk_2, mla_w_uv_2, cf_dw_w_2, cf_dw_b_2, cf_ln_g_2, cf_ln_b_2, swa_sinks_2,
        mix_norm_g_2, w_out_2, ln1_g_2, ln1_b_2, peer_w_q_2, peer_sub_keys_2, peer_u_2,
        peer_v_2, ln2_g_2, ln2_b_2,
    )


_drawn_inputs = setup_inputs


def setup_inputs(seed=0):
    import zlib

    import numpy as np

    out = dict(_drawn_inputs(seed))
    spreads = {}
    factors = {'ret_norm_g': 3.207,
     'dq_norm_g': 3.043,
     'dk_norm_g': 2.896,
     'diff_norm_g': 2.78,
     'mla_q_norm_2': 8.0,
     'mla_kv_norm_2': 7.001,
     'cf_dw_b_2': 4.803,
     'cf_ln_g_2': 7.205,
     'cf_ln_b_2': 6.94,
     'swa_sinks_2': 8.0,
     'mix_norm_g_2': 4.957}
    for name, (base, spread) in spreads.items():
        noise = np.random.default_rng([zlib.crc32(name.encode()), seed]).standard_normal(out[name].shape)
        drawn = base * np.exp(spread * noise) if base else spread * noise
        out[name] = __import__('jax').numpy.asarray(drawn.astype(out[name].dtype))
    for name, factor in factors.items():
        out[name] = (out[name] * factor).astype(out[name].dtype)
    return out
```

```python
from contextlib import ExitStack

import numpy as np

import concourse.bass as bass
from concourse import mybir

F32 = mybir.dt.float32
F32R = mybir.dt.float32r
BF16 = mybir.dt.bfloat16
U32 = mybir.dt.uint32
I32 = mybir.dt.int32
ALU = mybir.AluOpType
ACT = mybir.ActivationFunctionType
AX_X = mybir.AxisListType.X

P = 128
DEPTH = 2
SEQ = 256
D = 1024
TT = SEQ // P
DT = D // P
CH = 1024
D_FF = 2816
FF_BLOCKS = D_FF // P
EPS1 = 1e-6
EPS2 = 1e-5
ALPHA = (2 * DEPTH) ** 0.25
NEG = -1e30
REPLACED = -3.0e38
PI = 3.14159250

RH = 8
DH = 4
AH = 4
QK = 96
SC_K = 3
CF_K = 31
PH = 8
NK = 128
TOP = 16
QUARTERS = 4
JQ = NK // QUARTERS
GROUP = SEQ // JQ
PIECES = 3

N1 = 8 + 5 * 4 + 8 + 3 * FF_BLOCKS
N2_PRE = 13 + 4 + 1 + 8 + 16
N2 = N2_PRE + 2 * NK
RAW1, PAIR1 = 3, 6
RAW2, PAIR2 = 4, 4
AHEAD = 2
ROT = 4

ROW1 = dict(ret_g=64, dq_g=64, dk_g=64, diff_g=128, lq=128, lk=128, dec=16, lam_init=1, out_scale=1)
ROW2 = dict(ln1_g=D, ln1_b=D, ln2_g=D, ln2_b=D, cf_g=256, cf_b=256, sinks=AH)
COL2 = dict(sc_w=2 * SC_K, cf_w=2 * CF_K, cf_bias=2, mq_g=2, mkv_g=1, mix_g=DT)
SMALL2 = dict(uq=2 * AH * QK, ukv=512)


def spans(fields):
    out, at = {}, 0
    for k, n in fields.items():
        out[k] = (at, at + n)
        at += n
    return out, at


class Banks:

    def __init__(self, plan):
        self.plan = [(name, who) for name, who, _ in plan]
        self.index = {name: i for i, (name, _, _) in enumerate(plan)}
        self.nth = {}
        self.chunks = {}
        count, chunks = {}, 0
        for name, who, n in plan:
            count[who] = count.get(who, 0) + 1
            chunks += n
            self.nth[name] = (who, count[who])
            self.chunks[name] = chunks


def plan1():
    p = [(f"xT{i}", "dve", 0) for i in range(4)]
    p += [(f"qk{i}", "act", 2) for i in range(4)]
    p += [(f"{g}{t}", who, 4 * (t == 0)) for g, who in (("dq", "dve"), ("dk", "dve"), ("rv", "act"), ("dv", "act"),
                                                        ("rg", "act")) for t in range(TT)]
    p += [(f"S{h}", "dve", 0) for h in range(RH)]
    p += [(f"dT{h}", "act", 0) for h in range(DH)]
    p += [(f"sc{k}", "dve", 0) for k in range(2 * DH)]
    p += [(f"aT{h}", "act", 0) for h in range(DH)]
    p += [(f"mT{i}", "dve", 0) for i in range(4)]
    p += [(f"fT{i}", "dve", 8 * (i == 0)) for i in range(4)]
    return Banks(p)


def plan2():
    p = [(f"xT{i}", "dve", 0) for i in range(4)]
    p += [(n, "dve" if n == "sch" else "act", 1 if n == "swk" else 2)
          for n in ("cfa", "cfg", "scc", "sch", "scb", "swq", "swk")]
    p += [("m0", "act", 4), ("m1", "act", 0), ("kr", "act", 1)] + [(f"ws{h}", "dve", 0) for h in range(AH)]
    p += [("cqT", "dve", 0), ("ckvT", "dve", 0)] + [(n, "act", 0) for n in ("uq0", "uq1", "kv0", "kv1")]
    p += [(f"wT{h}", "act", 0) for h in range(AH)]
    p += [(f"kT{h}", "act", 0) for h in range(AH)]
    p += [(f"ms{h}", "dve", 0) for h in range(AH)]
    p += [(f"pT{h}", "act", 0) for h in range(AH)]
    p += [("scT", "act", 0), ("cvT", "act", 0)]
    p += [(f"mT{i}", "dve", 0) for i in range(4)]
    p += [(f"hT{i}", "dve", 8 * (i == 0)) for i in range(4)]
    p += [("q0", "act", 2)]
    for h in range(PH):
        p += ([(f"q{h + 1}", "act", 2)] if h + 1 < PH else []) + [(f"rs{h}", "act", 0)]
    p += [("iT", "act", 0), ("gT", "act", 0)]
    return Banks(p)


def two_blocks_kernel(nc, x_in, pos_in, s1, col1, row1, s2, col2, row2, small2, sub2, inv_in, out):
    r1, NR1 = spans(ROW1)
    r2, NR2 = spans(ROW2)
    c2, NC2 = spans(COL2)
    m2, NM2 = spans(SMALL2)
    with ExitStack() as ctx:
        def sb(name, shape, dt=F32):
            return ctx.enter_context(nc.sbuf_tensor(name, shape, dt))

        def sem(name):
            return ctx.enter_context(nc.semaphore(name))

        x_res = sb("x_res", [P, TT, D])
        hT_hi = sb("hT_hi", [P, DT, SEQ], F32R)
        hT_lo = sb("hT_lo", [P, DT, SEQ], F32R)
        raw = sb("raw", [P, max(RAW1, RAW2), CH])
        w_hi = sb("w_hi", [P, max(PAIR1, PAIR2), CH], F32R)
        w_lo = sb("w_lo", [P, max(PAIR1, PAIR2), CH], F32R)
        ident = sb("ident", [P, P])
        iota_k = sb("iota_k", [P, NK])
        iota_b = sb("iota_b", [P, NK], BF16)
        rel = sb("rel", [P, 3 * P])
        after = sb("after", [P, 3 * P])
        before = sb("before", [P, 3 * P])
        absd = sb("absd", [P, 3 * P])
        causal = sb("causal", [P, 3 * P])
        window = sb("window", [P, AH, 3 * P])
        cos_t = sb("cos_t", [P, TT, 16])
        sin_t = sb("sin_t", [P, TT, 16])
        eps1 = sb("eps1", [P, 1])
        eps2 = sb("eps2", [P, 1])
        col1_sb = sb("col1_sb", [P, 2 * DT])
        row2_sb = sb("row2_sb", [P, NR2])
        row1_sb = row2_sb[:, 0:NR1]
        col2_sb = sb("col2_sb", [P, NC2])
        i1T = sb("i1T", [P, SEQ], BF16)
        i2T = sb("i2T", [P, SEQ], BF16)
        hidw_hi = sb("hidw_hi", [P, 2, SEQ], F32R)
        hidw_lo = sb("hidw_lo", [P, 2, SEQ], F32R)
        one_i = sb("one_i", [P, 2, GROUP, NK], BF16)
        one_j = sb("one_j", [P, 2, GROUP, JQ], BF16)
        gate_j = sb("gate_j", [P, 2, GROUP, PIECES, JQ], BF16)
        ARENA = 18400
        arena = sb("arena", [P, ARENA])
        used = [0]

        def carve(*shape):
            n = int(np.prod(shape))
            a = arena[:, used[0]:used[0] + n]
            used[0] += n
            assert used[0] <= ARENA, used[0]
            if len(shape) == 1:
                return a
            names = "abcd"[:len(shape)]
            return a.rearrange(f"p ({' '.join(names)}) -> p {' '.join(names)}", **dict(zip(names[1:], shape[1:])))

        used[0] = ARENA - 2 * 512 - 256 - 384
        hid = carve(2, SEQ)
        gated_hid = carve(2, SEQ)
        gT = carve(SEQ)
        g_part = carve(PIECES * SEQ // 2).bitcast(BF16).rearrange("p (m t) -> p m t", m=PIECES)
        used[0] = 0

        xn = carve(TT, D)
        rqkT = carve(8, SEQ)
        ret = rqkT[:, 0:4, :].rearrange("p k t -> p (k t)").rearrange("p (t c) -> p t c", t=TT)
        rv = carve(TT, 512)
        rgate = carve(TT, 512)
        dqk = carve(TT, 2, 512)
        dv = carve(TT, 512)
        decay_flat = carve(RH * 3 * P)
        decay = decay_flat.rearrange("p (h c) -> p h c", h=RH)
        dqkT = decay_flat[:, 0:DH * 2 * SEQ].rearrange("p (h k t) -> p h k t", h=DH, k=2)
        scm = carve(2, TT, SEQ)
        attnT = scm
        prob = carve(4, 2, SEQ)
        sq = prob[:, 0:2].rearrange("p k m c -> p k (m c)")
        attn = carve(4, SEQ)
        mix = xn
        st1 = carve(456)
        ss_x, std_x, rstd_x = st1[:, 0:2], st1[:, 2:4], st1[:, 4:6]
        ss_r, std_r, rstd_r = (st1[:, 256 + 16 * k:272 + 16 * k].rearrange("p (t g) -> p t g", t=TT) for k in range(3))
        ss_d, std_d, rstd_d = (st1[:, 304 + 8 * k:312 + 8 * k].rearrange("p (t g) -> p t g", t=TT) for k in range(3))
        gd = st1[:, 328:456]
        ss_g = st1[:, 8:40].rearrange("p (t b g) -> p t b g", t=TT, b=2)
        std_g = st1[:, 40:72].rearrange("p (t b g) -> p t b g", t=TT, b=2)
        rstd_g = st1[:, 72:104].rearrange("p (t b g) -> p t b g", t=TT, b=2)
        negmax = st1[:, 104:120].rearrange("p (k m) -> p k m", m=2)
        sums = st1[:, 120:136].rearrange("p (k m) -> p k m", m=2)
        rsum = st1[:, 136:152].rearrange("p (k m) -> p k m", m=2)
        rowmax = st1[:, 152:168].rearrange("p (k m) -> p k m", m=2)
        dece = st1[:, 168:184]
        lam_s, lam_e, lam = st1[:, 184:186], st1[:, 186:188], st1[:, 188:189]
        lam_d = st1[:, 189:190]
        gq = st1[:, 192:256]
        used1, used[0] = used[0], 0

        mix2 = carve(TT, D)
        hpre = mix2
        small_sb = carve(NM2)
        sub_sb = carve(2 * PH, NK)
        st2 = carve(328)
        routing_from = used[0]
        cfa = carve(2, SEQ)
        cvt = cfa.rearrange("p k t -> p (k t)").rearrange("p (t c) -> p t c", t=TT)
        cfg = carve(2, SEQ)
        cqT = cfg
        cv = carve(2, SEQ)
        scc = carve(2, SEQ)
        ckvT = scc[:, 0, :]
        scy = carve(2, SEQ)
        early = carve(AH * 2 * SEQ)
        cfu = early[:, 0:572].rearrange("p (k t) -> p k t", k=2)
        scu = early[:, 572:1088].rearrange("p (k t) -> p k t", k=2)
        scb = early[:, 1088:1600].rearrange("p (k t) -> p k t", k=2)
        swqk = carve(3, SEQ)
        qkT = early[:, 0:AH * 2 * SEQ].rearrange("p (h k t) -> p h k t", h=AH, k=2)
        mtok = carve(TT, 512)
        krt = carve(TT, 32)
        qtok = carve(TT, AH, QK)
        kcat = carve(TT, AH, QK)
        vtok = carve(TT, AH, 64)
        prob2 = carve(4, TT, SEQ)
        sq2 = prob2[:, 0:2].rearrange("p k t c -> p (k t c)")
        probT = carve(2, TT, SEQ)
        rt = carve(4, AH, 16)
        used[0] = routing_from
        pqT = carve(2, 2, SEQ)
        rs = carve(PH, TT, 2, NK)
        rs2 = carve(TT, 2, NK)
        cand = carve(TT, TOP * TOP)
        cand2 = carve(TT, TOP * TOP)
        eq = carve(PH, TOP, TOP)
        topv = carve(PH, TT, 2, TOP)
        topf = carve(PH, TT, 2, TOP)
        best = carve(PH, TT, TOP)
        bestf = carve(2, PH, TT, TOP)
        chosen = carve(3, TT, PH * TOP)
        topi = carve(PH, TT, 2, TOP).bitcast(U32)
        besti = carve(PH, TT, TOP).bitcast(U32)
        bestab = carve(2, PH, TT, TOP).bitcast(U32)
        gsum = carve(2, PH)
        used[0] = 0
        gates = carve(2, SEQ, JQ)
        a_c2 = st2
        ss_m, std_m, rstd_m = a_c2[:, 0:4], a_c2[:, 4:8], a_c2[:, 8:12]
        bn = a_c2[:, 12:36].rearrange("p (t c s) -> p t c s", t=TT, c=2)
        mv = a_c2[:, 36:40].rearrange("p (t s) -> p t s", t=TT)
        std_l, rstd_l = a_c2[:, 40:42], a_c2[:, 42:44]
        negmax2 = a_c2[:, 44:60].rearrange("p (k m) -> p k m", m=2)
        sums2 = a_c2[:, 60:76].rearrange("p (k m) -> p k m", m=2)
        rsum2 = a_c2[:, 76:92].rearrange("p (k m) -> p k m", m=2)
        rowmax2 = a_c2[:, 92:108].rearrange("p (k m) -> p k m", m=2)
        esink = a_c2[:, 108:116].rearrange("p (k m) -> p k m", m=2)
        ss_x2 = a_c2[:, 120:152].rearrange("p (t g) -> p t g", t=TT)
        std_x2 = a_c2[:, 152:184].rearrange("p (t g) -> p t g", t=TT)
        rstd_x2 = a_c2[:, 184:216].rearrange("p (t g) -> p t g", t=TT)
        invf, pos_f = a_c2[:, 216:232], a_c2[:, 232:234]
        pos_i = a_c2[:, 234:236].bitcast(I32)
        turns = a_c2[:, 240:304].rearrange("p (b t f) -> p b t f", b=2, t=TT)
        angle = a_c2[:, 304:320]
        nsink = a_c2[:, 320:324]
        turn_n = rt.rearrange("p (b t) h f -> p b t h f", b=2)[:, :, :, 0, :]
        ypre = gates.rearrange("p q a b -> p (q a b)")[:, 0:TT * D].rearrange("p (t d) -> p t d", t=TT)
        st3 = sb("st3", [P, 64])
        bn3 = st3[:, 0:24].rearrange("p (t c s) -> p t c s", t=TT, c=2)
        mv3 = st3[:, 24:28].rearrange("p (t s) -> p t s", t=TT)
        std3, rstd3 = st3[:, 28:30], st3[:, 30:32]

        ps = ctx.enter_context(nc.psum_tensor("ps", [P, 8, 512], F32))
        acc = [ps[:, i, :] for i in range(4)]

        const_ready = sem("const_ready")
        setup_in = sem("setup_in")
        rel_ready = sem("rel_ready")
        turn_step = sem("turn_step")
        turn_ready = sem("turn_ready")
        setup_done = sem("setup_done")
        opened = sem("opened")
        out_done = sem("out_done")
        arrived = {n: sem(f"{n}_arrived") for n in ("pe", "act", "dve", "pool")}
        first = sem("layer_first")
        entered = {n: sem(f"{n}_entered") for n in ("pe", "act", "dve", "pool")}
        par_ready = sem("par_ready")
        w_ready = [sem(f"w_ready{i}") for i in range(max(RAW1, RAW2))]
        hi_ready = sem("hi_ready")
        lo_ready = sem("lo_ready")
        w_used = sem("w_used")
        xhi_ready = sem("xhi_ready")
        gate_step = sem("gate_step")
        onehot_step = sem("onehot_step")
        bank_full = sem("bank_full")
        emptied = dict(act=sem("act_emptied"), dve=sem("dve_emptied"))
        dve_step = sem("dve_step")
        act_step = sem("act_step")
        ms_ready = sem("ms_ready")
        std_ready = sem("std_ready")
        rows_ready = sem("rows_ready")
        dec_ready = sem("dec_ready")
        dist_ready = sem("dist_ready")
        decay_ready = sem("decay_ready")
        lam_ready = sem("lam_ready")
        lame_ready = sem("lame_ready")
        out_full = sem("out_full")
        ret_copied = sem("ret_copied")
        dqk_ready = sem("dqk_ready")
        negmax_ready = sem("negmax_ready")
        exp_ready = sem("exp_ready")
        attn_ready = sem("attn_ready")
        hid_full = sem("hid_full")
        hid_ready = sem("hid_ready")
        hidw_ready = sem("hidw_ready")
        conv_ready = sem("conv_ready")
        cfg_ready = sem("cfg_ready")
        cfmix_ready = sem("cfmix_ready")
        rope_ready = sem("rope_ready")
        cn_ready = sem("cn_ready")
        score_ready = sem("score_ready")
        gexp_ready = sem("gexp_ready")
        chosen_ready = sem("chosen_ready")
        onehot_ready = sem("onehot_ready")
        onehot_used = sem("onehot_used")
        gates_out = sem("gates_out")
        last = sem("layer_last")
        banks1, banks2 = plan1(), plan2()

        def bank(banks, name):
            return ps[:, 4 + banks.index[name] % ROT, :]

        def open_bank(pe, banks, name):
            i = banks.index[name]
            if i >= ROT:
                who, n = banks.nth[banks.plan[i - ROT][0]]
                pe.wait_ge(emptied[who], n)
            return bank(banks, name)

        def take_bank(eng, banks, name):
            eng.wait_ge(bank_full, banks.index[name] + 1)
            return bank(banks, name)

        def after_emptied(eng, banks, name):
            who, n = banks.nth[name]
            eng.wait_ge(emptied[who], n)

        class Steps:

            def __init__(self, eng, s):
                self.eng, self.s, self.n = eng, s, 0

            def __call__(self, ins):
                ins.then_inc(self.s, 1)
                self.n += 1

            def settle(self):
                self.eng.wait_ge(self.s, self.n)

        def enter_layer(eng, name, n):
            eng.wait_ge(opened, n)
            eng.sem_inc(entered[name], 1)

        def leave_layer(eng, name, s, n):
            eng.wait_ge(s, n)
            eng.sem_inc(arrived[name], 1)

        block = ctx.enter_context(nc.Block())

        @block.sync
        def _(sp):
            sp.dma_start(x_res[:], x_in.rearrange("(t p) d -> p t d", p=P)).then_inc(setup_in, 16)
            with nc.allow_non_contiguous_dma(reason="256 positions"):
                sp.dma_start(pos_i, pos_in.rearrange("(t p) -> p t", p=P)).then_inc(setup_in, 16)
            sp.dma_start(invf, inv_in.partition_broadcast(P)).then_inc(setup_in, 16)

            def load_layer(l, stream, n, slots, params):
                for dst, src in params:
                    sp.dma_start(dst, src).then_inc(par_ready, 16)
                head = slots + n % slots

                def load(c, slot):
                    sp.dma_start(raw[:, slot, :], stream[l, c]).then_inc(w_ready[slot], 16)

                for c in range(head):
                    if c >= slots:
                        sp.wait_ge(lo_ready, c - slots + 1)
                    load(c, c % slots)
                with sp.Fori(0, (n - head) // slots) as i:
                    for k in range(slots):
                        sp.wait_ge(lo_ready, i * slots + (head + k - slots + 1))
                        load(i * slots + (head + k), (head + k) % slots)

            def turn(n):
                for s in arrived.values():
                    sp.wait_ge(s, n)
                sp.sem_inc(first, 1)
                sp.wait_ge(first, 1)
                sp.sem_clear(range(first.num, last.num + 1))
                sp.sem_inc(opened, 1)

            sp.wait_ge(setup_done, 1)
            sp.sem_inc(opened, 1)
            with sp.Fori(0, DEPTH) as l:
                load_layer(l, s1, N1, RAW1, ((col1_sb[:], col1[l]), (row1_sb, row1[l].partition_broadcast(P))))
                turn(l + 1)
            with sp.Fori(0, DEPTH) as l:
                load_layer(l, s2, N2, RAW2, ((col2_sb[:], col2[l]), (row2_sb[:], row2[l].partition_broadcast(P)),
                                            (small_sb, small2[l]), (sub_sb, sub2[l])))
                turn(l + 1 + DEPTH)
            sp.dma_start(out.rearrange("(t p) d -> p t d", p=P), x_res[:]).then_inc(out_done, 16)
            sp.wait_ge(out_done, 16)

        @block.gpsimd
        def _(pool):
            pool.memset(ident[:], 0.0).then_inc(const_ready, 1)
            pool.iota(iota_k[:], pattern=[[1, NK]], base=0, channel_multiplier=0,
                      allow_small_or_imprecise_dtypes=True).then_inc(rel_ready, 1)
            pool.iota(rel[:], pattern=[[1, 3 * P]], base=-P, channel_multiplier=-1,
                      allow_small_or_imprecise_dtypes=True).then_inc(rel_ready, 1)
            pool.wait_ge(const_ready, 1)
            pool.affine_select(out=ident[:], in_=ident[:], compare_op=ALU.not_equal, fill=1.0, base=0,
                               pattern=[[-1, P]], channel_multiplier=1).then_inc(const_ready, 1)
            pool.memset(causal[:], 0.0).then_inc(const_ready, 1)
            pool.wait_ge(const_ready, 3)
            pool.affine_select(out=causal[:], in_=causal[:], compare_op=ALU.is_ge, fill=NEG, base=P,
                               pattern=[[-1, 3 * P]], channel_multiplier=1).then_inc(const_ready, 1)
            pool.wait_ge(rel_ready, 2)
            for h in range(AH):
                pool.tensor_scalar(window[:, h], rel[:], 2.0 ** (-2.0 * (h + 1)), 0.0, ALU.mult,
                                   ALU.add).then_inc(const_ready, 1)
            pool.wait_ge(const_ready, 4 + AH)
            for h in range(AH):
                pool.affine_select(out=window[:, h], in_=window[:, h], compare_op=ALU.is_ge, fill=NEG, base=P,
                                   pattern=[[-1, 3 * P]], channel_multiplier=1).then_inc(const_ready, 1)
            pool.wait_ge(const_ready, 4 + 2 * AH)
            for h in range(AH):
                pool.affine_select(out=window[:, h], in_=window[:, h], compare_op=ALU.is_gt, fill=NEG, base=0,
                                   pattern=[[1, 3 * P]], channel_multiplier=-1).then_inc(const_ready, 1)
            pool.iota(iota_b[:], pattern=[[1, NK]], base=0, channel_multiplier=0,
                      allow_small_or_imprecise_dtypes=True).then_inc(const_ready, 1)
            pool.memset(eps1[:], EPS1).then_inc(const_ready, 1)
            pool.memset(eps2[:], EPS2).then_inc(const_ready, 1)

            def split_layer(n, raws, pairs):
                def one(c, at):
                    pool.wait_ge(hi_ready, c + 1)
                    if at >= pairs:
                        pool.wait_ge(w_used, c - pairs + 1)
                    pool.tensor_tensor(w_lo[:, at % pairs, :], raw[:, at % raws, :], w_hi[:, at % pairs, :].bitcast(F32),
                                       ALU.subtract).then_inc(lo_ready, 1)

                turn = max(raws, pairs)
                head = turn + n % turn
                for c in range(head):
                    one(c, c)
                with pool.Fori(0, (n - head) // turn) as i:
                    for k in range(turn):
                        one(i * turn + (head + k), head + k)

            for n, sizes in ((1, (N1, RAW1, PAIR1)), (1 + DEPTH, (N2, RAW2, PAIR2))):
                with pool.Fori(0, DEPTH) as l:
                    enter_layer(pool, "pool", l + n)
                    split_layer(*sizes)
                    leave_layer(pool, "pool", lo_ready, sizes[0])

        CONSTS = 4 + 3 * AH + 3
        LAST_SUMS = 2 + 2 * TT + 1

        @block.tensor
        def _(pe):
            class Stream:

                def __init__(self, slots):
                    self.slots, self.c, self.owed = slots, 0, 0

                def take(self):
                    pe.wait_ge(lo_ready, self.c + 1)
                    slot = self.c % self.slots
                    self.c += 1
                    return w_hi[:, slot, :], w_lo[:, slot, :]

                def mm(self, o, lhsT, rhs, start, stop, signal=None):
                    ins = nc.tensor.matmul(o, lhsT, rhs, start=start, stop=stop)
                    if signal is not None:
                        ins.then_inc(signal, 1)
                    elif self.owed:
                        ins.then_inc(w_used, self.owed)
                        self.owed = 0
                    return ins

                def mm3(self, o, a, b, start, stop, signal=None):
                    self.mm(o, a[0], b[0], start, False)
                    self.mm(o, a[0], b[1], False, False)
                    return self.mm(o, a[1], b[0], False, stop, signal)

            def part(pair, *at):
                return tuple(x[at] for x in pair)

            hT = (hT_hi, hT_lo)
            ALL = slice(None)

            def transpose_rows(banks, name, src):
                for i in range(4):
                    b = open_bank(pe, banks, f"{name}{i}")
                    for k in range(2):
                        for t in range(TT):
                            f = 2 * i + k
                            ins = nc.tensor.transpose(b[:, k * SEQ + t * P:k * SEQ + (t + 1) * P],
                                                      src[:, t, f * P:(f + 1) * P], ident[:])
                    ins.then_inc(bank_full, 1)
                for i in range(4):
                    after_emptied(pe, banks, f"{name}{i}")

            def feature_block(w, o, signal):
                ww = [x.rearrange("p (d c) -> p d c", d=DT) for x in w.take()]
                for d in range(DT):
                    end = d == DT - 1
                    w.mm3(o, part(ww, ALL, d), part(hT, ALL, d), d == 0, end, signal if end else None)
                w.owed += 1

            def token_group(w, outs, signal):
                for c in range(DT // 2):
                    ww = [x.rearrange("p (d c) -> p d c", d=2) for x in w.take()]
                    for t in range(TT):
                        for k in range(2):
                            d = 2 * c + k
                            end = d == DT - 1
                            w.mm3(outs[t], part(hT, ALL, d, slice(t * P, (t + 1) * P)), part(ww, ALL, k), d == 0, end,
                                  signal if end else None)
                    w.owed += 1

            def hidden_blocks(w, n, ups, unroll, done, begin, finish, beside=None):
                per = ups + 1
                base = w.c

                def chunk(at, i):
                    pe.wait_ge(lo_ready, i * (unroll * per) + (base + at + 1))
                    slot = (base + at) % w.slots
                    return w_hi[:, slot, :], w_lo[:, slot, :]

                def way_in(at, i, parity, owed):
                    o = ps[:, 4 + parity, :]
                    for k in range(ups):
                        ww = [x.rearrange("p (d c) -> p d c", d=DT) for x in chunk(at + k, i)]
                        w.owed += owed
                        owed = 0
                        for d in range(DT):
                            w.mm3(o[:, k * SEQ:(k + 1) * SEQ], part(ww, ALL, d), part(hT, ALL, d), d == 0, d == DT - 1,
                                  None if d < DT - 1 else hid_full if k == ups - 1 else w_used)

                def way_out(at, i, parity, u, owed, start, stop):
                    ww = chunk(at, i)
                    pe.wait_ge(hidw_ready, i * unroll + (done + u + 1))
                    w.owed += owed
                    for t in range(TT):
                        for c in range(2):
                            end = t == TT - 1 and c == 1
                            w.mm3(acc[2 * t + c], (hidw_hi[:, parity, t * P:(t + 1) * P], hidw_lo[:, parity, t * P:(t + 1) * P]),
                                  part(ww, ALL, slice(c * 512, (c + 1) * 512)), start, stop,
                                  None if not end else out_full if stop else w_used)

                def one_pass(i, is_first=False, is_last=False):
                    for u in range(unroll):
                        at = ups + u * per
                        more = not (is_last and u == unroll - 1)
                        if more:
                            way_in(at, i, (u + 1) % 2, 0)
                        if beside is not None:
                            beside(i, u)
                        way_out(at + ups if more else at, i, u % 2, u, (2 if is_first and u == 0 else 1) if more else 0,
                                begin and is_first and u == 0, finish and not more)

                owed, w.owed = w.owed, 0
                way_in(0, 0, 0, owed)
                one_pass(0, is_first=True)
                with pe.Fori(1, n // unroll - 1) as i:
                    one_pass(i)
                one_pass(n // unroll - 1, is_last=True)
                w.c += n * per

            def block1():
                B = banks1
                w = Stream(PAIR1)
                pe.wait_ge(rows_ready, TT)
                transpose_rows(B, "xT", xn)
                for i in range(4):
                    b = open_bank(pe, B, f"qk{i}")
                    for k in range(2):
                        feature_block(w, b[:, k * SEQ:(k + 1) * SEQ], bank_full if k else None)
                for g in ("dq", "dk", "rv", "dv", "rg"):
                    token_group(w, [open_bank(pe, B, f"{g}{t}") for t in range(TT)], bank_full)

                def ret_scores(h):
                    b = open_bank(pe, B, f"S{h}")
                    r = slice(64 * (h % 2), 64 * (h % 2) + 64)
                    for s in range(TT):
                        w.mm(b[:, s * SEQ:(s + 1) * SEQ], rqkT[r, 4 + h // 2, s * P:(s + 1) * P],
                             rqkT[r, h // 2, :], True, True, bank_full if s else None)

                def ret_out(h):
                    after_emptied(pe, B, f"S{h}")
                    for t in range(TT):
                        for s in range(TT):
                            end = h == RH - 1 and t == TT - 1 and s == TT - 1
                            w.mm(acc[t][:, h * 64:(h + 1) * 64], scm[:, h % 2, s, t * P:(t + 1) * P],
                                 rv[:, s, h * 64:(h + 1) * 64], s == 0, s == TT - 1, out_full if end else None)

                after_emptied(pe, B, "qk3")
                ret_scores(0)
                after_emptied(pe, B, "rv1")
                for h in range(RH):
                    if h + 1 < RH:
                        ret_scores(h + 1)
                    ret_out(h)

                pe.wait_ge(dqk_ready, 1)
                for h in range(DH):
                    b = open_bank(pe, B, f"dT{h}")
                    for k in range(2):
                        for t in range(TT):
                            ins = nc.tensor.transpose(b[:, k * SEQ + t * P:k * SEQ + (t + 1) * P],
                                                      dqk[:, t, k, h * P:(h + 1) * P], ident[:])
                    ins.then_inc(bank_full, 1)
                for k in range(2 * DH):
                    h, m = k // 2, k % 2
                    b = open_bank(pe, B, f"sc{k}")
                    after_emptied(pe, B, f"dT{h}")
                    r = slice(64 * m, 64 * m + 64)
                    for t in range(TT):
                        w.mm(b[:, t * SEQ:(t + 1) * SEQ], dqkT[r, h, 0, t * P:(t + 1) * P], dqkT[r, h, 1, :],
                             True, True, bank_full if t else None)

                def diff_out(h):
                    after_emptied(pe, B, f"aT{h}")
                    for t in range(TT):
                        for s in range(TT):
                            end = h == DH - 1 and t == TT - 1 and s == TT - 1
                            w.mm(acc[2 + t][:, h * P:(h + 1) * P], attnT[:, h % 2, s, t * P:(t + 1) * P],
                                 dv[:, s, h * P:(h + 1) * P], s == 0, s == TT - 1, out_full if end else None)

                for h in range(DH):
                    b = open_bank(pe, B, f"aT{h}")
                    pe.wait_ge(attn_ready, TT * (h + 1))
                    for s in range(TT):
                        for t in range(TT):
                            ins = nc.tensor.transpose(b[:, s * SEQ + t * P:s * SEQ + (t + 1) * P],
                                                      attn[:, (TT * h + t) % 4, s * P:(s + 1) * P], ident[:])
                    ins.then_inc(bank_full, 1)
                    if h >= 1:
                        diff_out(h - 1)
                diff_out(DH - 1)

                pe.wait_ge(rows_ready, 2 * TT)
                transpose_rows(B, "mT", mix)
                for c in range(2):
                    token_group(w, [acc[2 * t + c] for t in range(TT)], out_full)

                pe.wait_ge(rows_ready, 3 * TT)
                transpose_rows(B, "fT", xn)
                hidden_blocks(w, FF_BLOCKS, 2, 2, 0, True, True)

            def block2():
                B = banks2
                w = Stream(PAIR2)
                transpose_rows(B, "xT", x_res)
                for name in ("cfa", "cfg", "scc", "sch", "scb", "swq", "swk"):
                    b = open_bank(pe, B, name)
                    n = 1 if name == "swk" else 2
                    for k in range(n):
                        feature_block(w, b[:, k * SEQ:(k + 1) * SEQ], bank_full if k == n - 1 else None)
                token_group(w, [open_bank(pe, B, f"m{t}") for t in range(TT)], bank_full)
                b = open_bank(pe, B, "kr")
                ww = [x[:, 0:DT * 32].rearrange("p (d c) -> p d c", d=DT) for x in w.take()]
                for t in range(TT):
                    for d in range(DT):
                        end = t == TT - 1 and d == DT - 1
                        w.mm3(b[:, t * 32:(t + 1) * 32], part(hT, ALL, d, slice(t * P, (t + 1) * P)), part(ww, ALL, d),
                              d == 0, d == DT - 1, bank_full if end else None)
                w.owed += 1

                after_emptied(pe, B, "swk")
                for h in range(AH):
                    b = open_bank(pe, B, f"ws{h}")
                    r = slice(64 * (h // 2), 64 * (h // 2) + 64)
                    for t in range(TT):
                        w.mm(b[:, t * SEQ:(t + 1) * SEQ], swqk[r, h % 2, t * P:(t + 1) * P], swqk[r, 2, :],
                             True, True, bank_full if t else None)

                pe.wait_ge(cn_ready, 1)
                b = open_bank(pe, B, "cqT")
                for k in range(2):
                    for t in range(TT):
                        ins = nc.tensor.transpose(b[:, k * SEQ + t * P:k * SEQ + (t + 1) * P],
                                                  mtok[:, t, k * P:(k + 1) * P], ident[:])
                ins.then_inc(bank_full, 1)
                b = open_bank(pe, B, "ckvT")
                for t in range(TT):
                    ins = nc.tensor.transpose(b[:, t * P:(t + 1) * P], mtok[:, t, 2 * P:3 * P], ident[:])
                ins.then_inc(bank_full, 1)
                pe.wait_ge(par_ready, 64)
                uq = small_sb[:, slice(*m2["uq"])].rearrange("p (k c) -> p k c", k=2)
                after_emptied(pe, B, "cqT")
                for t in range(TT):
                    b = open_bank(pe, B, f"uq{t}")
                    for k in range(2):
                        w.mm(b[:, 0:AH * QK], cqT[:, k, t * P:(t + 1) * P], uq[:, k, :], k == 0, k == 1,
                             bank_full if k else None)
                after_emptied(pe, B, "ckvT")
                for t in range(TT):
                    b = open_bank(pe, B, f"kv{t}")
                    w.mm(b, ckvT[:, t * P:(t + 1) * P], small_sb[:, slice(*m2["ukv"])], True, True, bank_full)

                def attend(k0, name, values, sums):
                    def outs(h):
                        after_emptied(pe, B, f"{name}{h}")
                        for t in range(TT):
                            for s in range(t + 1):
                                end = h == AH - 1 and t == TT - 1 and s == t
                                w.mm(sums[t][:, h * 64:(h + 1) * 64], probT[:, h % 2, s, t * P:(t + 1) * P],
                                     values(s, h), s == 0, s == t, out_full if end else None)

                    for h in range(AH):
                        b = open_bank(pe, B, f"{name}{h}")
                        pe.wait_ge(exp_ready, k0 + h + 1)
                        for s in range(TT):
                            for t in range(TT):
                                ins = nc.tensor.transpose(b[:, s * SEQ + t * P:s * SEQ + (t + 1) * P],
                                                          prob2[:, (k0 + h) % 4, t, s * P:(s + 1) * P], ident[:])
                        ins.then_inc(bank_full, 1)
                        if h >= 1:
                            outs(h - 1)
                    outs(AH - 1)

                attend(0, "wT", lambda s, h: mtok[:, s, 384 + 64 * (h // 2):448 + 64 * (h // 2)], acc[2:4])

                pe.wait_ge(rope_ready, 1)
                for h in range(AH):
                    b = open_bank(pe, B, f"kT{h}")
                    for k, src in ((0, qtok), (1, kcat)):
                        for t in range(TT):
                            ins = nc.tensor.transpose(b[0:QK, k * SEQ + t * P:k * SEQ + (t + 1) * P],
                                                      src[:, t, h, :], ident[:])
                    ins.then_inc(bank_full, 1)
                for h in range(AH):
                    b = open_bank(pe, B, f"ms{h}")
                    after_emptied(pe, B, f"kT{h}")
                    for t in range(TT):
                        w.mm(b[:, t * SEQ:(t + 1) * SEQ], qkT[0:QK, h, 0, t * P:(t + 1) * P], qkT[0:QK, h, 1, :],
                             True, True, bank_full if t else None)
                attend(AH, "pT", lambda s, h: vtok[:, s, h, :], acc[0:2])

                pe.wait_ge(conv_ready, 2)
                for name, src in (("scT", scy), ("cvT", cv)):
                    b = open_bank(pe, B, name)
                    for t in range(TT):
                        for k in range(2):
                            ins = nc.tensor.transpose(b[:, t * SEQ + k * P:t * SEQ + (k + 1) * P],
                                                      src[:, k, t * P:(t + 1) * P], ident[:])
                    ins.then_inc(bank_full, 1)

                pe.wait_ge(rows_ready, TT)
                transpose_rows(B, "mT", mix2)
                for c in range(2):
                    token_group(w, [acc[2 * t + c] for t in range(TT)], out_full)

                pe.wait_ge(rows_ready, 2 * TT)
                transpose_rows(B, "hT", x_res)

                def queries(h):
                    b = open_bank(pe, B, f"q{h}")
                    for k in range(2):
                        feature_block(w, b[:, k * SEQ:(k + 1) * SEQ], bank_full if k else None)

                def key_scores(h):
                    b = open_bank(pe, B, f"rs{h}")
                    after_emptied(pe, B, f"q{h}")
                    for t in range(TT):
                        for k in range(2):
                            at = (2 * t + k) * NK
                            w.mm(b[:, at:at + NK], pqT[:, h % 2, k, t * P:(t + 1) * P], sub_sb[:, 2 * h + k, :],
                                 True, True, bank_full if t and k else None)

                queries(0)
                for h in range(PH):
                    if h + 1 < PH:
                        queries(h + 1)
                    key_scores(h)

                pe.wait_ge(chosen_ready, 1)
                for name, parts in (("iT", (0, 1)), ("gT", (2,))):
                    b = open_bank(pe, B, name)
                    for k, c in enumerate(parts):
                        for t in range(TT):
                            ins = nc.tensor.transpose(b[:, k * SEQ + t * P:k * SEQ + (t + 1) * P], chosen[:, c, t, :],
                                                      ident[:])
                    ins.then_inc(bank_full, 1)
                after_emptied(pe, B, "gT")

                def gate_group(q, i, u, unroll, free):
                    b = ps[:, 6 + u % 2, :]
                    if free:
                        pe.wait_ge(gates_out, i * unroll + (q * JQ + u - 1))
                    pe.wait_ge(onehot_ready, i * unroll + (q * JQ + u + 1))
                    for k in range(GROUP):
                        for m in range(PIECES):
                            ins = nc.tensor.matmul(b[:, k * JQ:(k + 1) * JQ], one_i[:, u % 2, k, :],
                                                   gate_j[:, u % 2, k, m, :], start=m == 0, stop=m == PIECES - 1)
                    ins.then_inc(onehot_used, 1)

                for u in range(4):
                    gate_group(0, 0, u, 4, u >= 2)
                with pe.Fori(1, JQ // 4) as i:
                    for u in range(4):
                        gate_group(0, i, u, 4, True)
                for q in range(QUARTERS):
                    hidden_blocks(w, JQ, 1, 4, q * JQ, q == 0, q == QUARTERS - 1,
                                  (lambda i, u: gate_group(q + 1, i, u, 4, True)) if q + 1 < QUARTERS else None)

            pe.wait_ge(const_ready, CONSTS)
            for n, layer in ((1, block1), (1 + DEPTH, block2)):
                with pe.Fori(0, DEPTH) as l:
                    enter_layer(pe, "pe", l + n)
                    layer()
                    leave_layer(pe, "pe", out_full, LAST_SUMS)

        @block.scalar
        def _(act):
            A = nc.scalar.activation

            def root(n, std, ms, scale, eps):
                act.wait_ge(ms_ready, n)
                A(std, ms, ACT.Sqrt, bias=eps[:, 0:1], scale=scale).then_inc(std_ready, 1)

            class Split:

                def __init__(self, raws, pairs, head):
                    self.raws, self.pairs, self.head, self.c = raws, pairs, head, 0

                def one(self, c, i=0, step=0):
                    slot = c % self.raws
                    act.wait_ge(w_ready[slot], i * (16 * step // self.raws) + 16 * (c // self.raws + 1))
                    if c >= self.pairs:
                        act.wait_ge(w_used, i * step + (c - self.pairs + 1))
                    A(w_hi[:, c % self.pairs, :], raw[:, slot, :], ACT.Copy).then_inc(hi_ready, 1)

                def upto(self, n):
                    n = min(n + AHEAD, self.head)
                    for c in range(self.c, n):
                        self.one(c)
                    self.c = max(self.c, n)

            def filled(B, w, name):
                w.upto(B.chunks[name])
                return take_bank(act, B, name)

            def empty_transposed(B, w, name, scale):
                for i in range(4):
                    b = filled(B, w, f"{name}{i}")
                    if scale is None:
                        ins = A(hT_hi[:, 2 * i:2 * i + 2, :], b.rearrange("p (k t) -> p k t", k=2), ACT.Copy)
                    else:
                        for k in range(2):
                            f = 2 * i + k
                            ins = A(hT_hi[:, f, :], b[:, k * SEQ:(k + 1) * SEQ], ACT.Copy, scale=scale[:, f:f + 1])
                    ins.then_inc(xhi_ready, 1)

            def empty(B, w, name, dst, n=512, func=ACT.Copy, scale=1.0):
                b = filled(B, w, name)
                A(dst, b[:, 0:n], func, scale=scale).then_inc(emptied["act"], 1)

            def hidden(w, base, n, ups, unroll, done, func, finish, beside=None):
                per = ups + 1

                def one(i, u, free, ahead):
                    for k in range(ahead):
                        w.one(base + ups + per * u + k, i, unroll * per)
                    act.wait_ge(hid_full, i * unroll + (done + u + 1))
                    if free:
                        act.wait_ge(hidw_ready, i * unroll + (done + u - 1))
                    A(hid[:, u % 2, :], ps[:, 4 + u % 2, 0:SEQ], func).then_inc(hid_ready, 1)
                    if beside is not None:
                        beside(i, u)

                passes = n // unroll
                for u in range(unroll):
                    one(0, u, done > 0 or u >= 2, per)
                with act.Fori(1, passes - 1) as i:
                    for u in range(unroll):
                        one(i, u, True, per)
                for u in range(unroll):
                    one(passes - 1, u, True, per - ups if finish and u == unroll - 1 else per)

            def block1():
                B = banks1
                base = N1 - 3 * FF_BLOCKS
                w = Split(RAW1, PAIR1, base + 2)
                act.wait_ge(par_ready, 32)
                A(dece, row1_sb[:, slice(*r1["dec"])], ACT.Exp).then_inc(dec_ready, 1)
                act.wait_ge(lam_ready, 1)
                A(lam_e, lam_s, ACT.Exp).then_inc(lame_ready, 1)
                root(1, std_x, ss_x, 1.0 / D, eps1)
                empty_transposed(B, w, "xT", col1_sb[:, 0:DT])
                for i in range(4):
                    empty(B, w, f"qk{i}", rqkT[:, 2 * i:2 * i + 2, :].rearrange("p k t -> p (k t)"),
                          scale=1.0 if i < 2 else 64 ** -0.5)
                act.wait_ge(dist_ready, 1)
                A(decay, decay, ACT.Exp, scale=-1.0).then_inc(decay_ready, 1)
                for t in range(TT):
                    empty(B, w, f"rv{t}", rv[:, t, :])
                root(2, std_g, ss_g, 1.0 / 64, eps1)
                for t in range(TT):
                    empty(B, w, f"dv{t}", dv[:, t, :])
                for t in range(TT):
                    empty(B, w, f"rg{t}", rgate[:, t, :], func=ACT.Silu)
                act.wait_ge(out_full, 1)
                for t in range(TT):
                    nc.scalar.copy(ret[:, t, :], acc[t]).then_inc(ret_copied, 1)
                for h in range(DH):
                    empty(B, w, f"dT{h}", dqkT[:, h].rearrange("p k t -> p (k t)"))

                def exps(k):
                    act.wait_ge(negmax_ready, k + 1)
                    for m in range(2):
                        ins = A(prob[:, k % 4, m, :], prob[:, k % 4, m, :], ACT.Exp, bias=negmax[:, k, m:m + 1],
                                accum_out=sums[:, k, m:m + 1])
                    ins.then_inc(exp_ready, 1)

                for k in range(4):
                    exps(k)
                for h in range(DH):
                    empty(B, w, f"aT{h}", attnT[:, h % 2].rearrange("p s t -> p (s t)"))
                    if h < 2:
                        exps(4 + 2 * h)
                        exps(5 + 2 * h)
                root(3, std_r, ss_r, 1.0 / 64, eps1)
                root(4, std_d, ss_d, 1.0 / 128, eps1)
                empty_transposed(B, w, "mT", None)
                w.upto(B.chunks["fT0"])
                root(5, std_x, ss_x, 1.0 / D, eps1)
                empty_transposed(B, w, "fT", col1_sb[:, DT:2 * DT])
                hidden(w, base, FF_BLOCKS, 2, 2, 0, ACT.Silu, True)

            def block2():
                B = banks2
                w = Split(RAW2, PAIR2, N2_PRE + 1)
                sinks = row2_sb[:, slice(*r2["sinks"])]
                act.wait_ge(par_ready, 64)
                empty_transposed(B, w, "xT", None)
                flat = lambda x: x.rearrange("p k t -> p (k t)")
                empty(B, w, "cfa", flat(cfa))
                empty(B, w, "cfg", flat(cfg), func=ACT.Sigmoid)
                empty(B, w, "scc", flat(scc))
                empty(B, w, "scb", flat(scb))
                empty(B, w, "swq", flat(swqk[:, 0:2, :]))
                empty(B, w, "swk", swqk[:, 2, :], n=SEQ)
                for t in range(TT):
                    empty(B, w, f"m{t}", mtok[:, t, :])
                empty(B, w, "kr", flat(krt), n=TT * 32)
                root(1, std_m, ss_m, 1.0, eps2)

                def exps(k):
                    act.wait_ge(negmax_ready, k + 1)
                    for t in range(TT):
                        ins = A(prob2[:, k % 4, t, :], prob2[:, k % 4, t, :], ACT.Exp, bias=negmax2[:, k, t:t + 1],
                                accum_out=sums2[:, k, t:t + 1])
                    if k < AH:
                        ins = A(esink[:, k, :], negmax2[:, k, :], ACT.Exp, bias=sinks[:, k:k + 1])
                    ins.then_inc(exp_ready, 1)

                for h in range(AH):
                    exps(h)
                for t in range(TT):
                    empty(B, w, f"uq{t}", qtok[:, t].rearrange("p h c -> p (h c)"), n=AH * QK)
                for t in range(TT):
                    b = filled(B, w, f"kv{t}").rearrange("p (k h c) -> p k h c", k=2, h=AH)
                    nc.scalar.copy(kcat[:, t, :, 0:64], b[:, 0])
                    nc.scalar.copy(vtok[:, t], b[:, 1]).then_inc(emptied["act"], 1)
                for h in range(AH):
                    empty(B, w, f"wT{h}", flat(probT[:, h % 2]))
                for h in range(AH):
                    b = filled(B, w, f"kT{h}")
                    A(flat(qkT[0:QK, h]), b[0:QK, :], ACT.Copy).then_inc(emptied["act"], 1)
                for h in range(AH):
                    exps(AH + h)
                for h in range(AH):
                    empty(B, w, f"pT{h}", flat(probT[:, h % 2]))
                b = filled(B, w, "scT")
                nc.scalar.copy(mix2[:, :, 0:256], b.rearrange("p (t c) -> p t c", t=TT)).then_inc(emptied["act"], 1)
                empty(B, w, "cvT", flat(cvt))
                root(2, std_l, mv[:, :, 1], 1.0, eps2)
                act.wait_ge(cfg_ready, 1)
                A(mix2[:, :, 512:768], cvt, ACT.Silu).then_inc(cfmix_ready, 1)
                root(3, std_x2, ss_x2, 1.0 / 64, eps2)
                empty_transposed(B, w, "mT", col2_sb[:, slice(*c2["mix_g"])])
                w.upto(B.chunks["hT0"])
                root(4, std_l, mv[:, :, 1], 1.0, eps2)
                empty_transposed(B, w, "hT", None)

                def queries(h):
                    empty(B, w, f"q{h}", flat(pqT[:, h % 2]))

                queries(0)
                for h in range(PH):
                    if h + 1 < PH:
                        queries(h + 1)
                    empty(B, w, f"rs{h}", rs[:, h].rearrange("p t k n -> p (t k n)"))
                act.wait_ge(score_ready, 1)
                A(chosen[:, 2], chosen[:, 2], ACT.Exp).then_inc(gexp_ready, 1)
                b = filled(B, w, "iT")
                nc.scalar.copy(i1T[:], b[:, 0:SEQ])
                nc.scalar.copy(i2T[:], b[:, SEQ:2 * SEQ]).then_inc(emptied["act"], 1)
                empty(B, w, "gT", gT[:], n=SEQ)

                def gates_of(q, i, u):
                    act.wait_ge(onehot_used, i * 4 + (q * JQ + u + 1))
                    at = i * (4 * GROUP) + u * GROUP
                    tokens = slice(at, at + GROUP) if isinstance(i, int) else bass.ds(at, GROUP)
                    nc.scalar.copy(gates[:, q % 2, tokens, :], ps[:, 6 + u % 2, 0:GROUP * JQ].rearrange(
                        "p (t j) -> p t j", t=GROUP)).then_inc(gates_out, 1)

                for u in range(4):
                    gates_of(0, 0, u)
                with act.Fori(1, JQ // 4) as i:
                    for u in range(4):
                        gates_of(0, i, u)
                for q in range(QUARTERS):
                    def gates_before(i, u):
                        if u > 0:
                            gates_of(q + 1, i, u - 1)
                        elif not (isinstance(i, int) and i == 0):
                            gates_of(q + 1, i - 1, 3)

                    more = q + 1 < QUARTERS
                    hidden(w, N2_PRE + 2 * q * JQ, JQ, 1, 4, q * JQ, ACT.Gelu, not more, gates_before if more else None)
                    if more:
                        gates_of(q + 1, JQ // 4 - 1, 3)
                root(5, std3, mv3[:, :, 1], 1.0, eps2)

            act.wait_ge(const_ready, CONSTS)
            act.wait_ge(turn_ready, 1)
            A(sin_t[:], turns[:, 0], ACT.Sin)
            A(cos_t[:], turns[:, 1], ACT.Sin).then_inc(setup_done, 1)
            for n, layer, s, m in ((1, block1, hid_ready, FF_BLOCKS), (1 + DEPTH, block2, std_ready, 5)):
                with act.Fori(0, DEPTH) as l:
                    enter_layer(act, "act", l + n)
                    layer()
                    leave_layer(act, "act", s, m)

        @block.vector
        def _(dve):
            V = nc.vector

            def setup():
                step = Steps(dve, turn_step)
                dve.wait_ge(rel_ready, 2)
                step(V.tensor_scalar(after[:], rel[:], 0.0, None, ALU.max))
                step(V.tensor_scalar(before[:], rel[:], -1.0, 0.0, ALU.mult, ALU.max))
                dve.wait_ge(setup_in, 48)
                step(V.tensor_copy(pos_f, pos_i))
                step.settle()
                step(V.tensor_tensor(absd[:], after[:], before[:], ALU.add))
                two_pi = 2 * np.pi
                parts = [6.28125]
                parts.append(float(np.float32(np.round((two_pi - parts[0]) * 2 ** 22) / 2 ** 22)))
                parts.append(float(np.float32(two_pi - parts[0] - parts[1])))
                big = 1.5 * 2 ** 23
                for t in range(TT):
                    step(V.tensor_scalar(angle, invf, pos_f[:, t:t + 1], None, ALU.mult))
                    step.settle()
                    for b in range(2):
                        r, n = turns[:, b, t, :], turn_n[:, b, t, :]
                        step(V.tensor_scalar(n, angle, float(1 / two_pi), 0.25 * b, ALU.mult, ALU.add))
                        step.settle()
                        step(V.tensor_scalar(n, n, big, None, ALU.add))
                        step.settle()
                        step(V.tensor_scalar(n, n, -big, None, ALU.add))
                        step.settle()
                        for k, c in enumerate(parts):
                            step(V.scalar_tensor_tensor(out=r, in0=n, scalar=-c, in1=angle if k == 0 else r,
                                                        op0=ALU.mult, op1=ALU.add))
                            step.settle()
                        step(V.tensor_scalar(r, r, float(np.pi / 2) * b, PI, ALU.add, ALU.min))
                        step.settle()
                        step(V.tensor_scalar(r, r, -PI, None, ALU.max))
                        step.settle()
                dve.sem_inc(turn_ready, 1)

            class Transposed:

                def __init__(self):
                    self.n = 0

                def __call__(self, B, name, scale):
                    for i in range(4):
                        self.n += 1
                        dve.wait_ge(xhi_ready, self.n)
                        b = bank(B, f"{name}{i}")
                        if scale is None:
                            f = slice(2 * i, 2 * i + 2)
                            ins = V.tensor_tensor(hT_lo[:, f, :], b.rearrange("p (k t) -> p k t", k=2),
                                                  hT_hi[:, f, :].bitcast(F32), ALU.subtract)
                        else:
                            for k in range(2):
                                f = 2 * i + k
                                ins = V.scalar_tensor_tensor(out=hT_lo[:, f, :], in0=b[:, k * SEQ:(k + 1) * SEQ],
                                                             scalar=scale[:, f:f + 1], in1=hT_hi[:, f, :].bitcast(F32),
                                                             op0=ALU.mult, op1=ALU.subtract)
                        ins.then_inc(emptied["dve"], 1)

            def gated(i, unroll, u, done, base, ups, gate, free):
                s = u % 2
                dve.wait_ge(hid_ready, i * unroll + (done + u + 1))
                if free:
                    dve.wait_ge(w_used, i * (unroll * (ups + 1)) + (base + (ups + 1) * (u - 1) + ups))
                V.tensor_tensor(gated_hid[:, s, :], hid[:, s, :], gate, ALU.mult).then_inc(gate_step, 1)
                V.tensor_tensor(hidw_hi[:, s, :], hid[:, s, :], gate, ALU.mult).then_inc(gate_step, 1)
                dve.wait_ge(gate_step, i * (2 * unroll) + 2 * (done + u + 1))
                V.tensor_tensor(hidw_lo[:, s, :], gated_hid[:, s, :], hidw_hi[:, s, :].bitcast(F32),
                                ALU.subtract).then_inc(hidw_ready, 1)

            def root_of(step, n):
                step.settle()
                dve.sem_inc(ms_ready, 1)
                dve.wait_ge(std_ready, n)

            def over(x, n):
                return x.unsqueeze(2).broadcast_to([P, x.shape[1], n])

            def under(x, g):
                return x.unsqueeze(1).broadcast_to([P, g, x.shape[1]])

            def grouped(x, g):
                return x.rearrange("p (g c) -> p g c", g=g)

            def slice_of(t):
                return slice(P - t * P, P - t * P + SEQ)

            def norm_x(step, n):
                for t in range(TT):
                    step(V.tensor_tensor_reduce(out=xn[:, t, :], in0=x_res[:, t, :], in1=x_res[:, t, :], scale=1.0,
                                                scalar=0.0, op0=ALU.mult, op1=ALU.add, accum_out=ss_x[:, t:t + 1]))
                root_of(step, n)
                step(V.reciprocal(rstd_x, std_x))
                step.settle()
                for t in range(TT):
                    V.tensor_scalar(xn[:, t, :], x_res[:, t, :], rstd_x[:, t:t + 1], None,
                                    ALU.mult).then_inc(rows_ready, 1)

            def block1():
                B = banks1
                step = Steps(dve, dve_step)
                empty_transposed = Transposed()
                par = lambda k: row1_sb[:, slice(*r1[k])]
                dve.wait_ge(par_ready, 32)
                lq, lk = par("lq"), par("lk")
                for m in range(2):
                    s = slice(64 * m, 64 * m + 64)
                    step(V.tensor_tensor_reduce(out=sq[:, 0, s], in0=lq[:, s], in1=lk[:, s], scale=1.0, scalar=0.0,
                                                op0=ALU.mult, op1=ALU.add, accum_out=lam_s[:, m:m + 1]))
                step(V.tensor_scalar(gq, par("dq_g"), 64 ** -0.5, None, ALU.mult))
                step(V.tensor_scalar(gd, par("diff_g"), par("out_scale"), None, ALU.mult))
                step.settle()
                dve.sem_inc(lam_ready, 1)
                norm_x(step, 1)
                dve.wait_ge(lame_ready, 1)
                step(V.tensor_tensor(lam_d, lam_e[:, 0:1], lam_e[:, 1:2], ALU.subtract))
                step.settle()
                step(V.tensor_tensor(lam, lam_d, par("lam_init"), ALU.add))
                dve.wait_ge(dec_ready, 1)
                for h in range(RH):
                    step(V.tensor_scalar(decay[:, h], after[:], dece[:, h:h + 1], None, ALU.mult))
                empty_transposed(B, "xT", col1_sb[:, 0:DT])
                step.settle()
                for h in range(RH):
                    step(V.scalar_tensor_tensor(out=decay[:, h], in0=before[:], scalar=dece[:, RH + h:RH + h + 1],
                                                in1=decay[:, h], op0=ALU.mult, op1=ALU.add))
                step.settle()
                dve.sem_inc(dist_ready, 1)

                for k, g in enumerate(("dq", "dk")):
                    for t in range(TT):
                        b = take_bank(dve, B, f"{g}{t}")
                        V.tensor_copy(dqk[:, t, k, :], b).then_inc(emptied["dve"], 1)
                    for t in range(TT):
                        after_emptied(dve, B, f"{g}{t}")
                        step(V.tensor_tensor(sq[:, t, :], dqk[:, t, k, :], dqk[:, t, k, :], ALU.mult))
                    step.settle()
                    for t in range(TT):
                        step(V.tensor_reduce(ss_g[:, t, k, :], grouped(sq[:, t, :], 8), AX_X, ALU.add))
                root_of(step, 2)
                step(V.reciprocal(rstd_g, std_g))
                step.settle()
                for k in range(2):
                    for t in range(TT):
                        x = grouped(dqk[:, t, k, :], 8)
                        step(V.tensor_tensor(x, x, over(rstd_g[:, t, k, :], 64), ALU.mult))
                step.settle()
                for k in range(2):
                    for t in range(TT):
                        x = grouped(dqk[:, t, k, :], 8)
                        ins = V.tensor_tensor(x, x, under(gq if k == 0 else par("dk_g"), 8), ALU.mult)
                ins.then_inc(dqk_ready, 1)

                dve.wait_ge(decay_ready, 1)
                for h in range(RH):
                    b = take_bank(dve, B, f"S{h}")
                    for s in range(TT):
                        ins = V.tensor_tensor(scm[:, h % 2, s, :], b[:, s * SEQ:(s + 1) * SEQ], decay[:, h, slice_of(s)],
                                              ALU.mult)
                    ins.then_inc(emptied["dve"], 1)

                def biased(k):
                    h = k // 2
                    b = take_bank(dve, B, f"sc{k}")
                    if h >= 2:
                        dve.wait_ge(attn_ready, TT * (h - 1))
                    for t in range(TT):
                        ins = V.scalar_tensor_tensor(out=prob[:, k % 4, t, :], in0=absd[:, slice_of(t)],
                                                     scalar=-(2.0 ** (-2.0 * (h + 1))), in1=b[:, t * SEQ:(t + 1) * SEQ],
                                                     op0=ALU.mult, op1=ALU.add)
                    ins.then_inc(emptied["dve"], 1)
                    after_emptied(dve, B, f"sc{k}")
                    step(V.tensor_reduce(rowmax[:, k, :], prob[:, k % 4], AX_X, ALU.max))
                    step.settle()
                    V.tensor_scalar(negmax[:, k, :], rowmax[:, k, :], -1.0, None, ALU.mult).then_inc(negmax_ready, 1)

                def difference(h):
                    dve.wait_ge(exp_ready, 2 * h + 2)
                    one, two = 2 * h, 2 * h + 1
                    step(V.reciprocal(rsum[:, one:two + 1, :], sums[:, one:two + 1, :]))
                    step.settle()
                    step(V.tensor_scalar(rsum[:, two, :], rsum[:, two, :], lam, None, ALU.mult))
                    step.settle()
                    if h >= 2:
                        dve.wait_ge(bank_full, B.index[f"aT{h - 2}"] + 1)
                    slots = [(TT * h + t) % 4 for t in range(TT)]
                    for t in range(TT):
                        step(V.tensor_scalar(attn[:, slots[t], :], prob[:, two % 4, t, :], rsum[:, two, t:t + 1], None,
                                             ALU.mult))
                    step.settle()
                    for t in range(TT):
                        V.scalar_tensor_tensor(out=attn[:, slots[t], :], in0=prob[:, one % 4, t, :],
                                               scalar=rsum[:, one, t:t + 1], in1=attn[:, slots[t], :],
                                               op0=ALU.mult, op1=ALU.subtract).then_inc(attn_ready, 1)

                for h in range(DH):
                    biased(2 * h)
                    biased(2 * h + 1)
                    if h >= 1:
                        difference(h - 1)
                difference(DH - 1)

                dve.wait_ge(ret_copied, TT)
                for t in range(TT):
                    step(V.tensor_tensor(sq[:, t, :], ret[:, t, :], ret[:, t, :], ALU.mult))
                step.settle()
                for t in range(TT):
                    step(V.tensor_reduce(ss_r[:, t, :], grouped(sq[:, t, :], RH), AX_X, ALU.add))
                root_of(step, 3)
                step(V.reciprocal(rstd_r, std_r))
                step.settle()
                after_emptied(dve, B, "rg1")
                for t in range(TT):
                    x = grouped(ret[:, t, :], RH)
                    step(V.tensor_tensor(x, x, over(rstd_r[:, t, :], 64), ALU.mult))
                step.settle()
                for t in range(TT):
                    x = grouped(ret[:, t, :], RH)
                    step(V.tensor_tensor(x, x, under(par("ret_g"), RH), ALU.mult))
                step.settle()
                for t in range(TT):
                    step(V.tensor_tensor(mix[:, t, 0:512], ret[:, t, :], rgate[:, t, :], ALU.mult))
                dve.wait_ge(out_full, 2)
                for t in range(TT):
                    step(V.tensor_copy(mix[:, t, 512:D], acc[2 + t]))
                step.settle()
                for t in range(TT):
                    step(V.tensor_tensor(sq[:, t, :], mix[:, t, 512:D], mix[:, t, 512:D], ALU.mult))
                step.settle()
                for t in range(TT):
                    step(V.tensor_reduce(ss_d[:, t, :], grouped(sq[:, t, :], DH), AX_X, ALU.add))
                root_of(step, 4)
                step(V.reciprocal(rstd_d, std_d))
                step.settle()
                for t in range(TT):
                    x = grouped(mix[:, t, 512:D], DH)
                    step(V.tensor_tensor(x, x, over(rstd_d[:, t, :], P), ALU.mult))
                step.settle()
                for t in range(TT):
                    x = grouped(mix[:, t, 512:D], DH)
                    V.tensor_tensor(x, x, under(gd, DH), ALU.mult).then_inc(rows_ready, 1)
                empty_transposed(B, "mT", None)

                for c in range(2):
                    dve.wait_ge(out_full, 2 + TT * (c + 1))
                    for t in range(TT):
                        x = x_res[:, t, c * 512:(c + 1) * 512]
                        step(V.tensor_tensor(x, x, acc[2 * t + c], ALU.add))
                step.settle()
                norm_x(step, 5)
                empty_transposed(B, "fT", col1_sb[:, DT:2 * DT])

                base = N1 - 3 * FF_BLOCKS
                up = lambda u: ps[:, 4 + u, SEQ:2 * SEQ]
                for u in range(2):
                    gated(0, 2, u, 0, base, 2, up(u), False)
                with dve.Fori(1, FF_BLOCKS // 2) as i:
                    for u in range(2):
                        gated(i, 2, u, 0, base, 2, up(u), True)
                dve.wait_ge(out_full, LAST_SUMS)
                for t in range(TT):
                    for c in range(2):
                        x = x_res[:, t, c * 512:(c + 1) * 512]
                        step(V.tensor_tensor(x, x, acc[2 * t + c], ALU.add))
                return step.n

            def layer_norm(step, n, dst, g, b, stats, mean_var, std, rstd, signal):
                for t in range(TT):
                    for c in range(2):
                        x = slice(c * 512, (c + 1) * 512)
                        step(V.scalar_tensor_tensor(out=dst[:, t, x], in0=x_res[:, t, x], scalar=ALPHA, in1=acc[2 * t + c],
                                                    op0=ALU.mult, op1=ALU.add))
                step.settle()
                for t in range(TT):
                    for c in range(2):
                        step(V.bn_stats(stats[:, t, c, :], dst[:, t, c * 512:(c + 1) * 512]))
                step.settle()
                for t in range(TT):
                    step(V.bn_aggr(mean_var[:, t, :], stats[:, t].rearrange("p c s -> p (c s)")))
                root_of(step, n)
                step(V.reciprocal(rstd, std))
                step.settle()
                for t in range(TT):
                    step(V.tensor_scalar(x_res[:, t, :], dst[:, t, :], mean_var[:, t, 0:1], rstd[:, t:t + 1],
                                         ALU.subtract, ALU.mult))
                step.settle()
                for t in range(TT):
                    step(V.tensor_tensor(x_res[:, t, :], x_res[:, t, :], g, ALU.mult))
                step.settle()
                for t in range(TT):
                    ins = V.tensor_tensor(x_res[:, t, :], x_res[:, t, :], b, ALU.add)
                    if signal is not None:
                        ins.then_inc(signal, 1)
                    else:
                        step(ins)

            def block2():
                B = banks2
                step = Steps(dve, dve_step)
                empty_transposed = Transposed()
                par = lambda k: row2_sb[:, slice(*r2[k])]
                col = lambda k: col2_sb[:, slice(*c2[k])]
                dve.wait_ge(par_ready, 64)
                step(V.memset(cfu[:, :, 0:CF_K - 1], 0.0))
                step(V.memset(scu[:, :, 0:SC_K - 1], 0.0))
                step(V.tensor_scalar(nsink, par("sinks"), -1.0, None, ALU.mult))
                empty_transposed(B, "xT", None)

                after_emptied(dve, B, "cfg")
                step(V.tensor_tensor(cfu[:, :, CF_K - 1:], cfa, cfg, ALU.mult))
                after_emptied(dve, B, "scc")
                b = take_bank(dve, B, "sch")
                V.tensor_tensor(scu[:, :, SC_K - 1:], b.rearrange("p (k t) -> p k t", k=2), scc,
                                ALU.mult).then_inc(emptied["dve"], 1)
                after_emptied(dve, B, "sch")

                def conv(dst, src, taps, w, bias):
                    step.settle()
                    for k in range(taps):
                        for c in range(2):
                            x, tap = src[:, c, k:k + SEQ], w[:, c * taps + k:c * taps + k + 1]
                            if k == 0:
                                step(V.tensor_scalar(dst[:, c, :], x, tap, 0.0 if bias is None else bias[:, c:c + 1],
                                                     ALU.mult, ALU.add))
                            else:
                                step(V.scalar_tensor_tensor(out=dst[:, c, :], in0=x, scalar=tap, in1=dst[:, c, :],
                                                            op0=ALU.mult, op1=ALU.add))
                        step.settle()

                conv(scy, scu, SC_K, col("sc_w"), None)
                after_emptied(dve, B, "scb")
                V.tensor_tensor(scy, scy, scb, ALU.mult).then_inc(conv_ready, 1)
                conv(cv, cfu, CF_K, col("cf_w"), col("cf_bias"))
                dve.sem_inc(conv_ready, 1)

                after_emptied(dve, B, "m1")
                parts = ((0, 256), (256, 384))
                for t in range(TT):
                    for k, (a, z) in enumerate(parts):
                        x = mtok[:, t, a:z]
                        step(V.tensor_tensor_reduce(out=sq2[:, t * 512 + a:t * 512 + z], in0=x, in1=x, scale=1.0 / (z - a),
                                                    scalar=0.0, op0=ALU.mult, op1=ALU.add,
                                                    accum_out=ss_m[:, 2 * t + k:2 * t + k + 1]))
                root_of(step, 1)
                step(V.reciprocal(rstd_m, std_m))
                step.settle()
                for t in range(TT):
                    for k, (a, z) in enumerate(parts):
                        step(V.tensor_scalar(mtok[:, t, a:z], mtok[:, t, a:z], rstd_m[:, 2 * t + k:2 * t + k + 1], None,
                                             ALU.mult))
                step.settle()
                dve.sem_inc(cn_ready, 1)

                def biased(k):
                    h, sinks = k % AH, k < AH
                    name = f"ws{h}" if sinks else f"ms{h}"
                    b = take_bank(dve, B, name)
                    if k >= 4:
                        dve.wait_ge(bank_full, B.index[f"wT{h}"] + 1)
                    for t in range(TT):
                        mask = window[:, h, slice_of(t)] if sinks else causal[:, slice_of(t)]
                        ins = V.scalar_tensor_tensor(out=prob2[:, k % 4, t, :], in0=b[:, t * SEQ:(t + 1) * SEQ],
                                                     scalar=(64 if sinks else QK) ** -0.5, in1=mask,
                                                     op0=ALU.mult, op1=ALU.add)
                    ins.then_inc(emptied["dve"], 1)
                    after_emptied(dve, B, name)
                    step(V.tensor_reduce(rowmax2[:, k, :], prob2[:, k % 4], AX_X, ALU.max))
                    step.settle()
                    if sinks:
                        ins = V.tensor_scalar(negmax2[:, k, :], rowmax2[:, k, :], -1.0, nsink[:, h:h + 1], ALU.mult, ALU.min)
                    else:
                        ins = V.tensor_scalar(negmax2[:, k, :], rowmax2[:, k, :], -1.0, None, ALU.mult)
                    ins.then_inc(negmax_ready, 1)

                for k in range(AH):
                    biased(k)
                for name, dst, n, g in (("cqT", cqT, 2, "mq_g"), ("ckvT", ckvT.unsqueeze(1), 1, "mkv_g")):
                    b = take_bank(dve, B, name)
                    for k in range(n):
                        ins = V.tensor_scalar(dst[:, k, :], b[:, k * SEQ:(k + 1) * SEQ], col(g)[:, k:k + 1], None, ALU.mult)
                    ins.then_inc(emptied["dve"], 1)
                dve.wait_ge(exp_ready, AH)
                step(V.tensor_tensor(sums2[:, 0:AH, :], sums2[:, 0:AH, :], esink, ALU.add))
                step.settle()
                step(V.reciprocal(rsum2[:, 0:AH, :], sums2[:, 0:AH, :]))

                def rotate(x1, x2, cos, sin, n):
                    r = [rt[:, k, 0:n, :] for k in range(4)]
                    step.settle()
                    for o, x, w in ((0, x1, cos), (1, x2, sin), (2, x2, cos), (3, x1, sin)):
                        step(V.tensor_tensor(r[o], x, w, ALU.mult))
                    step.settle()
                    step(V.tensor_tensor(x1, r[0], r[1], ALU.subtract))
                    step(V.tensor_tensor(x2, r[2], r[3], ALU.add))

                after_emptied(dve, B, "kv1")
                for t in range(TT):
                    q = qtok[:, t]
                    rotate(q[:, :, 64:80], q[:, :, 80:96], under(cos_t[:, t, :], AH), under(sin_t[:, t, :], AH), AH)
                    k = krt[:, t, :].unsqueeze(1)
                    rotate(k[:, :, 0:16], k[:, :, 16:32], under(cos_t[:, t, :], 1), under(sin_t[:, t, :], 1), 1)
                step.settle()
                for t in range(TT):
                    ins = V.tensor_copy(kcat[:, t, :, 64:96], under(krt[:, t, :], AH))
                ins.then_inc(rope_ready, 1)

                for k in range(AH, 2 * AH):
                    biased(k)

                after_emptied(dve, B, "cvT")
                for t in range(TT):
                    step(V.bn_stats(bn[:, t, 0, :], cvt[:, t, :]))
                step.settle()
                for t in range(TT):
                    step(V.bn_aggr(mv[:, t, :], bn[:, t, 0, :]))
                root_of(step, 2)
                step(V.reciprocal(rstd_l, std_l))
                step.settle()
                for t in range(TT):
                    step(V.tensor_scalar(cvt[:, t, :], cvt[:, t, :], mv[:, t, 0:1], rstd_l[:, t:t + 1], ALU.subtract, ALU.mult))
                step.settle()
                step(V.tensor_tensor(cvt, cvt, under(par("cf_g"), TT), ALU.mult))
                step.settle()
                step(V.tensor_tensor(cvt, cvt, under(par("cf_b"), TT), ALU.add))
                step.settle()
                dve.sem_inc(cfg_ready, 1)

                dve.wait_ge(exp_ready, 2 * AH)
                step(V.reciprocal(rsum2[:, AH:, :], sums2[:, AH:, :]))
                step.settle()
                dve.wait_ge(out_full, 2)
                for t in range(TT):
                    for at, a, k in ((256, acc[t], AH), (768, acc[2 + t], 0)):
                        step(V.tensor_tensor(grouped(mix2[:, t, at:at + 256], AH), grouped(a[:, 0:256], AH),
                                             over(rsum2[:, k:k + AH, t], 64), ALU.mult))
                dve.wait_ge(cfmix_ready, 1)
                for t in range(TT):
                    step.settle()
                    step(V.tensor_tensor(sq2, mix2[:, t, :], mix2[:, t, :], ALU.mult))
                    step.settle()
                    step(V.tensor_reduce(ss_x2[:, t, :], grouped(sq2, 16), AX_X, ALU.add))
                root_of(step, 3)
                step(V.reciprocal(rstd_x2, std_x2))
                step.settle()
                for t in range(TT):
                    x = grouped(mix2[:, t, :], 16)
                    V.tensor_tensor(x, x, over(rstd_x2[:, t, :], 64), ALU.mult).then_inc(rows_ready, 1)
                empty_transposed(B, "mT", col("mix_g"))
                dve.wait_ge(out_full, 2 + 2 * TT)
                layer_norm(step, 4, hpre, par("ln1_g"), par("ln1_b"), bn, mv, std_l, rstd_l, rows_ready)
                empty_transposed(B, "hT", None)

                def top16(vals, idx, src, src2):
                    n = range(len(src))
                    step.settle()
                    for i in n:
                        step(V.max(vals[i][:, 0:8], src[i]))
                    step.settle()
                    for i in n:
                        step(V.max_index(idx[i][:, 0:8], vals[i][:, 0:8], src[i]))
                        step(V.match_replace(src2[i], vals[i][:, 0:8], src[i], REPLACED))
                    step.settle()
                    for i in n:
                        step(V.max(vals[i][:, 8:16], src2[i]))
                    step.settle()
                    for i in n:
                        step(V.max_index(idx[i][:, 8:16], vals[i][:, 8:16], src2[i]))

                for h in range(PH):
                    after_emptied(dve, B, f"rs{h}")
                    sides = [(t, k) for t in range(TT) for k in range(2)]
                    top16([topv[:, h, t, k, :] for t, k in sides], [topi[:, h, t, k, :] for t, k in sides],
                          [rs[:, h, t, k, :] for t, k in sides], [rs2[:, t, k, :] for t, k in sides])
                    for t in range(TT):
                        step(V.tensor_tensor(grouped(cand[:, t, :], TOP), over(topv[:, h, t, 0, :], TOP),
                                             under(topv[:, h, t, 1, :], TOP), ALU.add))
                    step.settle()
                    top16([best[:, h, t, :] for t in range(TT)], [besti[:, h, t, :] for t in range(TT)],
                          [cand[:, t, :] for t in range(TT)], [cand2[:, t, :] for t in range(TT)])
                step.settle()
                gate = chosen[:, 2].rearrange("p t (h k) -> p t h k", h=PH)
                for t in range(TT):
                    step(V.tensor_tensor(gate[:, t], best[:, :, t, :], best[:, :, t, 0:1].broadcast_to([P, PH, TOP]),
                                         ALU.subtract))
                step(V.tensor_scalar(bestab[:, 0], besti, 4, None, ALU.logical_shift_right))
                step(V.tensor_scalar(bestab[:, 1], besti, TOP - 1, None, ALU.bitwise_and))
                step(V.tensor_copy(topf, topi))
                step.settle()
                dve.sem_inc(score_ready, 1)
                step(V.tensor_copy(bestf, bestab))
                places = iota_k[:, 0:TOP].unsqueeze(1).unsqueeze(1).broadcast_to([P, PH, TOP, TOP])
                for t in range(TT):
                    for k in range(2):
                        step.settle()
                        step(V.tensor_tensor(eq, places, bestf[:, k, :, t, :].unsqueeze(3).broadcast_to([P, PH, TOP, TOP]),
                                             ALU.is_equal))
                        step.settle()
                        step(V.tensor_tensor(eq, eq, topf[:, :, t, k, :].unsqueeze(2).broadcast_to([P, PH, TOP, TOP]),
                                             ALU.mult))
                        step.settle()
                        step(V.tensor_reduce(chosen[:, k, t, :].rearrange("p (h k) -> p h k", h=PH), eq, AX_X, ALU.add))
                dve.wait_ge(gexp_ready, 1)
                for t in range(TT):
                    step(V.tensor_reduce(gsum[:, t, :], gate[:, t], AX_X, ALU.add))
                step.settle()
                step(V.reciprocal(gsum, gsum))
                step.settle()
                for t in range(TT):
                    step(V.tensor_tensor(gate[:, t], gate[:, t], over(gsum[:, t, :], TOP), ALU.mult))
                step.settle()
                dve.sem_inc(chosen_ready, 1)
                after_emptied(dve, B, "gT")

                for m in range(PIECES):
                    step(V.tensor_copy(g_part[:, m, :], gT[:]))
                    step.settle()
                    if m + 1 < PIECES:
                        step(V.tensor_tensor(gT[:], gT[:], g_part[:, m, :], ALU.subtract))
                        step.settle()

                def onehots(q, i, u, free):
                    if free:
                        dve.wait_ge(onehot_used, i * 4 + (q * JQ + u - 1))
                    s = u % 2
                    at = i * (4 * GROUP) + u * GROUP
                    tokens = slice(at, at + GROUP) if isinstance(i, int) else bass.ds(at, GROUP)
                    keys = iota_b[:, q * JQ:(q + 1) * JQ]
                    V.tensor_tensor(one_j[:, s], under(keys, GROUP), over(i2T[:, tokens], JQ),
                                    ALU.is_equal).then_inc(onehot_step, 1)
                    V.tensor_tensor(one_i[:, s], under(iota_b[:], GROUP), over(i1T[:, tokens], NK),
                                    ALU.is_equal).then_inc(onehot_step, 1)
                    dve.wait_ge(onehot_step, i * 8 + 2 * (q * JQ + u + 1))
                    V.tensor_tensor(gate_j[:, s], one_j[:, s].unsqueeze(2).broadcast_to([P, GROUP, PIECES, JQ]),
                                    g_part[:, :, tokens].rearrange("p m t -> p t m").unsqueeze(3).broadcast_to(
                                        [P, GROUP, PIECES, JQ]), ALU.mult).then_inc(onehot_ready, 1)

                for u in range(4):
                    onehots(0, 0, u, u >= 2)
                with dve.Fori(1, JQ // 4) as i:
                    for u in range(4):
                        onehots(0, i, u, True)
                for q in range(QUARTERS):
                    base = N2_PRE + 2 * q * JQ
                    more = q + 1 < QUARTERS

                    def one(i, u, free):
                        if more:
                            onehots(q + 1, i, u, True)
                        j = i * 4 + u
                        gated(i, 4, u, q * JQ, base, 1, gates[:, q % 2, :, j], free)

                    dve.wait_ge(gates_out, (q + 1) * JQ)
                    if q:
                        dve.wait_ge(w_used, base)
                    for u in range(4):
                        one(0, u, u >= 2)
                    with dve.Fori(1, JQ // 4) as i:
                        for u in range(4):
                            one(i, u, True)
                dve.wait_ge(out_full, LAST_SUMS)
                layer_norm(step, 5, ypre, par("ln2_g"), par("ln2_b"), bn3, mv3, std3, rstd3, None)
                return step.n

            dve.wait_ge(const_ready, CONSTS)
            setup()
            for n, layer in ((1, block1), (1 + DEPTH, block2)):
                with dve.Fori(0, DEPTH) as l:
                    enter_layer(dve, "dve", l + n)
                    n_steps = layer()
                    leave_layer(dve, "dve", dve_step, n_steps)


def _feature_chunk(w, c):
    return w[:, c:c + P].reshape(DT, P, P).transpose(1, 0, 2).reshape(P, CH)


def _token_chunks(w, c):
    x = w[:, c:c + 512].reshape(DT // 2, 2, P, 512).transpose(0, 2, 1, 3)
    return [x[i].reshape(P, CH) for i in range(DT // 2)]


def _woven(ups, downs):
    out = list(ups[0])
    for j in range(len(downs)):
        if j + 1 < len(ups):
            out += ups[j + 1]
        out.append(downs[j])
    return out


def _stream1(w_in, w_out, w_gate, w_up, w_down):
    out = [_feature_chunk(w_in, c) for c in range(0, 1024, P)]
    for c in (2048, 2560, 1024, 3072, 1536):
        out += _token_chunks(w_in, c)
    for c in (0, 512):
        out += _token_chunks(w_out, c)
    out += _woven([[_feature_chunk(w_gate, f), _feature_chunk(w_up, f)] for f in range(0, D_FF, P)],
                  [w_down[f:f + P] for f in range(0, D_FF, P)])
    return out


def _stream2(w_in, w_out, w_q, u, v, out):
    at = dict(scb=0, scc=256, sch=512, cq=768, cfa=1184, cfg=1440, swq=1696, swk=1952, swv=2080)
    q = w_in[:, at["swq"]:at["swk"]].reshape(D, AH, 64)[:, [0, 2, 1, 3]].reshape(D, 256)
    cols = [w_in[:, at[k] + c:at[k] + c + P] for k in ("cfa", "cfg", "scc", "sch", "scb") for c in (0, P)]
    cols += [q[:, 0:P], q[:, P:], w_in[:, at["swk"]:at["swv"]]]
    parts = [_feature_chunk(x, 0) for x in cols]
    m = np.concatenate([w_in[:, at["cq"]:at["cq"] + 384], w_in[:, at["swv"]:at["swv"] + P]], axis=1)
    parts += _token_chunks(m, 0)
    kr = np.zeros((P, CH), w_in.dtype)
    kr[:, 0:DT * 32] = w_in[:, 1152:1184].reshape(DT, P, 32).transpose(1, 0, 2).reshape(P, -1)
    parts.append(kr)
    for c in (0, 512):
        parts += _token_chunks(w_out, c)
    parts += [_feature_chunk(w_q, c) for c in range(0, 2 * PH * P, P)]
    for i, x in enumerate(parts):
        out[i] = x
    ut = u.reshape(NK, NK, DT, P).transpose(1, 3, 2, 0)
    vt = v.reshape(NK, NK, D).transpose(1, 0, 2)
    for quarter in range(QUARTERS):
        a = N2_PRE + 2 * quarter * JQ
        j = quarter * JQ
        out[a] = ut[j].reshape(P, CH)
        out[a + 1:a + 2 * JQ - 1:2] = ut[j + 1:j + JQ].reshape(JQ - 1, P, CH)
        out[a + 2:a + 2 * JQ - 1:2] = vt[j:j + JQ - 1]
        out[a + 2 * JQ - 1] = vt[j + JQ - 1]


def _cols(x):
    return x.reshape(-1, P).T


def kernel(**inputs):
    import concourse.bacc as bacc
    from concourse.bass_utils import run_bass_kernel_spmd

    a = {k: np.asarray(v) for k, v in inputs.items()}
    L = range(DEPTH)
    f = np.float32
    s1 = np.stack([np.stack(_stream1(a["w_in"][l], a["w_out"][l], a["w_gate"][l], a["w_up"][l], a["w_down"][l]))
                   for l in L])
    s2 = np.empty((DEPTH, N2, P, CH), a["w_in_2"].dtype)
    for l in L:
        _stream2(a["w_in_2"][l], a["w_out_2"][l], a["peer_w_q_2"][l], a["peer_u_2"][l], a["peer_v_2"][l], s2[l])
    lam_init = [0.8 - 0.6 * float(np.exp(-0.3 * l)) for l in L]
    col1 = np.stack([np.concatenate([_cols(a["attn_norm_g"][l]), _cols(a["ffn_norm_g"][l])], 1) for l in L])
    row1 = np.stack([np.concatenate([
        a["ret_norm_g"][l], a["dq_norm_g"][l], a["dk_norm_g"][l], a["diff_norm_g"][l],
        a["lambda_q1"][l], a["lambda_q2"][l], a["lambda_k1"][l], a["lambda_k2"][l],
        a["ret_decay_fwd"][l], a["ret_decay_bwd"][l], np.array([lam_init[l], 1.0 - lam_init[l]], f)]) for l in L])
    row2 = np.stack([np.concatenate([
        a["ln1_g_2"][l], a["ln1_b_2"][l], a["ln2_g_2"][l], a["ln2_b_2"][l],
        a["cf_ln_g_2"][l], a["cf_ln_b_2"][l], a["swa_sinks_2"][l]]) for l in L])

    def taps(w):
        return w.reshape(w.shape[0], 2, P).transpose(2, 1, 0).reshape(P, -1)

    col2 = np.stack([np.concatenate([
        taps(a["sc_conv_w_2"][l]), taps(a["cf_dw_w_2"][l]), _cols(a["cf_dw_b_2"][l]), _cols(a["mla_q_norm_2"][l]),
        _cols(a["mla_kv_norm_2"][l]), _cols(a["mix_norm_g_2"][l])], 1) for l in L])
    small2 = np.stack([np.concatenate([
        a["mla_w_uq_2"][l].reshape(2, P, AH * QK).transpose(1, 0, 2).reshape(P, -1),
        a["mla_w_uk_2"][l], a["mla_w_uv_2"][l]], 1) for l in L])
    sub2 = a["peer_sub_keys_2"].reshape(DEPTH, 2 * PH, NK, P).transpose(0, 3, 1, 2)
    inv = (10000.0 ** (-np.arange(16, dtype=f) / f(16))).astype(f)
    arrays = dict(in_x=a["x"][0], in_pos=a["positions_2"][0], in_s1=s1, in_col1=col1, in_row1=row1, in_s2=s2, in_col2=col2,
                  in_row2=row2, in_small2=small2, in_sub2=sub2, in_inv=inv)
    arrays = {k: np.ascontiguousarray(v) for k, v in arrays.items()}
    nc = bacc.Bacc("TRN2", target_bir_lowering=False, num_devices=1)
    args = [nc.dram_tensor(k, v.shape, mybir.dt.from_np(v.dtype), kind="ExternalInput").ap() for k, v in arrays.items()]
    out = nc.dram_tensor("out_x", (SEQ, D), F32, kind="ExternalOutput").ap()
    two_blocks_kernel(nc, *args, out)
    r = run_bass_kernel_spmd(nc, [arrays], core_ids=[0])
    return r.results[0]["out_x"].reshape(1, SEQ, D)
```

```python
from contextlib import ExitStack

import numpy as np

import concourse.bass as bass
from concourse import mybir

F32 = mybir.dt.float32
F32R = mybir.dt.float32r
BF16 = mybir.dt.bfloat16
U32 = mybir.dt.uint32
I32 = mybir.dt.int32
ALU = mybir.AluOpType
ACT = mybir.ActivationFunctionType
AX_X = mybir.AxisListType.X

P = 128
DEPTH = 2
SEQ = 256
D = 1024
TT = SEQ // P
DT = D // P
CH = 1024
D_FF = 2816
FF_BLOCKS = D_FF // P
EPS1 = 1e-6
EPS2 = 1e-5
ALPHA = (2 * DEPTH) ** 0.25
NEG = -1e30
REPLACED = -3.0e38
PI = 3.14159250

RH = 8
DH = 4
AH = 4
QK = 96
SC_K = 3
CF_K = 31
CF_SPLIT = 21
PH = 8
NK = 128
TOP = 16
QUARTERS = 4
JQ = NK // QUARTERS
GROUP = SEQ // JQ
PIECES = 3

N1_MIX = 8 + 5 * 4
N1 = N1_MIX + 8 + 3 * FF_BLOCKS
N2_MIX = 13 + 4 + 1
N2_PRE = N2_MIX + 8 + 16
STASH = 48
N2_OUT = N2_PRE + STASH
RUNS = ((0, JQ), (JQ, STASH - JQ), (STASH, 2 * JQ - STASH), (2 * JQ, JQ), (3 * JQ, JQ))
N2 = N2_PRE + 2 * NK
RAW1, PAIR1 = 3, 6
RAW2, PAIR2 = 4, 4
EARLY = 3
AHEAD = 2
ROT = 4

ROW1 = dict(ret_g=64, dq_g=64, dk_g=64, diff_g=128, lq=128, lk=128, dec=16, lam_init=1, out_scale=1)
ROW2 = dict(ln1_g=D, ln1_b=D, ln2_g=D, ln2_b=D, cf_g=256, cf_b=256, sinks=AH)
COL2 = dict(sc_w=2 * SC_K, cf_w=2 * CF_K, cf_bias=2, mq_g=2, mkv_g=1, mix_g=DT)
SMALL2 = dict(uq=2 * AH * QK, ukv=512)


def run_base(first):
    return N2_OUT + first if first < STASH else N2_PRE + 2 * first


def spans(fields):
    out, at = {}, 0
    for k, n in fields.items():
        out[k] = (at, at + n)
        at += n
    return out, at


class Banks:

    def __init__(self, plan):
        self.plan = [(name, who) for name, who, _ in plan]
        self.index = {name: i for i, (name, _, _) in enumerate(plan)}
        self.nth = {}
        self.chunks = {}
        count, chunks = {}, 0
        for name, who, n in plan:
            count[who] = count.get(who, 0) + 1
            chunks += n
            self.nth[name] = (who, count[who])
            self.chunks[name] = chunks


def plan1():
    p = [(f"xT{i}", "dve", 0) for i in range(4)]
    p += [(f"qk{i}", "act", 2) for i in range(4)]
    p += [(f"{g}{t}", who, 4 * (t == 0)) for g, who in (("dq", "dve"), ("dk", "dve"), ("rv", "act"), ("dv", "act"),
                                                        ("rg", "act")) for t in range(TT)]
    p += [(f"S{h}", "dve", 0) for h in range(RH)]
    p += [(f"dT{h}", "act", 0) for h in range(DH)]
    p += [(f"sc{k}", "dve", 0) for k in range(2 * DH)]
    p += [(f"aT{h}", "act", 0) for h in range(DH)]
    p += [(f"mT{i}", "dve", 0) for i in range(4)]
    p += [(f"fT{i}", "dve", 8 * (i == 0)) for i in range(4)]
    return Banks(p)


def plan2():
    p = [(f"xT{i}", "dve", 0) for i in range(4)]
    p += [(n, "dve" if n == "sch" else "act", 1 if n == "swk" else 2)
          for n in ("cfa", "cfg", "scc", "sch", "scb", "swq", "swk")]
    p += [("m0", "act", 4), ("m1", "act", 0), ("kr", "act", 1)] + [(f"ws{h}", "dve", 0) for h in range(AH)]
    p += [("cqT", "dve", 0), ("ckvT", "dve", 0)] + [(n, "act", 0) for n in ("uq0", "uq1", "kv0", "kv1")]
    p += [(f"wT{h}", "act", 0) for h in range(AH)]
    p += [("scT", "act", 0), ("cvT", "act", 0)]
    p += [(f"kT{h}", "act", 0) for h in range(AH)]
    p += [(f"ms{h}", "dve", 0) for h in range(AH)]
    p += [(f"pT{h}", "act", 0) for h in range(AH)]
    p += [(f"mT{i}", "dve", 0) for i in range(4)]
    p += [(f"hT{i}", "dve", 8 * (i == 0)) for i in range(4)]
    p += [("q0", "act", 2)]
    for h in range(PH):
        p += ([(f"q{h + 1}", "act", 2)] if h + 1 < PH else []) + [(f"rs{h}", "act", 0)]
    p += [("iT", "act", 0), ("gT", "act", 0)]
    return Banks(p)


def two_blocks_kernel(nc, x_in, pos_in, stream, col1, row1, col2, row2, small2, sub2, inv_in, out):
    r1, NR1 = spans(ROW1)
    r2, NR2 = spans(ROW2)
    c2, NC2 = spans(COL2)
    m2, NM2 = spans(SMALL2)
    with ExitStack() as ctx:
        def sb(name, shape, dt=F32):
            return ctx.enter_context(nc.sbuf_tensor(name, shape, dt))

        def sem(name):
            return ctx.enter_context(nc.semaphore(name))

        x_res = sb("x_res", [P, TT, D])
        hT_hi = sb("hT_hi", [P, DT, SEQ], F32R)
        hT_lo = sb("hT_lo", [P, DT, SEQ], F32R)
        raw = sb("raw", [P, max(RAW1, RAW2), CH])
        RING = max(PAIR1, PAIR2)
        w_split = sb("w_split", [P, 2 * RING, CH], F32R)
        w_hi = [w_split[:, k, :] for k in range(RING)]
        w_lo = [w_split[:, 2 * RING - 1 - k, :] for k in range(RING)]
        ident = sb("ident", [P, P])
        iota_k = sb("iota_k", [P, NK])
        iota_b = sb("iota_b", [P, NK, 2], BF16)
        rel = sb("rel", [P, 3 * P])
        after = sb("after", [P, 3 * P])
        before = sb("before", [P, 3 * P])
        absd = sb("absd", [P, 3 * P])
        causal = sb("causal", [P, 3 * P])
        window = sb("window", [P, AH, 3 * P])
        alibi = window
        cos_t = sb("cos_t", [P, TT, 16])
        sin_t = sb("sin_t", [P, TT, 16])
        trig = sb("trig", [P, 164])
        invf, pos_f, pos_i, angle = trig[:, 0:16], trig[:, 16:18], trig[:, 18:20].bitcast(I32), trig[:, 20:36]
        turns = trig[:, 36:100].rearrange("p (b t f) -> p b t f", b=2, t=TT)
        turn_n = trig[:, 100:164].rearrange("p (b t f) -> p b t f", b=2, t=TT)
        eps1 = sb("eps1", [P, 1])
        eps2 = sb("eps2", [P, 1])
        col1_sb = sb("col1_sb", [P, 2 * DT])
        row2_sb = sb("row2_sb", [P, NR2])
        row1_sb = row2_sb[:, 0:NR1]
        col2_sb = sb("col2_sb", [P, NC2])
        i1T = sb("i1T", [P, SEQ], BF16)
        i2T = sb("i2T", [P, SEQ], BF16)
        hidw_hi = sb("hidw_hi", [P, 2, SEQ], F32R)
        hidw_lo = sb("hidw_lo", [P, 2, SEQ], F32R)
        one_i = sb("one_i", [P, 2, GROUP // 2, NK, 2], BF16)
        one_j = sb("one_j", [P, 2, GROUP // 2, JQ, 2], BF16)
        gate_j = sb("gate_j", [P, 2, GROUP // 2, PIECES, JQ, 2], BF16)
        ARENA = 18400
        arena = sb("arena", [P, ARENA])
        used = [0]

        def carve(*shape):
            n = int(np.prod(shape))
            a = arena[:, used[0]:used[0] + n]
            used[0] += n
            assert used[0] <= ARENA, used[0]
            if len(shape) == 1:
                return a
            names = "abcd"[:len(shape)]
            return a.rearrange(f"p ({' '.join(names)}) -> p {' '.join(names)}", **dict(zip(names[1:], shape[1:])))

        used[0] = ARENA - 2 * 512 - 256 - 384
        hid = carve(2, SEQ)
        gated_hid = carve(2, SEQ)
        gT = carve(SEQ)
        g_part = carve(PIECES * SEQ // 2).bitcast(BF16).rearrange("p (m t) -> p m t", m=PIECES)
        used[0] = 0

        xn = carve(TT, D)
        rqkT = carve(8, SEQ)
        ret = rqkT[:, 0:4, :].rearrange("p k t -> p (k t)").rearrange("p (t c) -> p t c", t=TT)
        rv = carve(TT, 512)
        rgate = carve(TT, 512)
        dqk = carve(TT, 2, 512)
        dv = carve(TT, 512)
        decay_flat = carve(RH * 3 * P)
        decay = decay_flat.rearrange("p (h c) -> p h c", h=RH)
        dqkT = decay_flat[:, 0:DH * 2 * SEQ].rearrange("p (h k t) -> p h k t", h=DH, k=2)
        ret_sq = decay_flat[:, DH * 2 * SEQ:DH * 2 * SEQ + TT * 512].rearrange("p (t c) -> p t c", t=TT)
        scm = carve(2, TT, SEQ)
        attnT = scm
        prob = carve(4, 2, SEQ)
        sq = prob[:, 0:2].rearrange("p k m c -> p k (m c)")
        attn = carve(4, SEQ)
        mix = xn
        st1 = carve(456)
        ss_x, std_x, rstd_x = st1[:, 0:2], st1[:, 2:4], st1[:, 4:6]
        ss_r, std_r, rstd_r = (st1[:, 256 + 16 * k:272 + 16 * k].rearrange("p (t g) -> p t g", t=TT) for k in range(3))
        ss_d, std_d, rstd_d = (st1[:, 304 + 8 * k:312 + 8 * k].rearrange("p (t g) -> p t g", t=TT) for k in range(3))
        gd = st1[:, 328:456]
        ss_g = st1[:, 8:40].rearrange("p (t b g) -> p t b g", t=TT, b=2)
        std_g = st1[:, 40:72].rearrange("p (t b g) -> p t b g", t=TT, b=2)
        rstd_g = st1[:, 72:104].rearrange("p (t b g) -> p t b g", t=TT, b=2)
        negmax = st1[:, 104:120].rearrange("p (k m) -> p k m", m=2)
        sums = st1[:, 120:136].rearrange("p (k m) -> p k m", m=2)
        rsum = st1[:, 136:152].rearrange("p (k m) -> p k m", m=2)
        rowmax = st1[:, 152:168].rearrange("p (k m) -> p k m", m=2)
        dece = st1[:, 168:184]
        lam_s, lam_e, lam = st1[:, 184:186], st1[:, 186:188], st1[:, 188:189]
        lam_d = st1[:, 189:190]
        gq = st1[:, 192:256]
        used1, used[0] = used[0], 0

        HALF = SEQ * JQ
        st2 = carve(328)
        routing_from = used[0]
        mix2 = carve(TT, D)
        hpre = mix2
        small_sb = carve(NM2)
        cfa = carve(2, SEQ)
        cvt = cfa.rearrange("p k t -> p (k t)").rearrange("p (t c) -> p t c", t=TT)
        cfg_cv = carve(4, SEQ)
        cfg = cfg_cv[:, 0:2]
        cqT = cfg
        cv = cfg_cv[:, 2:4]
        sq3 = cfg_cv.rearrange("p k t -> p (k t)")
        scc = carve(2, SEQ)
        ckvT = scc[:, 0, :]
        scy = carve(2, SEQ)
        krt = carve(TT, 32)
        vtok = carve(TT, AH, 64)
        rt = carve(4, AH, 16)
        qtok = carve(TT, AH, QK)
        assert used[0] <= HALF
        used[0] = HALF
        sub_sb = carve(2 * PH, NK)
        queries_from = used[0]
        early = carve(AH * 2 * SEQ)
        cfu = early[:, 0:572].rearrange("p (k t) -> p k t", k=2)
        scu = early[:, 572:1088].rearrange("p (k t) -> p k t", k=2)
        scb = early[:, 1088:1600].rearrange("p (k t) -> p k t", k=2)
        qkT = early[:, 0:AH * 2 * SEQ].rearrange("p (h k t) -> p h k t", h=AH, k=2)
        swqk = carve(3, SEQ)
        mtok = carve(TT, 512)
        kcat = carve(TT, AH, QK)
        prob2 = carve(4, TT, SEQ)
        sq2 = prob2[:, 0:2].rearrange("p k t c -> p (k t c)")
        probT = carve(2, TT, SEQ)
        used[0] = queries_from
        pqT = carve(2, 2, SEQ)
        used[0] = routing_from
        rs_flat = carve(PH * TT * 2 * NK)
        rs = rs_flat.rearrange("p (h t k n) -> p h t k n", h=PH, t=TT, k=2)
        eq = rs_flat[:, 0:PH * TOP * TOP].rearrange("p (h a b) -> p h a b", h=PH, a=TOP)
        rs2 = carve(TT, 2, NK)
        cand = carve(TT, TOP * TOP)
        cand2 = carve(TT, TOP * TOP)
        pairs_of = lambda x: x.rearrange("p t c -> p (t c)").rearrange("p (k h t c) -> p k h t c", k=2, h=PH, t=TT)
        bestab = pairs_of(cand).bitcast(U32)
        bestf = pairs_of(cand2)
        topv = carve(PH, TT, 2, TOP)
        topf = carve(PH, TT, 2, TOP)
        best = carve(PH, TT, TOP)
        topi = carve(PH, TT, 2, TOP).bitcast(U32)
        besti = carve(PH, TT, TOP).bitcast(U32)
        gsum = carve(2, PH)
        assert used[0] <= HALF
        used[0] = 2 * HALF
        chosen = carve(3, TT, PH * TOP)
        assert used[0] <= ARENA - 512 - 256 - 384
        used[0] = 0
        gates = carve(2, SEQ, JQ)
        stash = [gates[:, 1].rearrange("p t j -> p (t j)").rearrange("p (b t) -> p b t", t=SEQ),
                 w_split[:, PAIR2:2 * RING - PAIR2, :].rearrange("p k c -> p (k c)").bitcast(F32).rearrange(
                     "p (b t) -> p b t", t=SEQ)]
        a_c2 = st2
        ss_m, std_m, rstd_m = a_c2[:, 0:4], a_c2[:, 4:8], a_c2[:, 8:12]
        bn = a_c2[:, 12:36].rearrange("p (t c s) -> p t c s", t=TT, c=2)
        mv = a_c2[:, 36:40].rearrange("p (t s) -> p t s", t=TT)
        std_l, rstd_l = a_c2[:, 40:42], a_c2[:, 42:44]
        negmax2 = a_c2[:, 44:60].rearrange("p (k m) -> p k m", m=2)
        sums2 = a_c2[:, 60:76].rearrange("p (k m) -> p k m", m=2)
        rsum2 = a_c2[:, 76:92].rearrange("p (k m) -> p k m", m=2)
        rowmax2 = a_c2[:, 92:108].rearrange("p (k m) -> p k m", m=2)
        esink = a_c2[:, 108:116].rearrange("p (k m) -> p k m", m=2)
        ss_x2 = a_c2[:, 120:152].rearrange("p (t g) -> p t g", t=TT)
        std_x2 = a_c2[:, 152:184].rearrange("p (t g) -> p t g", t=TT)
        rstd_x2 = a_c2[:, 184:216].rearrange("p (t g) -> p t g", t=TT)
        nsink = a_c2[:, 320:324]
        ypre = gates.rearrange("p q a b -> p (q a b)")[:, 0:TT * D].rearrange("p (t d) -> p t d", t=TT)
        st3 = sb("st3", [P, 64])
        bn3 = st3[:, 0:24].rearrange("p (t c s) -> p t c s", t=TT, c=2)
        mv3 = st3[:, 24:28].rearrange("p (t s) -> p t s", t=TT)
        std3, rstd3 = st3[:, 28:30], st3[:, 30:32]

        ps = ctx.enter_context(nc.psum_tensor("ps", [P, 8, 512], F32))
        FF_BANK, PEER_BANK = 6, 4
        acc = [ps[:, i, :] for i in range(4)]

        const_ready = sem("const_ready")
        x_loaded = sem("x_loaded")
        setup_in = sem("setup_in")
        rel_ready = sem("rel_ready")
        mask_ready = sem("mask_ready")
        dist_step = sem("dist_step")
        opened = sem("opened")
        out_done = sem("out_done")
        arrived = {n: sem(f"{n}_arrived") for n in ("pe", "act", "dve", "pool")}
        w_ready = [sem(f"w_ready{i}") for i in range(max(RAW1, RAW2))]
        first = sem("layer_first")
        entered = {n: sem(f"{n}_entered") for n in ("pe", "act", "dve", "pool")}
        par_ready = sem("par_ready")
        late_ready = sem("late_ready")
        hi_ready = sem("hi_ready")
        lo_ready = sem("lo_ready")
        w_used = sem("w_used")
        xhi_ready = sem("xhi_ready")
        gate_step = sem("gate_step")
        onehot_step = sem("onehot_step")
        bank_full = sem("bank_full")
        emptied = dict(act=sem("act_emptied"), dve=sem("dve_emptied"))
        turn_ready = sem("turn_ready")
        dve_step = sem("dve_step")
        act_step = sem("act_step")
        ms_ready = sem("ms_ready")
        std_ready = sem("std_ready")
        rows_ready = sem("rows_ready")
        dec_ready = sem("dec_ready")
        dist_ready = sem("dist_ready")
        decay_ready = sem("decay_ready")
        lam_ready = sem("lam_ready")
        lame_ready = sem("lame_ready")
        out_full = sem("out_full")
        ret_copied = sem("ret_copied")
        pool_step = sem("pool_step")
        retsq_ready = sem("retsq_ready")
        rstd_ready = sem("rstd_ready")
        mixnorm_ready = sem("mixnorm_ready")
        retmix_ready = sem("retmix_ready")
        dqk_ready = sem("dqk_ready")
        negmax_ready = sem("negmax_ready")
        exp_ready = sem("exp_ready")
        attn_ready = sem("attn_ready")
        hid_full = sem("hid_full")
        hid_ready = sem("hid_ready")
        hidw_ready = sem("hidw_ready")
        conv_ready = sem("conv_ready")
        cfg_ready = sem("cfg_ready")
        cfmix_ready = sem("cfmix_ready")
        rope_ready = sem("rope_ready")
        cn_ready = sem("cn_ready")
        score_ready = sem("score_ready")
        gexp_ready = sem("gexp_ready")
        chosen_ready = sem("chosen_ready")
        onehot_ready = sem("onehot_ready")
        onehot_used = sem("onehot_used")
        gates_out = sem("gates_out")
        last = sem("layer_last")
        banks1, banks2 = plan1(), plan2()
        assert [4 + banks1.index[f"fT{i}"] % ROT for i in range(2)] == [FF_BANK, FF_BANK + 1]

        def bank(banks, name):
            return ps[:, 4 + banks.index[name] % ROT, :]

        def open_bank(pe, banks, name):
            i = banks.index[name]
            if i >= ROT:
                who, n = banks.nth[banks.plan[i - ROT][0]]
                pe.wait_ge(emptied[who], n)
            return bank(banks, name)

        def take_bank(eng, banks, name):
            eng.wait_ge(bank_full, banks.index[name] + 1)
            return bank(banks, name)

        def after_emptied(eng, banks, name):
            who, n = banks.nth[name]
            eng.wait_ge(emptied[who], n)

        class Steps:

            def __init__(self, eng, s):
                self.eng, self.s, self.n = eng, s, 0

            def __call__(self, ins):
                ins.then_inc(self.s, 1)
                self.n += 1

            def settle(self):
                self.eng.wait_ge(self.s, self.n)

        def enter_layer(eng, name, n):
            eng.wait_ge(opened, n)
            eng.sem_inc(entered[name], 1)

        def leave_layer(eng, name, s, n):
            eng.wait_ge(s, n)
            eng.sem_inc(arrived[name], 1)

        block = ctx.enter_context(nc.Block())

        @block.sync
        def _(sp):
            def load(c, slot):
                sp.dma_start(raw[:, slot, :], stream[c]).then_inc(w_ready[slot], 16)

            def load_layer(base, n, slots, params, late):
                def parameters():
                    for dst, src in params:
                        sp.dma_start(dst, src).then_inc(par_ready, 16)

                head = slots + n % slots
                if not late:
                    parameters()
                for c in range(EARLY, head):
                    if c >= slots:
                        sp.wait_ge(lo_ready, c - slots + 1)
                    load(base + c, c % slots)
                    if late and c == slots - 1:
                        parameters()
                for dst, src in late:
                    sp.dma_start(dst, src).then_inc(late_ready, 16)
                with sp.Fori(0, (n - head) // slots) as i:
                    for k in range(slots):
                        sp.wait_ge(lo_ready, i * slots + (head + k - slots + 1))
                        load(base + i * slots + (head + k), (head + k) % slots)

            def load_early(base):
                for c in range(EARLY):
                    load(base + c, c)

            def turn(n, chunks, following):
                sp.wait_ge(hi_ready, chunks)
                sp.wait_ge(lo_ready, chunks)
                sp.sem_inc(first, 1)
                sp.wait_ge(first, 1)
                sp.sem_clear(range(w_ready[0].num, w_ready[-1].num + 1))
                if following is not None:
                    load_early(following)
                for s in arrived.values():
                    sp.wait_ge(s, n)
                sp.sem_inc(first, 1)
                sp.wait_ge(first, 2)
                sp.sem_clear(range(first.num, last.num + 1))
                sp.sem_inc(opened, 1)

            sp.dma_start(x_res[:], x_in.rearrange("(t p) d -> p t d", p=P)).then_inc(x_loaded, 16)
            load_early(0)
            with nc.allow_non_contiguous_dma(reason="256 positions"):
                sp.dma_start(pos_i, pos_in.rearrange("(t p) -> p t", p=P)).then_inc(setup_in, 16)
            sp.dma_start(invf, inv_in.partition_broadcast(P)).then_inc(setup_in, 16)
            sp.wait_ge(x_loaded, 16)
            sp.sem_inc(opened, 1)
            with sp.Fori(0, DEPTH) as l:
                load_layer(l * N1, N1, RAW1, ((col1_sb[:], col1[l]), (row1_sb, row1[l].partition_broadcast(P))), ())
                turn(l + 1, N1, l * N1 + N1)

            def layer2(l, following):
                load_layer(l * N2 + DEPTH * N1, N2, RAW2, ((col2_sb[:], col2[l]), (row2_sb[:], row2[l].partition_broadcast(P))),
                           ((small_sb, small2[l]), (sub_sb, sub2[l])))
                turn(l + (1 + DEPTH), N2, following)

            with sp.Fori(0, DEPTH - 1) as l:
                layer2(l, l * N2 + (DEPTH * N1 + N2))
            layer2(DEPTH - 1, None)
            sp.dma_start(out.rearrange("(t p) d -> p t d", p=P), x_res[:]).then_inc(out_done, 16)
            sp.wait_ge(out_done, 16)

        @block.gpsimd
        def _(pool):
            pool.memset(ident[:], 0.0).then_inc(const_ready, 1)
            pool.iota(rel[:], pattern=[[1, 3 * P]], base=-P, channel_multiplier=-1,
                      allow_small_or_imprecise_dtypes=True).then_inc(rel_ready, 1)
            pool.wait_ge(const_ready, 1)
            pool.affine_select(out=ident[:], in_=ident[:], compare_op=ALU.not_equal, fill=1.0, base=0,
                               pattern=[[-1, P]], channel_multiplier=1).then_inc(const_ready, 1)
            pool.memset(eps1[:], EPS1).then_inc(const_ready, 1)
            pool.memset(eps2[:], EPS2).then_inc(const_ready, 1)

            def second_constants():
                pool.iota(iota_k[:], pattern=[[1, NK]], base=0, channel_multiplier=0,
                          allow_small_or_imprecise_dtypes=True).then_inc(mask_ready, 1)
                pool.iota(iota_b[:], pattern=[[1, NK], [0, 2]], base=0, channel_multiplier=0,
                          allow_small_or_imprecise_dtypes=True).then_inc(mask_ready, 1)
                pool.memset(causal[:], 0.0).then_inc(mask_ready, 1)
                pool.wait_ge(rel_ready, 1)
                for h in range(AH):
                    pool.tensor_scalar(window[:, h], rel[:], 2.0 ** (-2.0 * (h + 1)) * 64 ** 0.5, 0.0, ALU.mult,
                                       ALU.add).then_inc(mask_ready, 1)
                pool.wait_ge(mask_ready, 3 + AH)
                pool.affine_select(out=causal[:], in_=causal[:], compare_op=ALU.is_ge, fill=NEG, base=P,
                                   pattern=[[-1, 3 * P]], channel_multiplier=1).then_inc(mask_ready, 1)
                for h in range(AH):
                    pool.affine_select(out=window[:, h], in_=window[:, h], compare_op=ALU.is_ge, fill=NEG, base=P,
                                       pattern=[[-1, 3 * P]], channel_multiplier=1).then_inc(mask_ready, 1)
                pool.wait_ge(mask_ready, 4 + 2 * AH)
                for h in range(AH):
                    pool.affine_select(out=window[:, h], in_=window[:, h], compare_op=ALU.is_gt, fill=NEG, base=0,
                                       pattern=[[1, 3 * P]], channel_multiplier=-1).then_inc(mask_ready, 1)

            def split_layer(n, raws, pairs, pause, between):
                def one(c, at):
                    pool.wait_ge(hi_ready, c + 1)
                    if at >= pairs:
                        pool.wait_ge(w_used, c - pairs + 1)
                    pool.tensor_tensor(w_lo[at % pairs], raw[:, at % raws, :], w_hi[at % pairs].bitcast(F32),
                                       ALU.subtract).then_inc(lo_ready, 1)

                turn = max(raws, pairs)
                head = max(turn, pause)
                head += (n - head) % turn
                for c in range(head):
                    if between is not None and c == pause:
                        between()
                    one(c, c)
                if between is not None and pause == head:
                    between()
                with pool.Fori(0, (n - head) // turn) as i:
                    for k in range(turn):
                        one(i * turn + (head + k), head + k)

            def retention_norm():
                step = Steps(pool, pool_step)
                T = pool.tensor_tensor
                after_emptied(pool, banks1, "rg1")
                pool.wait_ge(par_ready, 32)
                g = row1_sb[:, slice(*r1["ret_g"])].unsqueeze(1).broadcast_to([P, RH, 64])
                for t in range(TT):
                    x = rgate[:, t, :].rearrange("p (h c) -> p h c", h=RH)
                    step(T(x, x, g, ALU.mult))
                pool.wait_ge(ret_copied, TT)
                for t in range(TT):
                    T(ret_sq[:, t, :], ret[:, t, :], ret[:, t, :], ALU.mult).then_inc(retsq_ready, 1)
                pool.wait_ge(rstd_ready, 1)
                for t in range(TT):
                    x = ret[:, t, :].rearrange("p (h c) -> p h c", h=RH)
                    step(T(x, x, rstd_r[:, t, :].unsqueeze(2).broadcast_to([P, RH, 64]), ALU.mult))
                step.settle()
                for t in range(TT):
                    T(mix[:, t, 0:512], ret[:, t, :], rgate[:, t, :], ALU.mult).then_inc(retmix_ready, 1)

            def mix_norm():
                pool.wait_ge(rstd_ready, 1)
                for t in range(TT):
                    for a, z in ((0, 4), (8, 16)):
                        x = mix2[:, t, a * 64:z * 64].rearrange("p (g c) -> p g c", c=64)
                        pool.tensor_tensor(x, x, rstd_x2[:, t, a:z].unsqueeze(2).broadcast_to([P, z - a, 64]),
                                           ALU.mult).then_inc(mixnorm_ready, 1)

            with pool.Fori(0, DEPTH) as l:
                enter_layer(pool, "pool", l + 1)
                split_layer(N1, RAW1, PAIR1, N1_MIX + AHEAD, retention_norm)
                leave_layer(pool, "pool", lo_ready, N1)
            second_constants()
            with pool.Fori(0, DEPTH) as l:
                enter_layer(pool, "pool", l + (1 + DEPTH))
                split_layer(N2, RAW2, PAIR2, N2_MIX + AHEAD, mix_norm)
                leave_layer(pool, "pool", lo_ready, N2)

        CONSTS = 4
        MASKS = 4 + 3 * AH
        LAST_SUMS = 2 + 2 * TT + TT

        @block.tensor
        def _(pe):
            class Stream:

                def __init__(self, slots):
                    self.slots, self.c, self.owed, self.fresh = slots, 0, 0, None

                def rows(self, d):
                    if self.fresh is not None and d % 2 == 0:
                        banks, name = self.fresh
                        after_emptied(pe, banks, f"{name}{d // 2}")
                        if d == DT - 2:
                            self.fresh = None

                def take(self):
                    pe.wait_ge(lo_ready, self.c + 1)
                    slot = self.c % self.slots
                    self.c += 1
                    return w_hi[slot], w_lo[slot]

                def mm(self, o, lhsT, rhs, start, stop, signal=None):
                    ins = nc.tensor.matmul(o, lhsT, rhs, start=start, stop=stop)
                    if signal is not None:
                        ins.then_inc(signal, 1)
                    elif self.owed:
                        ins.then_inc(w_used, self.owed)
                        self.owed = 0
                    return ins

                def mm3(self, o, a, b, start, stop, signal=None):
                    self.mm(o, a[0], b[0], start, False)
                    self.mm(o, a[0], b[1], False, False)
                    return self.mm(o, a[1], b[0], False, stop, signal)

            def part(pair, *at):
                return tuple(x[at] for x in pair)

            hT = (hT_hi, hT_lo)
            ALL = slice(None)

            def transpose_rows(w, banks, name, src, rows, also=None):
                bs = [open_bank(pe, banks, f"{name}{i}") for i in range(4)]
                for t in range(TT):
                    if rows is not None:
                        pe.wait_ge(rows_ready, rows + t + 1)
                    if also is not None:
                        also(t)
                    for i in range(4):
                        for k in range(2):
                            f = 2 * i + k
                            ins = nc.tensor.transpose(bs[i][:, k * SEQ + t * P:k * SEQ + (t + 1) * P],
                                                      src[:, t, f * P:(f + 1) * P], ident[:])
                        if t == TT - 1:
                            ins.then_inc(bank_full, 1)
                w.fresh = (banks, name)

            def feature_block(w, o, signal):
                ww = [x.rearrange("p (d c) -> p d c", d=DT) for x in w.take()]
                for d in range(DT):
                    end = d == DT - 1
                    w.rows(d)
                    w.mm3(o, part(ww, ALL, d), part(hT, ALL, d), d == 0, end, signal if end else None)
                w.owed += 1

            def token_group(w, outs, signal):
                for c in range(DT // 2):
                    ww = [x.rearrange("p (d c) -> p d c", d=2) for x in w.take()]
                    w.rows(2 * c)
                    for t in range(TT):
                        for k in range(2):
                            d = 2 * c + k
                            end = d == DT - 1
                            w.mm3(outs[t], part(hT, ALL, d, slice(t * P, (t + 1) * P)), part(ww, ALL, k), d == 0, end,
                                  signal if end else None)
                    w.owed += 1

            def hidden_blocks(w, n, ups, unroll, done, begin, finish, at_bank, beside=None):
                per = ups + 1
                base = w.c

                def chunk(at, i):
                    pe.wait_ge(lo_ready, i * (unroll * per) + (base + at + 1))
                    slot = (base + at) % w.slots
                    return w_hi[slot], w_lo[slot]

                def way_in(at, i, parity, owed):
                    o = ps[:, at_bank + parity, :]
                    for k in range(ups):
                        ww = [x.rearrange("p (d c) -> p d c", d=DT) for x in chunk(at + k, i)]
                        w.owed += owed
                        owed = 0
                        for d in range(DT):
                            w.rows(d)
                            w.mm3(o[:, k * SEQ:(k + 1) * SEQ], part(ww, ALL, d), part(hT, ALL, d), d == 0, d == DT - 1,
                                  None if d < DT - 1 else hid_full if k == ups - 1 else w_used)

                def way_out(at, i, parity, u, owed, start, stop):
                    ww = chunk(at, i)
                    pe.wait_ge(hidw_ready, i * unroll + (done + u + 1))
                    w.owed += owed
                    for t in range(TT):
                        for c in range(2):
                            end = t == TT - 1 and c == 1
                            w.mm3(acc[2 * t + c], (hidw_hi[:, parity, t * P:(t + 1) * P], hidw_lo[:, parity, t * P:(t + 1) * P]),
                                  part(ww, ALL, slice(c * 512, (c + 1) * 512)), start, stop,
                                  out_full if stop and c == 1 else w_used if end else None)

                def one_pass(i, is_first=False, is_last=False):
                    for u in range(unroll):
                        at = ups + u * per
                        more = ups > 0 and not (is_last and u == unroll - 1)
                        if more:
                            way_in(at, i, (u + 1) % 2, 0)
                        if beside is not None:
                            beside(i, u)
                        way_out(at + ups if more else at, i, u % 2, u, (2 if is_first and u == 0 else 1) if more else 0,
                                begin and is_first and u == 0, finish and is_last and u == unroll - 1)

                if ups:
                    owed, w.owed = w.owed, 0
                    way_in(0, 0, 0, owed)
                one_pass(0, is_first=True)
                with pe.Fori(1, n // unroll - 1) as i:
                    one_pass(i)
                one_pass(n // unroll - 1, is_last=True)
                w.c += n * per

            def block1():
                B = banks1
                w = Stream(PAIR1)
                transpose_rows(w, B, "xT", xn, 0)
                for i in range(4):
                    b = open_bank(pe, B, f"qk{i}")
                    for k in range(2):
                        feature_block(w, b[:, k * SEQ:(k + 1) * SEQ], bank_full if k else None)
                for g in ("dq", "dk", "rv", "dv", "rg"):
                    token_group(w, [open_bank(pe, B, f"{g}{t}") for t in range(TT)], bank_full)

                def ret_scores(h):
                    b = open_bank(pe, B, f"S{h}")
                    r = slice(64 * (h % 2), 64 * (h % 2) + 64)
                    for s in range(TT):
                        w.mm(b[:, s * SEQ:(s + 1) * SEQ], rqkT[r, 4 + h // 2, s * P:(s + 1) * P],
                             rqkT[r, h // 2, :], True, True, bank_full if s else None)

                def ret_out(h):
                    after_emptied(pe, B, f"S{h}")
                    for t in range(TT):
                        for s in range(TT):
                            end = h == RH - 1 and t == TT - 1 and s == TT - 1
                            w.mm(acc[t][:, h * 64:(h + 1) * 64], scm[:, h % 2, s, t * P:(t + 1) * P],
                                 rv[:, s, h * 64:(h + 1) * 64], s == 0, s == TT - 1, out_full if end else None)

                after_emptied(pe, B, "qk3")
                ret_scores(0)
                after_emptied(pe, B, "rv1")
                for h in range(RH):
                    if h + 1 < RH:
                        ret_scores(h + 1)
                    ret_out(h)

                pe.wait_ge(dqk_ready, 1)
                for h in range(DH):
                    b = open_bank(pe, B, f"dT{h}")
                    for k in range(2):
                        for t in range(TT):
                            ins = nc.tensor.transpose(b[:, k * SEQ + t * P:k * SEQ + (t + 1) * P],
                                                      dqk[:, t, k, h * P:(h + 1) * P], ident[:])
                    ins.then_inc(bank_full, 1)
                for k in range(2 * DH):
                    h, m = k // 2, k % 2
                    b = open_bank(pe, B, f"sc{k}")
                    after_emptied(pe, B, f"dT{h}")
                    r = slice(64 * m, 64 * m + 64)
                    for t in range(TT):
                        w.mm(b[:, t * SEQ:(t + 1) * SEQ], dqkT[r, h, 0, t * P:(t + 1) * P], dqkT[r, h, 1, :],
                             True, True, bank_full if t else None)

                def diff_out(h):
                    after_emptied(pe, B, f"aT{h}")
                    for t in range(TT):
                        for s in range(TT):
                            end = h == DH - 1 and t == TT - 1 and s == TT - 1
                            w.mm(acc[2 + t][:, h * P:(h + 1) * P], attnT[:, h % 2, s, t * P:(t + 1) * P],
                                 dv[:, s, h * P:(h + 1) * P], s == 0, s == TT - 1, out_full if end else None)

                for h in range(DH):
                    b = open_bank(pe, B, f"aT{h}")
                    pe.wait_ge(attn_ready, TT * (h + 1))
                    for s in range(TT):
                        for t in range(TT):
                            ins = nc.tensor.transpose(b[:, s * SEQ + t * P:s * SEQ + (t + 1) * P],
                                                      attn[:, (TT * h + t) % 4, s * P:(s + 1) * P], ident[:])
                    ins.then_inc(bank_full, 1)
                    if h >= 1:
                        diff_out(h - 1)
                diff_out(DH - 1)

                pe.wait_ge(retmix_ready, TT)
                transpose_rows(w, B, "mT", mix, TT)
                for c in range(2):
                    token_group(w, [acc[2 * t + c] for t in range(TT)], out_full)

                transpose_rows(w, B, "fT", xn, 2 * TT)
                hidden_blocks(w, FF_BLOCKS, 2, 2, 0, True, True, FF_BANK)

            def block2():
                B = banks2
                w = Stream(PAIR2)
                transpose_rows(w, B, "xT", x_res, None)
                for name in ("cfa", "cfg", "scc", "sch", "scb", "swq", "swk"):
                    b = open_bank(pe, B, name)
                    n = 1 if name == "swk" else 2
                    for k in range(n):
                        feature_block(w, b[:, k * SEQ:(k + 1) * SEQ], bank_full if k == n - 1 else None)
                token_group(w, [open_bank(pe, B, f"m{t}") for t in range(TT)], bank_full)
                b = open_bank(pe, B, "kr")
                ww = [x[:, 0:DT * 32].rearrange("p (d c) -> p d c", d=DT) for x in w.take()]
                for t in range(TT):
                    for d in range(DT):
                        end = t == TT - 1 and d == DT - 1
                        w.mm3(b[:, t * 32:(t + 1) * 32], part(hT, ALL, d, slice(t * P, (t + 1) * P)), part(ww, ALL, d),
                              d == 0, d == DT - 1, bank_full if end else None)
                w.owed += 1

                after_emptied(pe, B, "swk")
                for h in range(AH):
                    b = open_bank(pe, B, f"ws{h}")
                    r = slice(64 * (h // 2), 64 * (h // 2) + 64)
                    for t in range(TT):
                        w.mm(b[:, t * SEQ:(t + 1) * SEQ], swqk[r, h % 2, t * P:(t + 1) * P], swqk[r, 2, :],
                             True, True, bank_full if t else None)

                pe.wait_ge(cn_ready, 1)
                b = open_bank(pe, B, "cqT")
                for k in range(2):
                    for t in range(TT):
                        ins = nc.tensor.transpose(b[:, k * SEQ + t * P:k * SEQ + (t + 1) * P],
                                                  mtok[:, t, k * P:(k + 1) * P], ident[:])
                ins.then_inc(bank_full, 1)
                b = open_bank(pe, B, "ckvT")
                for t in range(TT):
                    ins = nc.tensor.transpose(b[:, t * P:(t + 1) * P], mtok[:, t, 2 * P:3 * P], ident[:])
                ins.then_inc(bank_full, 1)
                pe.wait_ge(late_ready, 32)
                uq = small_sb[:, slice(*m2["uq"])].rearrange("p (k c) -> p k c", k=2)
                after_emptied(pe, B, "cqT")
                for t in range(TT):
                    b = open_bank(pe, B, f"uq{t}")
                    for k in range(2):
                        w.mm(b[:, 0:AH * QK], cqT[:, k, t * P:(t + 1) * P], uq[:, k, :], k == 0, k == 1,
                             bank_full if k else None)
                after_emptied(pe, B, "ckvT")
                for t in range(TT):
                    b = open_bank(pe, B, f"kv{t}")
                    w.mm(b, ckvT[:, t * P:(t + 1) * P], small_sb[:, slice(*m2["ukv"])], True, True, bank_full)

                def attend(k0, name, values, sums):
                    def outs(h):
                        after_emptied(pe, B, f"{name}{h}")
                        for t in range(TT):
                            for s in range(t + 1):
                                end = h == AH - 1 and t == TT - 1 and s == t
                                w.mm(sums[t][:, h * 64:(h + 1) * 64], probT[:, h % 2, s, t * P:(t + 1) * P],
                                     values(s, h), s == 0, s == t, out_full if end else None)

                    for h in range(AH):
                        b = open_bank(pe, B, f"{name}{h}")
                        pe.wait_ge(exp_ready, k0 + h + 1)
                        for s in range(TT):
                            for t in range(TT):
                                ins = nc.tensor.transpose(b[:, s * SEQ + t * P:s * SEQ + (t + 1) * P],
                                                          prob2[:, (k0 + h) % 4, t, s * P:(s + 1) * P], ident[:])
                        ins.then_inc(bank_full, 1)
                        if h >= 1:
                            outs(h - 1)
                    outs(AH - 1)

                attend(0, "wT", lambda s, h: mtok[:, s, 384 + 64 * (h // 2):448 + 64 * (h // 2)], acc[2:4])

                pe.wait_ge(conv_ready, 2)
                for name, src in (("scT", scy), ("cvT", cv)):
                    b = open_bank(pe, B, name)
                    for t in range(TT):
                        for k in range(2):
                            ins = nc.tensor.transpose(b[:, t * SEQ + k * P:t * SEQ + (k + 1) * P],
                                                      src[:, k, t * P:(t + 1) * P], ident[:])
                    ins.then_inc(bank_full, 1)

                pe.wait_ge(rope_ready, 1)
                for h in range(AH):
                    b = open_bank(pe, B, f"kT{h}")
                    for k, src in ((0, qtok), (1, kcat)):
                        for t in range(TT):
                            ins = nc.tensor.transpose(b[0:QK, k * SEQ + t * P:k * SEQ + (t + 1) * P],
                                                      src[:, t, h, :], ident[:])
                    ins.then_inc(bank_full, 1)
                for h in range(AH):
                    b = open_bank(pe, B, f"ms{h}")
                    after_emptied(pe, B, f"kT{h}")
                    for t in range(TT):
                        w.mm(b[:, t * SEQ:(t + 1) * SEQ], qkT[0:QK, h, 0, t * P:(t + 1) * P], qkT[0:QK, h, 1, :],
                             True, True, bank_full if t else None)
                attend(AH, "pT", lambda s, h: vtok[:, s, h, :], acc[0:2])

                transpose_rows(w, B, "mT", mix2, 0, lambda t: pe.wait_ge(mixnorm_ready, 2 * t + 2))
                for c in range(2):
                    token_group(w, [acc[2 * t + c] for t in range(TT)], out_full)

                transpose_rows(w, B, "hT", x_res, TT)

                def queries(h):
                    b = open_bank(pe, B, f"q{h}")
                    for k in range(2):
                        feature_block(w, b[:, k * SEQ:(k + 1) * SEQ], bank_full if k else None)

                def key_scores(h):
                    b = open_bank(pe, B, f"rs{h}")
                    after_emptied(pe, B, f"q{h}")
                    for t in range(TT):
                        for k in range(2):
                            at = (2 * t + k) * NK
                            w.mm(b[:, at:at + NK], pqT[:, h % 2, k, t * P:(t + 1) * P], sub_sb[:, 2 * h + k, :],
                                 True, True, bank_full if t and k else None)

                queries(0)
                for h in range(PH):
                    if h + 1 < PH:
                        queries(h + 1)
                    key_scores(h)

                def gate_group(n, i, step, free):
                    s = n % 2
                    b = ps[:, 6 + s, :]
                    if free:
                        pe.wait_ge(gates_out, i * step + (n - 1))
                    pe.wait_ge(onehot_ready, i * step + (n + 1))
                    for k in range(GROUP):
                        for m in range(PIECES):
                            ins = nc.tensor.matmul(b[:, k * JQ:(k + 1) * JQ], one_i[:, s, k // 2, :, k % 2],
                                                   gate_j[:, s, k // 2, m, :, k % 2], start=m == 0, stop=m == PIECES - 1)
                    ins.then_inc(onehot_used, 1)

                def stash_in(b, i, free):
                    if free:
                        pe.wait_ge(hid_ready, i * 4 + (b - 1))
                    pe.wait_ge(lo_ready, i * 4 + (N2_PRE + b + 1))
                    slot = (N2_PRE + b) % w.slots
                    ww = [x.rearrange("p (d c) -> p d c", d=DT) for x in (w_hi[slot], w_lo[slot])]
                    for d in range(DT):
                        w.mm3(ps[:, PEER_BANK + b % 2, 0:SEQ], part(ww, ALL, d), part(hT, ALL, d), d == 0, d == DT - 1,
                              hid_full if d == DT - 1 else None)
                    w.owed += 1

                after_emptied(pe, B, "rs7")
                for u in range(4):
                    stash_in(u, 0, u >= 2)
                with pe.Fori(1, JQ // 4) as i:
                    for u in range(4):
                        stash_in(u, i, True)

                pe.wait_ge(chosen_ready, 1)
                for name, parts in (("iT", (0, 1)), ("gT", (2,))):
                    b = open_bank(pe, B, name)
                    for k, c in enumerate(parts):
                        for t in range(TT):
                            ins = nc.tensor.transpose(b[:, k * SEQ + t * P:k * SEQ + (t + 1) * P], chosen[:, c, t, :],
                                                      ident[:])
                    ins.then_inc(bank_full, 1)
                after_emptied(pe, B, "gT")

                def stash_and_gates(u, i, first):
                    stash_in(JQ + u, i, True)
                    for g in (2 * u, 2 * u + 1):
                        gate_group(g, i, 8, not first or g >= 2)

                for u in range(4):
                    stash_and_gates(u, 0, True)
                with pe.Fori(1, (STASH - JQ) // 4) as i:
                    for u in range(4):
                        stash_and_gates(u, i, False)
                w.c += STASH
                for first, n in RUNS:
                    hidden_blocks(w, n, 0 if first < STASH else 1, 4, first, first == 0, first + n == NK, PEER_BANK,
                                  (lambda i, u: gate_group(JQ + first + u, i, 4, True)) if first < NK - JQ else None)

            pe.wait_ge(const_ready, CONSTS)
            for n, layer in ((1, block1), (1 + DEPTH, block2)):
                with pe.Fori(0, DEPTH) as l:
                    enter_layer(pe, "pe", l + n)
                    layer()
                    leave_layer(pe, "pe", out_full, LAST_SUMS)

        @block.scalar
        def _(act):
            A = nc.scalar.activation

            def root(n, std, ms, scale, eps):
                act.wait_ge(ms_ready, n)
                A(std, ms, ACT.Sqrt, bias=eps[:, 0:1], scale=scale).then_inc(std_ready, 1)

            class Split:

                def __init__(self, raws, pairs, head):
                    self.raws, self.pairs, self.head, self.c = raws, pairs, head, 0

                def one(self, c, i=0, step=0):
                    slot = c % self.raws
                    act.wait_ge(w_ready[slot], i * (16 * step // self.raws) + 16 * (c // self.raws + 1))
                    if c >= self.pairs:
                        act.wait_ge(w_used, i * step + (c - self.pairs + 1))
                    A(w_hi[c % self.pairs], raw[:, slot, :], ACT.Copy).then_inc(hi_ready, 1)

                def upto(self, n):
                    n = min(n + AHEAD, self.head)
                    for c in range(self.c, n):
                        self.one(c)
                    self.c = max(self.c, n)

            def filled(B, w, name):
                w.upto(B.chunks[name])
                return take_bank(act, B, name)

            def empty_transposed(B, w, name, scale):
                for i in range(4):
                    b = filled(B, w, f"{name}{i}")
                    if scale is None:
                        ins = A(hT_hi[:, 2 * i:2 * i + 2, :], b.rearrange("p (k t) -> p k t", k=2), ACT.Copy)
                    else:
                        for k in range(2):
                            f = 2 * i + k
                            ins = A(hT_hi[:, f, :], b[:, k * SEQ:(k + 1) * SEQ], ACT.Copy, scale=scale[:, f:f + 1])
                    ins.then_inc(xhi_ready, 1)

            def empty(B, w, name, dst, n=512, func=ACT.Copy, scale=1.0):
                b = filled(B, w, name)
                A(dst, b[:, 0:n], func, scale=scale).then_inc(emptied["act"], 1)

            def hidden(w, base, n, ups, unroll, done, func, finish, at_bank, beside=None):
                per = ups + 1

                def one(i, u, free, ahead):
                    for k in range(ahead):
                        w.one(base + ups + per * u + k, i, unroll * per)
                    act.wait_ge(hid_full, i * unroll + (done + u + 1))
                    if free:
                        act.wait_ge(hidw_ready, i * unroll + (done + u - 1))
                    A(hid[:, u % 2, :], ps[:, at_bank + u % 2, 0:SEQ], func).then_inc(hid_ready, 1)
                    if beside is not None:
                        beside(i, u)

                passes = n // unroll
                for u in range(unroll):
                    one(0, u, done > 0 or u >= 2, per)
                with act.Fori(1, passes - 1) as i:
                    for u in range(unroll):
                        one(i, u, True, per)
                for u in range(unroll):
                    one(passes - 1, u, True, per - ups if finish and u == unroll - 1 else per)

            def block1():
                B = banks1
                base = N1 - 3 * FF_BLOCKS
                w = Split(RAW1, PAIR1, base + 2)
                w.upto(0)
                root(1, std_x, ss_x, 1.0 / D, eps1)
                act.wait_ge(par_ready, 32)
                empty_transposed(B, w, "xT", col1_sb[:, 0:DT])
                A(dece, row1_sb[:, slice(*r1["dec"])], ACT.Exp).then_inc(dec_ready, 1)
                act.wait_ge(lam_ready, 1)
                A(lam_e, lam_s, ACT.Exp).then_inc(lame_ready, 1)
                for i in range(4):
                    empty(B, w, f"qk{i}", rqkT[:, 2 * i:2 * i + 2, :].rearrange("p k t -> p (k t)"),
                          scale=1.0 if i < 2 else 64 ** -0.5)
                act.wait_ge(dist_ready, 1)
                A(decay, decay, ACT.Exp, scale=-1.0).then_inc(decay_ready, 1)
                for t in range(TT):
                    empty(B, w, f"rv{t}", rv[:, t, :])
                root(2, std_g, ss_g, 1.0 / 64, eps1)
                for t in range(TT):
                    empty(B, w, f"dv{t}", dv[:, t, :])
                for t in range(TT):
                    empty(B, w, f"rg{t}", rgate[:, t, :], func=ACT.Silu)
                act.wait_ge(turn_ready, 1)
                A(sin_t[:], turns[:, 0], ACT.Sin)
                A(cos_t[:], turns[:, 1], ACT.Sin)
                act.wait_ge(out_full, 1)
                for t in range(TT):
                    nc.scalar.copy(ret[:, t, :], acc[t]).then_inc(ret_copied, 1)
                for h in range(DH):
                    empty(B, w, f"dT{h}", dqkT[:, h].rearrange("p k t -> p (k t)"))

                def exps(k):
                    act.wait_ge(negmax_ready, k + 1)
                    for m in range(2):
                        ins = A(prob[:, k % 4, m, :], prob[:, k % 4, m, :], ACT.Exp, bias=negmax[:, k, m:m + 1],
                                accum_out=sums[:, k, m:m + 1])
                    ins.then_inc(exp_ready, 1)

                for k in range(4):
                    exps(k)
                for h in range(DH):
                    empty(B, w, f"aT{h}", attnT[:, h % 2].rearrange("p s t -> p (s t)"))
                    if h < 2:
                        exps(4 + 2 * h)
                        exps(5 + 2 * h)
                root(3, std_r, ss_r, 1.0 / 64, eps1)
                act.wait_ge(out_full, 2)
                for t in range(TT):
                    for h in range(DH):
                        c = slice(h * P, (h + 1) * P)
                        ins = A(sq[:, t, c], acc[2 + t][:, c], ACT.Square, accum_out=ss_d[:, t, h:h + 1])
                ins.then_inc(act_step, 1)
                act.wait_ge(act_step, 1)
                A(std_d, ss_d, ACT.Sqrt, bias=eps1[:, 0:1], scale=1.0 / 128).then_inc(std_ready, 1)
                empty_transposed(B, w, "mT", None)
                w.upto(B.chunks["fT0"])
                root(4, std_x, ss_x, 1.0 / D, eps1)
                empty_transposed(B, w, "fT", col1_sb[:, DT:2 * DT])
                hidden(w, base, FF_BLOCKS, 2, 2, 0, ACT.Silu, True, FF_BANK)

            def block2():
                B = banks2
                w = Split(RAW2, PAIR2, N2_PRE + AHEAD)
                sinks = row2_sb[:, slice(*r2["sinks"])]
                empty_transposed(B, w, "xT", None)
                flat = lambda x: x.rearrange("p k t -> p (k t)")
                empty(B, w, "cfa", flat(cfa))
                empty(B, w, "cfg", flat(cfg), func=ACT.Sigmoid)
                empty(B, w, "scc", flat(scc))
                empty(B, w, "scb", flat(scb))
                empty(B, w, "swq", flat(swqk[:, 0:2, :]))
                empty(B, w, "swk", swqk[:, 2, :], n=SEQ)
                for t in range(TT):
                    empty(B, w, f"m{t}", mtok[:, t, :])
                empty(B, w, "kr", flat(krt), n=TT * 32)
                root(1, std_m, ss_m, 1.0, eps2)

                def exps(k):
                    act.wait_ge(negmax_ready, k + 1)
                    for t in range(TT):
                        ins = A(prob2[:, k % 4, t, :], prob2[:, k % 4, t, :], ACT.Exp, bias=negmax2[:, k, t:t + 1],
                                accum_out=sums2[:, k, t:t + 1])
                    if k < AH:
                        ins = A(esink[:, k, :], negmax2[:, k, :], ACT.Exp, bias=sinks[:, k:k + 1])
                    ins.then_inc(exp_ready, 1)

                act.wait_ge(par_ready, 32)
                for h in range(AH):
                    exps(h)
                for t in range(TT):
                    empty(B, w, f"uq{t}", qtok[:, t].rearrange("p h c -> p (h c)"), n=AH * QK)
                for t in range(TT):
                    b = filled(B, w, f"kv{t}").rearrange("p (k h c) -> p k h c", k=2, h=AH)
                    nc.scalar.copy(kcat[:, t, :, 0:64], b[:, 0])
                    nc.scalar.copy(vtok[:, t], b[:, 1]).then_inc(emptied["act"], 1)
                for h in range(AH):
                    empty(B, w, f"wT{h}", flat(probT[:, h % 2]))
                b = filled(B, w, "scT")
                nc.scalar.copy(mix2[:, :, 0:256], b.rearrange("p (t c) -> p t c", t=TT)).then_inc(emptied["act"], 1)
                empty(B, w, "cvT", flat(cvt))
                for h in range(AH):
                    b = filled(B, w, f"kT{h}")
                    A(flat(qkT[0:QK, h]), b[0:QK, :], ACT.Copy).then_inc(emptied["act"], 1)
                for h in range(AH):
                    exps(AH + h)
                empty(B, w, "pT0", flat(probT[:, 0]))
                root(2, std_l, mv[:, :, 1], 1.0, eps2)
                for h in (1, 2):
                    empty(B, w, f"pT{h}", flat(probT[:, h % 2]))
                act.wait_ge(cfg_ready, 1)
                A(mix2[:, :, 512:768], cvt, ACT.Silu).then_inc(cfmix_ready, 1)
                empty(B, w, "pT3", flat(probT[:, 1]))
                act.wait_ge(ms_ready, 3)
                A(std_x2[:, :, 0:4], ss_x2[:, :, 0:4], ACT.Sqrt, bias=eps2[:, 0:1], scale=1.0 / 64)
                root(3, std_x2[:, :, 8:16], ss_x2[:, :, 8:16], 1.0 / 64, eps2)
                root(4, std_x2[:, :, 4:8], ss_x2[:, :, 4:8], 1.0 / 64, eps2)
                empty_transposed(B, w, "mT", col2_sb[:, slice(*c2["mix_g"])])
                w.upto(B.chunks["hT0"])
                root(5, std_l, mv[:, :, 1], 1.0, eps2)
                empty_transposed(B, w, "hT", None)

                def queries(h):
                    empty(B, w, f"q{h}", flat(pqT[:, h % 2]))

                queries(0)
                for h in range(PH):
                    if h + 1 < PH:
                        queries(h + 1)
                    empty(B, w, f"rs{h}", rs[:, h].rearrange("p t k n -> p (t k n)"))
                def stash_in(b, i):
                    w.one(N2_PRE + AHEAD + b, i, 4)
                    act.wait_ge(hid_full, i * 4 + (b + 1))
                    k, at = (0, b + i * 4) if b < JQ else (1, b - JQ + i * 4)
                    dst = stash[k][:, at, :] if isinstance(at, int) else stash[k][:, bass.ds(at, 1), :].rearrange(
                        "p b t -> p (b t)")
                    A(dst, ps[:, PEER_BANK + b % 2, 0:SEQ], ACT.Gelu).then_inc(hid_ready, 1)

                def gates_of(n, i, step):
                    act.wait_ge(onehot_used, i * step + (n + 1))
                    at = i * (step * GROUP) + n % JQ * GROUP
                    tokens = slice(at, at + GROUP) if isinstance(i, int) else bass.ds(at, GROUP)
                    nc.scalar.copy(gates[:, n // JQ % 2, tokens, :], ps[:, 6 + n % 2, 0:GROUP * JQ].rearrange(
                        "p (t j) -> p t j", t=GROUP)).then_inc(gates_out, 1)

                exp_at = JQ // 8 * 6
                for u in range(4):
                    stash_in(u, 0)
                with act.Fori(1, exp_at // 4) as i:
                    for u in range(4):
                        stash_in(u, i)
                act.wait_ge(score_ready, 1)
                A(chosen[:, 2], chosen[:, 2], ACT.Exp).then_inc(gexp_ready, 1)
                with act.Fori(exp_at // 4, JQ // 4) as i:
                    for u in range(4):
                        stash_in(u, i)
                b = take_bank(act, B, "iT")
                nc.scalar.copy(i1T[:], b[:, 0:SEQ])
                nc.scalar.copy(i2T[:], b[:, SEQ:2 * SEQ]).then_inc(emptied["act"], 1)
                b = take_bank(act, B, "gT")
                nc.scalar.copy(gT, b[:, 0:SEQ]).then_inc(emptied["act"], 1)

                def stash_and_gates(u, i):
                    stash_in(JQ + u, i)
                    for g in (2 * u, 2 * u + 1):
                        gates_of(g, i, 8)

                with act.Fori(0, (STASH - JQ) // 4) as i:
                    for u in range(4):
                        stash_and_gates(u, i)

                for first, n in RUNS:
                    def gates_before(i, u):
                        if first < JQ and not (isinstance(i, int) and i * 4 + u == 0):
                            act.wait_ge(hidw_ready, i * 4 + u)
                        if u > 0:
                            gates_of(JQ + first + u - 1, i, 4)
                        elif not (isinstance(i, int) and i == 0):
                            gates_of(JQ + first + 3, i - 1, 4)

                    more = first < NK - JQ
                    if first == JQ:
                        act.wait_ge(hidw_ready, first)
                    if first < STASH:
                        def pass_on(i, ahead):
                            for u in range(4):
                                if u < ahead:
                                    w.one(N2_OUT + AHEAD + first + u, i, 4)
                                gates_before(i, u)

                        pass_on(0, 4)
                        with act.Fori(1, n // 4 - 1) as i:
                            pass_on(i, 4)
                        pass_on(n // 4 - 1, 4 if first + n < STASH else 3)
                    else:
                        hidden(w, run_base(first), n, 1, 4, first, ACT.Gelu, not more, PEER_BANK,
                               gates_before if more else None)
                    if more:
                        if first < JQ:
                            act.wait_ge(hidw_ready, n)
                        gates_of(JQ + first + n - 1, 0, 4)
                root(6, std3, mv3[:, :, 1], 1.0, eps2)

            act.wait_ge(const_ready, CONSTS)
            for n, layer, s, m in ((1, block1, hid_ready, FF_BLOCKS), (1 + DEPTH, block2, std_ready, 6)):
                with act.Fori(0, DEPTH) as l:
                    enter_layer(act, "act", l + n)
                    layer()
                    leave_layer(act, "act", s, m)

        @block.vector
        def _(dve):
            V = nc.vector

            def setup():
                step = Steps(dve, dist_step)
                dve.wait_ge(rel_ready, 1)
                step(V.tensor_scalar(after[:], rel[:], 0.0, None, ALU.max))
                step(V.tensor_scalar(before[:], rel[:], -1.0, 0.0, ALU.mult, ALU.max))
                step.settle()
                step(V.tensor_tensor(absd[:], after[:], before[:], ALU.add))
                step.settle()
                for h in range(DH):
                    step(V.tensor_scalar(alibi[:, h], absd[:], -(2.0 ** (-2.0 * (h + 1))), None, ALU.mult))

            def angles(step):
                dve.wait_ge(setup_in, 32)
                step(V.tensor_copy(pos_f, pos_i))
                step.settle()
                two_pi = 2 * np.pi
                parts = [6.28125]
                parts.append(float(np.float32(np.round((two_pi - parts[0]) * 2 ** 22) / 2 ** 22)))
                parts.append(float(np.float32(two_pi - parts[0] - parts[1])))
                big = 1.5 * 2 ** 23
                for t in range(TT):
                    step(V.tensor_scalar(angle, invf, pos_f[:, t:t + 1], None, ALU.mult))
                    step.settle()
                    for b in range(2):
                        r, n = turns[:, b, t, :], turn_n[:, b, t, :]
                        step(V.tensor_scalar(n, angle, float(1 / two_pi), 0.25 * b, ALU.mult, ALU.add))
                        step.settle()
                        step(V.tensor_scalar(n, n, big, None, ALU.add))
                        step.settle()
                        step(V.tensor_scalar(n, n, -big, None, ALU.add))
                        step.settle()
                        for k, c in enumerate(parts):
                            step(V.scalar_tensor_tensor(out=r, in0=n, scalar=-c, in1=angle if k == 0 else r,
                                                        op0=ALU.mult, op1=ALU.add))
                            step.settle()
                        step(V.tensor_scalar(r, r, float(np.pi / 2) * b, PI, ALU.add, ALU.min))
                        step.settle()
                        step(V.tensor_scalar(r, r, -PI, None, ALU.max))
                        step.settle()
                dve.sem_inc(turn_ready, 1)

            class Transposed:

                def __init__(self):
                    self.n = 0

                def __call__(self, B, name, scale):
                    for i in range(4):
                        self.n += 1
                        dve.wait_ge(xhi_ready, self.n)
                        b = bank(B, f"{name}{i}")
                        if scale is None:
                            f = slice(2 * i, 2 * i + 2)
                            ins = V.tensor_tensor(hT_lo[:, f, :], b.rearrange("p (k t) -> p k t", k=2),
                                                  hT_hi[:, f, :].bitcast(F32), ALU.subtract)
                        else:
                            for k in range(2):
                                f = 2 * i + k
                                ins = V.scalar_tensor_tensor(out=hT_lo[:, f, :], in0=b[:, k * SEQ:(k + 1) * SEQ],
                                                             scalar=scale[:, f:f + 1], in1=hT_hi[:, f, :].bitcast(F32),
                                                             op0=ALU.mult, op1=ALU.subtract)
                        ins.then_inc(emptied["dve"], 1)

            def gated(i, unroll, u, done, base, ups, value, gate, free):
                s = u % 2
                dve.wait_ge(hid_ready, i * unroll + (done + u + 1))
                if free:
                    first = isinstance(i, int) and i == 0 and u < 2
                    dve.wait_ge(w_used, base + u - 1 if first else i * (unroll * (ups + 1)) + (base + (ups + 1) * (u - 1) + ups))
                V.tensor_tensor(gated_hid[:, s, :], value, gate, ALU.mult).then_inc(gate_step, 1)
                V.tensor_tensor(hidw_hi[:, s, :], value, gate, ALU.mult).then_inc(gate_step, 1)
                dve.wait_ge(gate_step, i * (2 * unroll) + 2 * (done + u + 1))
                V.tensor_tensor(hidw_lo[:, s, :], gated_hid[:, s, :], hidw_hi[:, s, :].bitcast(F32),
                                ALU.subtract).then_inc(hidw_ready, 1)

            def root_of(step, n):
                step.settle()
                dve.sem_inc(ms_ready, 1)
                dve.wait_ge(std_ready, n)

            def over(x, n):
                return x.unsqueeze(2).broadcast_to([P, x.shape[1], n])

            def under(x, g):
                return x.unsqueeze(1).broadcast_to([P, g, x.shape[1]])

            def grouped(x, g):
                return x.rearrange("p (g c) -> p g c", g=g)

            def slice_of(t):
                return slice(P - t * P, P - t * P + SEQ)

            def norm_x(step, n):
                for t in range(TT):
                    step(V.tensor_tensor_reduce(out=xn[:, t, :], in0=x_res[:, t, :], in1=x_res[:, t, :], scale=1.0,
                                                scalar=0.0, op0=ALU.mult, op1=ALU.add, accum_out=ss_x[:, t:t + 1]))
                root_of(step, n)
                step(V.reciprocal(rstd_x, std_x))
                step.settle()
                for t in range(TT):
                    V.tensor_scalar(xn[:, t, :], x_res[:, t, :], rstd_x[:, t:t + 1], None,
                                    ALU.mult).then_inc(rows_ready, 1)

            def block1():
                B = banks1
                step = Steps(dve, dve_step)
                empty_transposed = Transposed()
                par = lambda k: row1_sb[:, slice(*r1[k])]
                norm_x(step, 1)
                dve.wait_ge(par_ready, 32)
                lq, lk = par("lq"), par("lk")
                for m in range(2):
                    s = slice(64 * m, 64 * m + 64)
                    step(V.tensor_tensor_reduce(out=sq[:, 0, s], in0=lq[:, s], in1=lk[:, s], scale=1.0, scalar=0.0,
                                                op0=ALU.mult, op1=ALU.add, accum_out=lam_s[:, m:m + 1]))
                step(V.tensor_scalar(gq, par("dq_g"), 64 ** -0.5, None, ALU.mult))
                step(V.tensor_scalar(gd, par("diff_g"), par("out_scale"), None, ALU.mult))
                step.settle()
                dve.sem_inc(lam_ready, 1)
                empty_transposed(B, "xT", col1_sb[:, 0:DT])
                dve.wait_ge(lame_ready, 1)
                step(V.tensor_tensor(lam_d, lam_e[:, 0:1], lam_e[:, 1:2], ALU.subtract))
                step.settle()
                step(V.tensor_tensor(lam, lam_d, par("lam_init"), ALU.add))
                dve.wait_ge(dec_ready, 1)
                for h in range(RH):
                    step(V.tensor_scalar(decay[:, h], after[:], dece[:, h:h + 1], None, ALU.mult))
                step.settle()
                for h in range(RH):
                    step(V.scalar_tensor_tensor(out=decay[:, h], in0=before[:], scalar=dece[:, RH + h:RH + h + 1],
                                                in1=decay[:, h], op0=ALU.mult, op1=ALU.add))
                step.settle()
                dve.sem_inc(dist_ready, 1)
                angles(step)

                for k, g in enumerate(("dq", "dk")):
                    for t in range(TT):
                        b = take_bank(dve, B, f"{g}{t}")
                        V.tensor_copy(dqk[:, t, k, :], b).then_inc(emptied["dve"], 1)
                    for t in range(TT):
                        after_emptied(dve, B, f"{g}{t}")
                        step(V.tensor_tensor(sq[:, t, :], dqk[:, t, k, :], dqk[:, t, k, :], ALU.mult))
                    step.settle()
                    for t in range(TT):
                        step(V.tensor_reduce(ss_g[:, t, k, :], grouped(sq[:, t, :], 8), AX_X, ALU.add))
                root_of(step, 2)
                step(V.reciprocal(rstd_g, std_g))
                step.settle()
                for k in range(2):
                    for t in range(TT):
                        x = grouped(dqk[:, t, k, :], 8)
                        step(V.tensor_tensor(x, x, over(rstd_g[:, t, k, :], 64), ALU.mult))
                step.settle()
                for k in range(2):
                    for t in range(TT):
                        x = grouped(dqk[:, t, k, :], 8)
                        ins = V.tensor_tensor(x, x, under(gq if k == 0 else par("dk_g"), 8), ALU.mult)
                ins.then_inc(dqk_ready, 1)

                dve.wait_ge(decay_ready, 1)
                for h in range(RH):
                    b = take_bank(dve, B, f"S{h}")
                    for s in range(TT):
                        ins = V.tensor_tensor(scm[:, h % 2, s, :], b[:, s * SEQ:(s + 1) * SEQ], decay[:, h, slice_of(s)],
                                              ALU.mult)
                    ins.then_inc(emptied["dve"], 1)

                def biased(k):
                    h = k // 2
                    b = take_bank(dve, B, f"sc{k}")
                    if h >= 2:
                        dve.wait_ge(attn_ready, TT * (h - 1))
                    for t in range(TT):
                        ins = V.tensor_tensor_reduce(out=prob[:, k % 4, t, :], in0=b[:, t * SEQ:(t + 1) * SEQ],
                                                     in1=alibi[:, h, slice_of(t)], scale=1.0, scalar=REPLACED,
                                                     op0=ALU.add, op1=ALU.max, accum_out=rowmax[:, k, t:t + 1])
                    ins.then_inc(emptied["dve"], 1)
                    after_emptied(dve, B, f"sc{k}")
                    V.tensor_scalar(negmax[:, k, :], rowmax[:, k, :], -1.0, None, ALU.mult).then_inc(negmax_ready, 1)

                def difference(h):
                    dve.wait_ge(exp_ready, 2 * h + 2)
                    one, two = 2 * h, 2 * h + 1
                    step(V.reciprocal(rsum[:, one:two + 1, :], sums[:, one:two + 1, :]))
                    step.settle()
                    step(V.tensor_scalar(rsum[:, two, :], rsum[:, two, :], lam, None, ALU.mult))
                    step.settle()
                    if h >= 2:
                        dve.wait_ge(bank_full, B.index[f"aT{h - 2}"] + 1)
                    slots = [(TT * h + t) % 4 for t in range(TT)]
                    for t in range(TT):
                        step(V.tensor_scalar(attn[:, slots[t], :], prob[:, two % 4, t, :], rsum[:, two, t:t + 1], None,
                                             ALU.mult))
                    step.settle()
                    for t in range(TT):
                        V.scalar_tensor_tensor(out=attn[:, slots[t], :], in0=prob[:, one % 4, t, :],
                                               scalar=rsum[:, one, t:t + 1], in1=attn[:, slots[t], :],
                                               op0=ALU.mult, op1=ALU.subtract).then_inc(attn_ready, 1)

                for h in range(DH):
                    biased(2 * h)
                    biased(2 * h + 1)
                    if h >= 1:
                        difference(h - 1)
                difference(DH - 1)

                dve.wait_ge(retsq_ready, TT)
                for t in range(TT):
                    step(V.tensor_reduce(ss_r[:, t, :], grouped(ret_sq[:, t, :], RH), AX_X, ALU.add))
                root_of(step, 3)
                V.reciprocal(rstd_r, std_r).then_inc(rstd_ready, 1)
                dve.wait_ge(out_full, 2)
                at = [(t, h, slice(h * P, (h + 1) * P)) for t in range(TT) for h in range(DH)]
                dve.wait_ge(std_ready, 4)
                step(V.reciprocal(rstd_d, std_d))
                step.settle()
                for t, h, c in at:
                    ins = V.scalar_tensor_tensor(out=mix[:, t, 512 + h * P:512 + (h + 1) * P], in0=acc[2 + t][:, c],
                                                 scalar=rstd_d[:, t, h:h + 1], in1=gd, op0=ALU.mult, op1=ALU.mult)
                    if h == DH - 1:
                        ins.then_inc(rows_ready, 1)
                empty_transposed(B, "mT", None)

                for c in range(2):
                    dve.wait_ge(out_full, 2 + TT * (c + 1))
                    for t in range(TT):
                        x = x_res[:, t, c * 512:(c + 1) * 512]
                        step(V.tensor_tensor(x, x, acc[2 * t + c], ALU.add))
                step.settle()
                norm_x(step, 5)
                empty_transposed(B, "fT", col1_sb[:, DT:2 * DT])

                base = N1 - 3 * FF_BLOCKS
                up = lambda u: ps[:, FF_BANK + u, SEQ:2 * SEQ]
                for u in range(2):
                    gated(0, 2, u, 0, base, 2, hid[:, u, :], up(u), False)
                with dve.Fori(1, FF_BLOCKS // 2) as i:
                    for u in range(2):
                        gated(i, 2, u, 0, base, 2, hid[:, u, :], up(u), True)
                for t in range(TT):
                    dve.wait_ge(out_full, LAST_SUMS - TT + t + 1)
                    for c in range(2):
                        x = x_res[:, t, c * 512:(c + 1) * 512]
                        step(V.tensor_tensor(x, x, acc[2 * t + c], ALU.add))
                return step.n

            def layer_norm(step, n, full, dst, g, b, stats, mean_var, std, rstd, signal):
                half = lambda c: slice(c * 512, (c + 1) * 512)
                for count, banks in full:
                    dve.wait_ge(out_full, count)
                    for t, c in banks:
                        step(V.scalar_tensor_tensor(out=dst[:, t, half(c)], in0=x_res[:, t, half(c)], scalar=ALPHA,
                                                    in1=acc[2 * t + c], op0=ALU.mult, op1=ALU.add))
                    step.settle()
                    for t, c in banks:
                        step(V.bn_stats(stats[:, t, c, :], dst[:, t, half(c)]))
                step.settle()
                for t in range(TT):
                    step(V.bn_aggr(mean_var[:, t, :], stats[:, t].rearrange("p c s -> p (c s)")))
                root_of(step, n)
                step(V.reciprocal(rstd, std))
                step.settle()
                for t in range(TT):
                    step(V.scalar_tensor_tensor(out=dst[:, t, :], in0=dst[:, t, :], scalar=mean_var[:, t, 0:1], in1=g,
                                                op0=ALU.subtract, op1=ALU.mult))
                    step.settle()
                    ins = V.scalar_tensor_tensor(out=x_res[:, t, :], in0=dst[:, t, :], scalar=rstd[:, t:t + 1], in1=b,
                                                 op0=ALU.mult, op1=ALU.add)
                    if signal is not None:
                        ins.then_inc(signal, 1)
                    else:
                        step(ins)

            def block2():
                B = banks2
                step = Steps(dve, dve_step)
                empty_transposed = Transposed()
                par = lambda k: row2_sb[:, slice(*r2[k])]
                col = lambda k: col2_sb[:, slice(*c2[k])]
                step(V.memset(cfu[:, :, 0:CF_K - 1], 0.0))
                step(V.memset(scu[:, :, 0:SC_K - 1], 0.0))
                empty_transposed(B, "xT", None)
                dve.wait_ge(mask_ready, MASKS)
                dve.wait_ge(par_ready, 32)
                step(V.tensor_scalar(nsink, par("sinks"), -1.0, None, ALU.mult))

                after_emptied(dve, B, "cfg")
                step(V.tensor_tensor(cfu[:, :, CF_K - 1:], cfa, cfg, ALU.mult))
                after_emptied(dve, B, "scc")
                b = take_bank(dve, B, "sch")
                V.tensor_tensor(scu[:, :, SC_K - 1:], b.rearrange("p (k t) -> p k t", k=2), scc,
                                ALU.mult).then_inc(emptied["dve"], 1)
                after_emptied(dve, B, "sch")

                def conv(dst, src, taps, w, bias, some):
                    step.settle()
                    for k in some:
                        for c in range(2):
                            x, tap = src[:, c, k:k + SEQ], w[:, c * taps + k:c * taps + k + 1]
                            if k == 0:
                                step(V.tensor_scalar(dst[:, c, :], x, tap, 0.0 if bias is None else bias[:, c:c + 1],
                                                     ALU.mult, ALU.add))
                            else:
                                step(V.scalar_tensor_tensor(out=dst[:, c, :], in0=x, scalar=tap, in1=dst[:, c, :],
                                                            op0=ALU.mult, op1=ALU.add))
                        step.settle()

                conv(scy, scu, SC_K, col("sc_w"), None, range(SC_K))
                after_emptied(dve, B, "scb")
                V.tensor_tensor(scy, scy, scb, ALU.mult).then_inc(conv_ready, 1)
                conv(cv, cfu, CF_K, col("cf_w"), col("cf_bias"), range(CF_SPLIT))

                after_emptied(dve, B, "m1")
                parts = ((0, 256), (256, 384))
                for t in range(TT):
                    for k, (a, z) in enumerate(parts):
                        x = mtok[:, t, a:z]
                        step(V.tensor_tensor_reduce(out=sq2[:, t * 512 + a:t * 512 + z], in0=x, in1=x, scale=1.0 / (z - a),
                                                    scalar=0.0, op0=ALU.mult, op1=ALU.add,
                                                    accum_out=ss_m[:, 2 * t + k:2 * t + k + 1]))
                root_of(step, 1)
                step(V.reciprocal(rstd_m, std_m))
                step.settle()
                for t in range(TT):
                    for k, (a, z) in enumerate(parts):
                        step(V.tensor_scalar(mtok[:, t, a:z], mtok[:, t, a:z], rstd_m[:, 2 * t + k:2 * t + k + 1], None,
                                             ALU.mult))
                step.settle()
                dve.sem_inc(cn_ready, 1)

                def biased(k):
                    h, sinks = k % AH, k < AH
                    name = f"ws{h}" if sinks else f"ms{h}"
                    b = take_bank(dve, B, name)
                    if k >= 4:
                        dve.wait_ge(bank_full, B.index[f"wT{h}"] + 1)
                    for t in range(TT):
                        mask = window[:, h, slice_of(t)] if sinks else causal[:, slice_of(t)]
                        ins = V.tensor_tensor_reduce(out=prob2[:, k % 4, t, :], in0=b[:, t * SEQ:(t + 1) * SEQ], in1=mask,
                                                     scale=(64 if sinks else QK) ** -0.5, scalar=REPLACED,
                                                     op0=ALU.add, op1=ALU.max, accum_out=rowmax2[:, k, t:t + 1])
                    ins.then_inc(emptied["dve"], 1)
                    after_emptied(dve, B, name)
                    if sinks:
                        ins = V.tensor_scalar(negmax2[:, k, :], rowmax2[:, k, :], -1.0, nsink[:, h:h + 1], ALU.mult, ALU.min)
                    else:
                        ins = V.tensor_scalar(negmax2[:, k, :], rowmax2[:, k, :], -1.0, None, ALU.mult)
                    ins.then_inc(negmax_ready, 1)

                for k in range(AH):
                    biased(k)
                for name, dst, n, g in (("cqT", cqT, 2, "mq_g"), ("ckvT", ckvT.unsqueeze(1), 1, "mkv_g")):
                    b = take_bank(dve, B, name)
                    for k in range(n):
                        ins = V.tensor_scalar(dst[:, k, :], b[:, k * SEQ:(k + 1) * SEQ], col(g)[:, k:k + 1], None, ALU.mult)
                    ins.then_inc(emptied["dve"], 1)
                dve.wait_ge(exp_ready, AH)
                step(V.tensor_tensor(sums2[:, 0:AH, :], sums2[:, 0:AH, :], esink, ALU.add))
                step.settle()
                step(V.reciprocal(rsum2[:, 0:AH, :], sums2[:, 0:AH, :]))

                conv(cv, cfu, CF_K, col("cf_w"), None, range(CF_SPLIT, CF_K))
                dve.sem_inc(conv_ready, 1)

                def rotate(x1, x2, cos, sin, n):
                    r = [rt[:, k, 0:n, :] for k in range(4)]
                    step.settle()
                    for o, x, w in ((0, x1, cos), (1, x2, sin), (2, x2, cos), (3, x1, sin)):
                        step(V.tensor_tensor(r[o], x, w, ALU.mult))
                    step.settle()
                    step(V.tensor_tensor(x1, r[0], r[1], ALU.subtract))
                    step(V.tensor_tensor(x2, r[2], r[3], ALU.add))

                after_emptied(dve, B, "kv1")
                for t in range(TT):
                    q = qtok[:, t]
                    rotate(q[:, :, 64:80], q[:, :, 80:96], under(cos_t[:, t, :], AH), under(sin_t[:, t, :], AH), AH)
                    k = krt[:, t, :].unsqueeze(1)
                    rotate(k[:, :, 0:16], k[:, :, 16:32], under(cos_t[:, t, :], 1), under(sin_t[:, t, :], 1), 1)
                step.settle()
                for t in range(TT):
                    ins = V.tensor_copy(kcat[:, t, :, 64:96], under(krt[:, t, :], AH))
                ins.then_inc(rope_ready, 1)

                def mixed(a, z):
                    for t in range(TT):
                        step(V.tensor_tensor(sq3[:, t * 512:t * 512 + z - a], mix2[:, t, a:z], mix2[:, t, a:z], ALU.mult))
                    step.settle()
                    for t in range(TT):
                        step(V.tensor_reduce(ss_x2[:, t, a // 64:z // 64], grouped(sq3[:, t * 512:t * 512 + z - a], (z - a) // 64),
                                             AX_X, ALU.add))
                    step.settle()

                def attended(sums, k, at):
                    for t in range(TT):
                        step(V.tensor_tensor(grouped(mix2[:, t, at:at + 256], AH), grouped(sums[t][:, 0:256], AH),
                                             over(rsum2[:, k:k + AH, t], 64), ALU.mult))
                    step.settle()

                dve.wait_ge(out_full, 1)
                attended(acc[2:4], 0, 768)
                after_emptied(dve, B, "cvT")
                mixed(0, 256)

                for k in range(AH, 2 * AH):
                    biased(k)

                for t in range(TT):
                    step(V.bn_stats(bn[:, t, 0, :], cvt[:, t, :]))
                step.settle()
                for t in range(TT):
                    step(V.bn_aggr(mv[:, t, :], bn[:, t, 0, :]))
                root_of(step, 2)
                step(V.reciprocal(rstd_l, std_l))
                step.settle()
                for t in range(TT):
                    step(V.tensor_scalar(cvt[:, t, :], cvt[:, t, :], mv[:, t, 0:1], rstd_l[:, t:t + 1], ALU.subtract, ALU.mult))
                step.settle()
                step(V.tensor_tensor(cvt, cvt, under(par("cf_g"), TT), ALU.mult))
                step.settle()
                step(V.tensor_tensor(cvt, cvt, under(par("cf_b"), TT), ALU.add))
                step.settle()
                dve.sem_inc(cfg_ready, 1)

                dve.wait_ge(exp_ready, 2 * AH)
                step(V.reciprocal(rsum2[:, AH:, :], sums2[:, AH:, :]))
                dve.wait_ge(cfmix_ready, 1)
                mixed(512, 1024)
                dve.sem_inc(ms_ready, 1)
                dve.wait_ge(out_full, 2)
                attended(acc[0:2], AH, 256)
                mixed(256, 512)
                dve.sem_inc(ms_ready, 1)
                dve.wait_ge(std_ready, 3)
                step(V.reciprocal(rstd_x2[:, :, 0:4], std_x2[:, :, 0:4]))
                V.reciprocal(rstd_x2[:, :, 8:16], std_x2[:, :, 8:16]).then_inc(rstd_ready, 1)
                dve.wait_ge(std_ready, 4)
                step(V.reciprocal(rstd_x2[:, :, 4:8], std_x2[:, :, 4:8]))
                step.settle()
                for t in range(TT):
                    x = grouped(mix2[:, t, 256:512], 4)
                    V.tensor_tensor(x, x, over(rstd_x2[:, t, 4:8], 64), ALU.mult).then_inc(rows_ready, 1)
                empty_transposed(B, "mT", col("mix_g"))
                layer_norm(step, 5, [(2 + TT * (c + 1), [(t, c) for t in range(TT)]) for c in range(2)], hpre,
                           par("ln1_g"), par("ln1_b"), bn, mv, std_l, rstd_l, rows_ready)
                empty_transposed(B, "hT", None)

                def top16(vals, idx, src, src2):
                    n = range(len(src))
                    step.settle()
                    for i in n:
                        step(V.max(vals[i][:, 0:8], src[i]))
                    step.settle()
                    for i in n:
                        step(V.max_index(idx[i][:, 0:8], vals[i][:, 0:8], src[i]))
                        step(V.match_replace(src2[i], vals[i][:, 0:8], src[i], REPLACED))
                    step.settle()
                    for i in n:
                        step(V.max(vals[i][:, 8:16], src2[i]))
                    step.settle()
                    for i in n:
                        step(V.max_index(idx[i][:, 8:16], vals[i][:, 8:16], src2[i]))

                for h in range(PH):
                    after_emptied(dve, B, f"rs{h}")
                    sides = [(t, k) for t in range(TT) for k in range(2)]
                    top16([topv[:, h, t, k, :] for t, k in sides], [topi[:, h, t, k, :] for t, k in sides],
                          [rs[:, h, t, k, :] for t, k in sides], [rs2[:, t, k, :] for t, k in sides])
                    for t in range(TT):
                        step(V.tensor_tensor(grouped(cand[:, t, :], TOP), over(topv[:, h, t, 0, :], TOP),
                                             under(topv[:, h, t, 1, :], TOP), ALU.add))
                    step.settle()
                    top16([best[:, h, t, :] for t in range(TT)], [besti[:, h, t, :] for t in range(TT)],
                          [cand[:, t, :] for t in range(TT)], [cand2[:, t, :] for t in range(TT)])
                step.settle()
                gate = chosen[:, 2].rearrange("p t (h k) -> p t h k", h=PH)
                for t in range(TT):
                    step(V.tensor_tensor(gate[:, t], best[:, :, t, :], best[:, :, t, 0:1].broadcast_to([P, PH, TOP]),
                                         ALU.subtract))
                step(V.tensor_scalar(bestab[:, 0], besti, 4, None, ALU.logical_shift_right))
                step(V.tensor_scalar(bestab[:, 1], besti, TOP - 1, None, ALU.bitwise_and))
                step(V.tensor_copy(topf, topi))
                step.settle()
                dve.sem_inc(score_ready, 1)
                step(V.tensor_copy(bestf, bestab))
                places = iota_k[:, 0:TOP].unsqueeze(1).unsqueeze(1).broadcast_to([P, PH, TOP, TOP])
                for t in range(TT):
                    for k in range(2):
                        step.settle()
                        step(V.tensor_tensor(eq, places, bestf[:, k, :, t, :].unsqueeze(3).broadcast_to([P, PH, TOP, TOP]),
                                             ALU.is_equal))
                        step.settle()
                        step(V.tensor_tensor(eq, eq, topf[:, :, t, k, :].unsqueeze(2).broadcast_to([P, PH, TOP, TOP]),
                                             ALU.mult))
                        step.settle()
                        step(V.tensor_reduce(chosen[:, k, t, :].rearrange("p (h k) -> p h k", h=PH), eq, AX_X, ALU.add))
                dve.wait_ge(gexp_ready, 1)
                for t in range(TT):
                    step(V.tensor_reduce(gsum[:, t, :], gate[:, t], AX_X, ALU.add))
                step.settle()
                step(V.reciprocal(gsum, gsum))
                step.settle()
                for t in range(TT):
                    step(V.tensor_tensor(gate[:, t], gate[:, t], over(gsum[:, t, :], TOP), ALU.mult))
                step.settle()
                dve.sem_inc(chosen_ready, 1)
                after_emptied(dve, B, "gT")

                for m in range(PIECES):
                    step(V.tensor_copy(g_part[:, m, :], gT[:]))
                    step.settle()
                    if m + 1 < PIECES:
                        step(V.tensor_tensor(gT[:], gT[:], g_part[:, m, :], ALU.subtract))
                        step.settle()

                def onehots(n, i, step, free):
                    if free:
                        dve.wait_ge(onehot_used, i * step + (n - 1))
                    s, q = n % 2, n // JQ
                    at = i * (step * GROUP) + n % JQ * GROUP
                    tokens = slice(at, at + GROUP) if isinstance(i, int) else bass.ds(at, GROUP)
                    pairs = lambda x: x.rearrange("p (c k) -> p c k", k=2)
                    shape = lambda keys: [P, GROUP // 2, keys, 2]
                    keys = iota_b[:, q * JQ:(q + 1) * JQ, :]
                    V.tensor_tensor(one_j[:, s], keys.unsqueeze(1).broadcast_to(shape(JQ)),
                                    pairs(i2T[:, tokens]).unsqueeze(2).broadcast_to(shape(JQ)),
                                    ALU.is_equal).then_inc(onehot_step, 1)
                    V.tensor_tensor(one_i[:, s], iota_b[:].unsqueeze(1).broadcast_to(shape(NK)),
                                    pairs(i1T[:, tokens]).unsqueeze(2).broadcast_to(shape(NK)),
                                    ALU.is_equal).then_inc(onehot_step, 1)
                    dve.wait_ge(onehot_step, i * (2 * step) + 2 * (n + 1))
                    for m in range(PIECES):
                        ins = V.tensor_tensor(gate_j[:, s, :, m], one_j[:, s],
                                              pairs(g_part[:, m, tokens]).unsqueeze(2).broadcast_to(shape(JQ)), ALU.mult)
                    ins.then_inc(onehot_ready, 1)

                for u in range(8):
                    onehots(u, 0, 8, u >= 2)
                with dve.Fori(1, JQ // 8) as i:
                    for u in range(8):
                        onehots(u, i, 8, True)
                for first, n in RUNS:
                    def one(i, u, free):
                        if first < NK - JQ:
                            onehots(JQ + first + u, i, 4, True)
                        j = i * 4 + (first % JQ + u)
                        b = i * 4 + (first % JQ + u)
                        if first >= STASH:
                            value = hid[:, u % 2, :]
                        elif isinstance(b, int):
                            value = stash[first // JQ][:, b, :]
                        else:
                            value = stash[first // JQ][:, bass.ds(b, 1), :].rearrange("p b t -> p (b t)")
                        gated(i, 4, u, first, run_base(first), int(first >= STASH), value, gates[:, first // JQ % 2, :, j], free)

                    if first % JQ == 0:
                        dve.wait_ge(gates_out, first + JQ)
                    for u in range(4):
                        one(0, u, first > 0 or u >= 2)
                    with dve.Fori(1, n // 4) as i:
                        for u in range(4):
                            one(i, u, True)
                layer_norm(step, 6, [(LAST_SUMS - TT + t + 1, [(t, c) for c in range(2)]) for t in range(TT)], ypre,
                           par("ln2_g"), par("ln2_b"), bn3, mv3, std3, rstd3, None)
                return step.n

            dve.wait_ge(const_ready, CONSTS)
            setup()
            for n, layer in ((1, block1), (1 + DEPTH, block2)):
                with dve.Fori(0, DEPTH) as l:
                    enter_layer(dve, "dve", l + n)
                    n_steps = layer()
                    leave_layer(dve, "dve", dve_step, n_steps)


def _feature_chunk(w, c):
    return w[:, c:c + P].reshape(DT, P, P).transpose(1, 0, 2).reshape(P, CH)


def _token_chunks(w, c):
    x = w[:, c:c + 512].reshape(DT // 2, 2, P, 512).transpose(0, 2, 1, 3)
    return [x[i].reshape(P, CH) for i in range(DT // 2)]


def _woven(ups, downs):
    out = list(ups[0])
    for j in range(len(downs)):
        if j + 1 < len(ups):
            out += ups[j + 1]
        out.append(downs[j])
    return out


def _stream1(w_in, w_out, w_gate, w_up, w_down):
    out = [_feature_chunk(w_in, c) for c in range(0, 1024, P)]
    for c in (2048, 2560, 1024, 3072, 1536):
        out += _token_chunks(w_in, c)
    for c in (0, 512):
        out += _token_chunks(w_out, c)
    out += _woven([[_feature_chunk(w_gate, f), _feature_chunk(w_up, f)] for f in range(0, D_FF, P)],
                  [w_down[f:f + P] for f in range(0, D_FF, P)])
    return out


def _stream2(w_in, w_out, w_q, u, v, out):
    at = dict(scb=0, scc=256, sch=512, cq=768, cfa=1184, cfg=1440, swq=1696, swk=1952, swv=2080)
    q = w_in[:, at["swq"]:at["swk"]].reshape(D, AH, 64)[:, [0, 2, 1, 3]].reshape(D, 256)
    cols = [w_in[:, at[k] + c:at[k] + c + P] for k in ("cfa", "cfg", "scc", "sch", "scb") for c in (0, P)]
    cols += [q[:, 0:P], q[:, P:], w_in[:, at["swk"]:at["swv"]]]
    parts = [_feature_chunk(x, 0) for x in cols]
    m = np.concatenate([w_in[:, at["cq"]:at["cq"] + 384], w_in[:, at["swv"]:at["swv"] + P]], axis=1)
    parts += _token_chunks(m, 0)
    kr = np.zeros((P, CH), w_in.dtype)
    kr[:, 0:DT * 32] = w_in[:, 1152:1184].reshape(DT, P, 32).transpose(1, 0, 2).reshape(P, -1)
    parts.append(kr)
    for c in (0, 512):
        parts += _token_chunks(w_out, c)
    parts += [_feature_chunk(w_q, c) for c in range(0, 2 * PH * P, P)]
    for i, x in enumerate(parts):
        out[i] = x
    ut = u.reshape(NK, NK, DT, P).transpose(1, 3, 2, 0)
    vt = v.reshape(NK, NK, D).transpose(1, 0, 2)
    out[N2_PRE:N2_OUT] = ut[0:STASH].reshape(STASH, P, CH)
    out[N2_OUT:N2_OUT + STASH] = vt[0:STASH]
    for first, n in RUNS:
        if first >= STASH:
            a, end = run_base(first), first + n
            out[a] = ut[first].reshape(P, CH)
            out[a + 1:a + 2 * n - 1:2] = ut[first + 1:end].reshape(n - 1, P, CH)
            out[a + 2:a + 2 * n - 1:2] = vt[first:end - 1]
            out[a + 2 * n - 1] = vt[end - 1]


def _cols(x):
    return x.reshape(-1, P).T


def kernel(**inputs):
    import concourse.bacc as bacc
    from concourse.bass_utils import run_bass_kernel_spmd

    a = {k: np.asarray(v) for k, v in inputs.items()}
    L = range(DEPTH)
    f = np.float32
    stream = np.empty((DEPTH * (N1 + N2), P, CH), a["w_in"].dtype)
    for l in L:
        for i, x in enumerate(_stream1(a["w_in"][l], a["w_out"][l], a["w_gate"][l], a["w_up"][l], a["w_down"][l])):
            stream[l * N1 + i] = x
        at = DEPTH * N1 + l * N2
        _stream2(a["w_in_2"][l], a["w_out_2"][l], a["peer_w_q_2"][l], a["peer_u_2"][l], a["peer_v_2"][l], stream[at:at + N2])
    lam_init = [0.8 - 0.6 * float(np.exp(-0.3 * l)) for l in L]
    col1 = np.stack([np.concatenate([_cols(a["attn_norm_g"][l]), _cols(a["ffn_norm_g"][l])], 1) for l in L])
    row1 = np.stack([np.concatenate([
        a["ret_norm_g"][l], a["dq_norm_g"][l], a["dk_norm_g"][l], a["diff_norm_g"][l],
        a["lambda_q1"][l], a["lambda_q2"][l], a["lambda_k1"][l], a["lambda_k2"][l],
        a["ret_decay_fwd"][l], a["ret_decay_bwd"][l], np.array([lam_init[l], 1.0 - lam_init[l]], f)]) for l in L])
    row2 = np.stack([np.concatenate([
        a["ln1_g_2"][l], a["ln1_b_2"][l], a["ln2_g_2"][l], a["ln2_b_2"][l],
        a["cf_ln_g_2"][l], a["cf_ln_b_2"][l], a["swa_sinks_2"][l]]) for l in L])

    def taps(w):
        return w.reshape(w.shape[0], 2, P).transpose(2, 1, 0).reshape(P, -1)

    col2 = np.stack([np.concatenate([
        taps(a["sc_conv_w_2"][l]), taps(a["cf_dw_w_2"][l]), _cols(a["cf_dw_b_2"][l]), _cols(a["mla_q_norm_2"][l]),
        _cols(a["mla_kv_norm_2"][l]), _cols(a["mix_norm_g_2"][l])], 1) for l in L])
    small2 = np.stack([np.concatenate([
        a["mla_w_uq_2"][l].reshape(2, P, AH * QK).transpose(1, 0, 2).reshape(P, -1),
        a["mla_w_uk_2"][l], a["mla_w_uv_2"][l]], 1) for l in L])
    sub2 = a["peer_sub_keys_2"].reshape(DEPTH, 2 * PH, NK, P).transpose(0, 3, 1, 2)
    inv = (10000.0 ** (-np.arange(16, dtype=f) / f(16))).astype(f)
    arrays = dict(in_x=a["x"][0], in_pos=a["positions_2"][0], in_stream=stream, in_col1=col1, in_row1=row1, in_col2=col2,
                  in_row2=row2, in_small2=small2, in_sub2=sub2, in_inv=inv)
    arrays = {k: np.ascontiguousarray(v) for k, v in arrays.items()}
    nc = bacc.Bacc("TRN2", target_bir_lowering=False, num_devices=1)
    args = [nc.dram_tensor(k, v.shape, mybir.dt.from_np(v.dtype), kind="ExternalInput").ap() for k, v in arrays.items()]
    out = nc.dram_tensor("out_x", (SEQ, D), F32, kind="ExternalOutput").ap()
    two_blocks_kernel(nc, *args, out)
    r = run_bass_kernel_spmd(nc, [arrays], core_ids=[0])
    return r.results[0]["out_x"].reshape(1, SEQ, D)
```
